# Optimizing a Trainium2 kernel written in Bass

```python
import math
import jax, jax.numpy as jnp
from jax import lax
import numpy as np

D_MODEL = 1024
BATCH = 1
SEQ = 256
DEPTH = 1

N_META = 16
N_HEADS = 8
HEAD_DIM = 64
ATTN_WIDTH = N_HEADS * HEAD_DIM
IDX_HEADS = 8
IDX_DIM = 64
TOPK_MAX = 256
Q_BLOCK = 64
CONV_CH = 512
CONV_WIDTH = 31
N_BUCKETS = 32
MAX_DISTANCE = 128
N_EXPERTS = 32
TOP_K_EXPERTS = 4
D_FF = 1024
SWIGLU_LIMIT = 7.0
SWIGLU_ALPHA = 1.702
EPS = 1e-6
IDX_SCALE = (IDX_DIM ** -0.5) * (IDX_HEADS ** -0.5)

COL_Q = ATTN_WIDTH
COL_K = ATTN_WIDTH
COL_V = ATTN_WIDTH
COL_IQ = IDX_HEADS * IDX_DIM
COL_IK = IDX_DIM
COL_IW = IDX_HEADS
COL_GLU = 2 * CONV_CH
COL_GATE = 2 * D_MODEL
SPLIT_POINTS = (COL_Q,
                COL_Q + COL_K,
                COL_Q + COL_K + COL_V,
                COL_Q + COL_K + COL_V + COL_IQ,
                COL_Q + COL_K + COL_V + COL_IQ + COL_IK,
                COL_Q + COL_K + COL_V + COL_IQ + COL_IK + COL_IW,
                COL_Q + COL_K + COL_V + COL_IQ + COL_IK + COL_IW + COL_GLU)
IN_COLS = COL_Q + COL_K + COL_V + COL_IQ + COL_IK + COL_IW + COL_GLU + COL_GATE

kernel_name = "hybrid_dsa_conformer_moe_block"

def rmsnorm(x, g):
    xf = x.astype(jnp.float32)
    y = xf * lax.rsqrt(jnp.mean(xf * xf, axis=-1, keepdims=True) + EPS)
    return (y * g.astype(jnp.float32)).astype(x.dtype)

def t5_bucket(n):
    max_exact = N_BUCKETS // 2
    nf = jnp.maximum(n, 1).astype(jnp.float32)
    large = max_exact + (jnp.log(nf / max_exact) / math.log(MAX_DISTANCE / max_exact)
                         * (N_BUCKETS - max_exact)).astype(jnp.int32)
    large = jnp.minimum(large, N_BUCKETS - 1)
    return jnp.where(n < max_exact, n, large)

def sparse_attention(q, k, v, iq, ik, iw, rel_bias, topk):
    B, T = q.shape[0], q.shape[1]
    nb = -(-T // Q_BLOCK)
    Tp = nb * Q_BLOCK

    def to_blocks(a):
        a = jnp.pad(a, [(0, 0), (0, Tp - T)] + [(0, 0)] * (a.ndim - 2))
        return jnp.moveaxis(a.reshape((B, nb, Q_BLOCK) + a.shape[2:]), 1, 0)

    key_pos = jnp.arange(T, dtype=jnp.int32)
    starts = jnp.arange(nb, dtype=jnp.int32) * Q_BLOCK
    gather = jax.vmap(lambda kb, ib: kb[ib])

    def block(args):
        qb, iqb, iwb, start = args
        qpos = start + jnp.arange(Q_BLOCK, dtype=jnp.int32)
        s = jnp.einsum('bqhd,bsd->bqhs', iqb, ik).astype(jnp.float32)
        score = jnp.einsum('bqh,bqhs->bqs', iwb.astype(jnp.float32), jax.nn.relu(s)) * IDX_SCALE
        causal = key_pos[None, :] <= qpos[:, None]
        score = jnp.where(causal[None], score, -jnp.inf)
        _, sel = lax.top_k(score, topk)
        k_sel = gather(k, sel)
        v_sel = gather(v, sel)
        logits = jnp.einsum('bqhd,bqkhd->bhqk', qb, k_sel).astype(jnp.float32) * (HEAD_DIM ** -0.5)
        dist = qpos[None, :, None] - sel
        bias = rel_bias[t5_bucket(jnp.maximum(dist, 0))]
        logits = logits + jnp.moveaxis(bias, 3, 1).astype(jnp.float32)
        logits = jnp.where((dist >= 0)[:, None], logits, -jnp.inf)
        p = jax.nn.softmax(logits, axis=-1).astype(v.dtype)
        return jnp.einsum('bhqk,bqkhd->bqhd', p, v_sel)

    out = lax.map(block, (to_blocks(q), to_blocks(iq), to_blocks(iw), starts))
    out = jnp.moveaxis(out, 0, 1).reshape(B, Tp, N_HEADS * HEAD_DIM)
    return out[:, :T]

def conformer_conv(u, conv_w, conv_b, ln_g, ln_b, w_conv_out):
    a, g = jnp.split(u, 2, axis=-1)
    y = a * jax.nn.sigmoid(g)
    y = lax.conv_general_dilated(y, conv_w[:, None, :].astype(y.dtype), window_strides=(1,),
                                 padding=[(CONV_WIDTH - 1, 0)],
                                 dimension_numbers=('NWC', 'WIO', 'NWC'),
                                 feature_group_count=CONV_CH) + conv_b
    yf = y.astype(jnp.float32)
    mu = jnp.mean(yf, axis=-1, keepdims=True)
    var = jnp.mean(jnp.square(yf - mu), axis=-1, keepdims=True)
    yf = (yf - mu) * lax.rsqrt(var + EPS) * ln_g.astype(jnp.float32) + ln_b.astype(jnp.float32)
    y = jax.nn.silu(yf).astype(u.dtype)
    return y @ w_conv_out

def moe_ffn(h, w_router, b_router, w_ug, b_ug, w_down, b_down):
    B, T, D = h.shape
    hf = h.reshape(B * T, D)
    logits = (hf @ w_router + b_router).astype(jnp.float32)
    vals, idx = lax.top_k(logits, TOP_K_EXPERTS)
    gates = jax.nn.softmax(vals, axis=-1)
    combine = jnp.sum(jax.nn.one_hot(idx, N_EXPERTS, dtype=jnp.float32) * gates[..., None], axis=1)

    def expert(acc, params):
        wug, bug, wd, bd, c = params
        ug = hf @ wug + bug
        gate = jnp.minimum(ug[:, :D_FF], SWIGLU_LIMIT)
        up = jnp.clip(ug[:, D_FF:], -SWIGLU_LIMIT, SWIGLU_LIMIT)
        act = (up + 1.0) * gate * jax.nn.sigmoid(SWIGLU_ALPHA * gate)
        y = act @ wd + bd
        return acc + c[:, None].astype(y.dtype) * y, None

    acc, _ = lax.scan(expert, jnp.zeros_like(hf), (w_ug, b_ug, w_down, b_down, combine.T))
    return acc.reshape(B, T, D)

def setup_inputs(seed: int = 0) -> dict:
    key = jax.random.key(seed)
    ks = jax.random.split(key, 24)
    f32 = jnp.float32
    nrm = lambda k, shape, s: jax.random.normal(k, shape, f32) * s
    return {
        "x": nrm(ks[0], (BATCH, SEQ, D_MODEL), 1.0),
        "meta_tokens": nrm(ks[1], (N_META, D_MODEL), 1.0),
        "rel_bias": nrm(ks[2], (N_BUCKETS, N_HEADS), 0.5),
        "norm_mix": 1.0 + nrm(ks[3], (DEPTH, D_MODEL), 0.02),
        "w_in": nrm(ks[4], (DEPTH, D_MODEL, IN_COLS), D_MODEL ** -0.5),
        "b_gate": nrm(ks[5], (DEPTH, 2 * D_MODEL), 0.1),
        "w_attn_out": nrm(ks[6], (DEPTH, ATTN_WIDTH, D_MODEL), ATTN_WIDTH ** -0.5),
        "conv_w": nrm(ks[7], (DEPTH, CONV_WIDTH, CONV_CH), CONV_WIDTH ** -0.5),
        "conv_b": nrm(ks[8], (DEPTH, CONV_CH), 0.01),
        "conv_ln_g": 1.0 + nrm(ks[9], (DEPTH, CONV_CH), 0.02),
        "conv_ln_b": nrm(ks[10], (DEPTH, CONV_CH), 0.01),
        "w_conv_out": nrm(ks[11], (DEPTH, CONV_CH, D_MODEL), CONV_CH ** -0.5),
        "w_out": nrm(ks[12], (DEPTH, D_MODEL, D_MODEL), D_MODEL ** -0.5),
        "norm_ffn": 1.0 + nrm(ks[13], (DEPTH, D_MODEL), 0.02),
        "w_router": nrm(ks[14], (DEPTH, D_MODEL, N_EXPERTS), D_MODEL ** -0.5),
        "b_router": nrm(ks[15], (DEPTH, N_EXPERTS), 0.01),
        "w_up_gate": nrm(ks[16], (DEPTH, N_EXPERTS, D_MODEL, 2 * D_FF), D_MODEL ** -0.5),
        "b_up_gate": nrm(ks[17], (DEPTH, N_EXPERTS, 2 * D_FF), 0.01),
        "w_down": nrm(ks[18], (DEPTH, N_EXPERTS, D_FF, D_MODEL), D_FF ** -0.5),
        "b_down": nrm(ks[19], (DEPTH, N_EXPERTS, D_MODEL), 0.01),
        "norm_final": 1.0 + nrm(ks[20], (D_MODEL,), 0.02),
    }

def reference(x, meta_tokens, rel_bias, norm_mix, w_in, b_gate, w_attn_out, conv_w, conv_b,
              conv_ln_g, conv_ln_b, w_conv_out, w_out, norm_ffn, w_router, b_router,
              w_up_gate, b_up_gate, w_down, b_down, norm_final):
    B, S, D = x.shape
    topk = min(TOPK_MAX, S // 4)
    meta = jnp.broadcast_to(meta_tokens[None].astype(x.dtype), (B, N_META, D))
    h = jnp.concatenate([meta, x], axis=1)
    T = h.shape[1]
    for l in range(DEPTH):
        hn = rmsnorm(h, norm_mix[l])
        proj = hn @ w_in[l]
        q, k, v, iq, ik, iw, glu_in, gate_in = jnp.split(proj, SPLIT_POINTS, axis=-1)
        q = q.reshape(B, T, N_HEADS, HEAD_DIM)
        k = k.reshape(B, T, N_HEADS, HEAD_DIM)
        v = v.reshape(B, T, N_HEADS, HEAD_DIM)
        iq = iq.reshape(B, T, IDX_HEADS, IDX_DIM)
        y_a = sparse_attention(q, k, v, iq, ik, iw, rel_bias, topk) @ w_attn_out[l]
        y_b = conformer_conv(glu_in, conv_w[l], conv_b[l], conv_ln_g[l], conv_ln_b[l], w_conv_out[l])
        g_a, g_b = jnp.split(jax.nn.sigmoid(gate_in + b_gate[l]), 2, axis=-1)
        h = h + (g_a * y_a + g_b * y_b) @ w_out[l]
        h = h + moe_ffn(rmsnorm(h, norm_ffn[l]), w_router[l], b_router[l], w_up_gate[l],
                        b_up_gate[l], w_down[l], b_down[l])
    return rmsnorm(h, norm_final)[:, N_META:]


_drawn_inputs = setup_inputs


def setup_inputs(seed=0):
    import zlib

    import numpy as np

    out = dict(_drawn_inputs(seed))
    spreads = {}
    factors = {'conv_b': 4.287,
     'conv_ln_g': 3.755,
     'conv_ln_b': 8.0,
     'b_router': 3.087,
     'b_up_gate': 8.0,
     'b_down': 8.0,
     'norm_final': 2.952}
    for name, (base, spread) in spreads.items():
        noise = np.random.default_rng([zlib.crc32(name.encode()), seed]).standard_normal(out[name].shape)
        drawn = base * np.exp(spread * noise) if base else spread * noise
        out[name] = __import__('jax').numpy.asarray(drawn.astype(out[name].dtype))
    for name, factor in factors.items():
        out[name] = (out[name] * factor).astype(out[name].dtype)
    return out
```

```python
from contextlib import ExitStack

import numpy as np

import concourse.bass as bass
from concourse import mybir

F32 = mybir.dt.float32
I32 = mybir.dt.int32
U32 = mybir.dt.uint32
ALU = mybir.AluOpType
ACT = mybir.ActivationFunctionType
AX_X = mybir.AxisListType.X

P = 128
META = 16
D = 1024
KD = D // P
SEQ = 256
QT = SEQ // P
T = META + SEQ
HEADS = 8
DH = 64
HP = HEADS // 2
TOPK = 64
IDX_SCALE = (64 ** -0.5) * (8 ** -0.5)
CH = 512
CT = CH // P
TAPS = 31
NB = 32
E = 32
FF = 1024
CAP = 64
PASS_CAP = 2 * CAP
PASSES = SEQ // PASS_CAP
PAIRS = E // 2
EPS = 1e-6
FAR = -1.0e30
TAKEN = -3.0e38
NTOE = 2 * T - 1

C_Q, C_K, C_V, C_IQ, C_IK, C_IW, C_GLU, C_GATE = 0, 512, 1024, 1536, 2048, 2112, 2120, 3144
UNIT_COLS = 256
SLOT = 2048

KEY0 = [0, META, META + P]
KEYN = [META, P, P]
SEEN = [META + P, T]

FRONT = [("in", C_GLU + CH), ("in", C_GLU), ("in", C_GLU + CH + UNIT_COLS), ("in", C_GLU + UNIT_COLS),
         ("in", C_IQ), ("in", C_IQ + UNIT_COLS), ("ik", C_IK),
         ("in", C_Q), ("in", C_Q + UNIT_COLS), ("in", C_K), ("in", C_K + UNIT_COLS),
         ("in", C_V), ("in", C_V + UNIT_COLS)]
FRONT += [("in", C_GATE + UNIT_COLS * i) for i in range(8)]
FRONT += [("ao", 0), ("ao", 2), ("co", 0), ("co", 2)] + [("wo", 2 * i) for i in range(4)]
NF = len(FRONT)
UP_UNITS, DOWN_UNITS = KD, FF // P
PAIR_UNITS = 2 * UP_UNITS + DOWN_UNITS
BODY_UNITS = 2 * PAIR_UNITS
RING = 12
assert BODY_UNITS % RING == 0
TURNS = BODY_UNITS // RING

V_MIX, V_FFN, V_CB, V_LG, V_LB, V_BG = 0, 8, 16, 20, 24, 28
V_ROWS = 44


def slot_of(u):
    return u % RING


def loads_before(u):
    return u // RING


def layer(nc, x, meta, rel_bias, norm_mix, w_in, b_gate, w_attn_out, conv_w, conv_b, ln_g, ln_b,
          w_conv_out, w_out, norm_ffn, w_router, b_router, w_ug, b_ug, w_down, b_down, norm_final,
          bucket_rows, out):
    with ExitStack() as ctx:
        def sb(name, shape, dt=F32):
            return ctx.enter_context(nc.sbuf_tensor(name, shape, dt))

        def sem(name):
            return ctx.enter_context(nc.semaphore(name))

        ring = sb("ring", [P, RING, SLOT])
        x_nat = sb("x_nat", [P, QT, D])
        gate_region = sb("gate_region", [P, 16 * SEQ])
        x_scaled = gate_region[:, 0:3 * D].rearrange("p (i n) -> p i n", i=3)
        meta_nat = gate_region[:, 3 * D:4 * D]
        gates = gate_region[:, :].rearrange("p (i n) -> p i n", i=16)
        h_scaled = gate_region[:, 0:2 * D].rearrange("p (i n) -> p i n", i=2)
        picked = gate_region[:, 2 * D:4 * D].rearrange("p (b k n) -> p b k n", b=2, k=KD)
        hn_region = sb("hn_region", [P, KD * T])
        hn = hn_region[:, :].rearrange("p (k t) -> p k t", k=KD)
        merged = hn_region[:, 0:KD * SEQ].rearrange("p (k t) -> p k t", k=KD)
        glu_steps = hn_region[:, 0:4 * 512].rearrange("p (i n) -> p i n", i=4)
        iq_region = sb("iq_region", [P, 4 * SEQ + 2 * T])
        iq = iq_region[:, 0:4 * SEQ].rearrange("p (k t) -> p k t", k=4)
        ik_half = iq_region[:, 4 * SEQ:].rearrange("p (k t) -> p k t", k=2)
        attn = iq_region[:, 0:4 * SEQ].rearrange("p (k t) -> p k t", k=4)
        pick0 = iq_region[:, 0:512].rearrange("p (i n) -> p i n", i=QT)[:, :, 0:P]
        give0 = iq_region[:, 512:1024].rearrange("p (i n) -> p i n", i=QT)[:, :, 0:P]
        choose = iq_region[:, 1280:1536].rearrange("p (b n) -> p b n", b=2)
        qk_region = sb("qk_region", [P, 4 * SEQ + HEADS * T])
        q_t = qk_region[:, 0:4 * SEQ].rearrange("p (k t) -> p k t", k=4)
        k_half = qk_region[:, 4 * SEQ:].rearrange("p (h t) -> p h t", h=HEADS)
        bu_sb = qk_region[0:E, 0:2 * FF]
        bd_sb = qk_region[0:E, 2 * FF:2 * FF + D]
        prob_region = sb("prob_region", [P, HEADS * (SEEN[0] + SEEN[1])])
        probs = [prob_region[:, 0:HEADS * SEEN[0]].rearrange("p (h s) -> p h s", h=HEADS),
                 prob_region[:, HEADS * SEEN[0]:].rearrange("p (h s) -> p h s", h=HEADS)]
        h2 = prob_region[:, 0:2 * D].rearrange("p (i n) -> p i n", i=2)
        pt_region = sb("pt_region", [P, 3 * HEADS * P])
        probs_t = pt_region[:, :].rearrange("p (i h q) -> p i h q", i=3, h=HEADS)
        centred = pt_region[:, 0:CT * SEQ].rearrange("p (c t) -> p c t", c=CT)
        squares = pt_region[:, CT * SEQ:2 * CT * SEQ].rearrange("p (c t) -> p c t", c=CT)
        swish = pt_region[:, 2 * CT * SEQ:3 * CT * SEQ].rearrange("p (c t) -> p c t", c=CT)
        hf = pt_region[:, 0:KD * SEQ].rearrange("p (k t) -> p k t", k=KD)
        gfin = pt_region[:, 2 * D:3 * D]
        v_region = sb("v_region", [P, 3 * 512])
        v_sb = v_region[:, :].rearrange("p (i n) -> p i n", i=3)
        glu_region = sb("glu_region", [P, CT * (TAPS - 1 + T)])
        glu = glu_region[:, :].rearrange("p (c t) -> p c t", c=CT)
        conv_region = sb("conv_region", [P, CT * SEQ])
        conv = conv_region[:, :].rearrange("p (c t) -> p c t", c=CT)
        picked2 = pt_region[:, 0:2 * D].rearrange("p (k n) -> p k n", k=2 * KD)[:, 0:KD, :]
        act_t = [conv_region[:, :].rearrange("p (e f n) -> p e f n", e=2, f=8),
                 prob_region[:, 2 * D:3 * D].rearrange("p (e f n) -> p e f n", e=2, f=8)]
        y_pair = [glu_region[:, 0:D], v_region[:, 0:D]]
        glu_sig = sb("glu_sig", [P, 2, T])
        score = sb("score", [P, QT, T])
        seen_bias = sb("seen_bias", [P, QT, T])
        relu = glu_sig
        pick = [pick0, seen_bias[:, :, 0:P]]
        give = [give0, v_region[:, D:D + SEQ].rearrange("p (i n) -> p i n", i=QT)]
        give_t = [iq_region[:, 1024:1280], v_region[:, D + SEQ:D + 2 * SEQ]]
        ln_rows = glu_region[:, 0:2 * SEQ].rearrange("p (i t) -> p i t", i=2)
        ident = sb("ident", [P, P])
        ones = sb("ones", [P, P])
        mean_w = sb("mean_w", [P, P])
        before = sb("before", [P, P])
        number = sb("number", [P, P])
        eps_col = sb("eps_col", [P, 1])
        vec_rows = pt_region[0:V_ROWS, 1600:1600 + P]
        vec = sb("vec", [P, V_ROWS])
        cw_rows = pt_region[0:TAPS, 1088:1088 + CH]
        cw = sb("cw", [P, CT, TAPS])
        rel_sb = sb("rel_sb", [NB + 1, HEADS])
        bucket_sb = pt_region[0:NB + 1, 0:NTOE]
        toe_sb = pt_region[0:HEADS, 544:544 + NTOE]
        iw_t = pt_region[0:72, 1728:1728 + SEQ]
        iw = sb("iw", [P, QT, HEADS])
        stat = sb("stat", [P, 16])
        top8 = sb("top8", [P, QT, 8])
        smax = sb("smax", [P, QT, HEADS])
        sneg = sb("sneg", [P, QT, HEADS])
        ssum = sb("ssum", [P, QT, HEADS])
        srec = sb("srec", [P, QT, HEADS])
        wr_sb = sb("wr_sb", [P, KD, E])
        br_sb = sb("br_sb", [1, E])
        rlog = sb("rlog", [P, QT, E])
        ridx = sb("ridx", [P, QT, 8], U32)
        ridxf = sb("ridxf", [P, QT, 8])
        rexp = sb("rexp", [P, QT, 4])
        hot = sb("hot", [P, QT, 4, E])
        chosen = sb("chosen", [P, QT, E])
        combine_w = sb("combine_w", [P, QT, E])
        combine_t = sb("combine_t", [E, SEQ])
        place = sb("place", [P, QT, E * PASSES + 2])
        weight = sb("weight", [P, QT, E * PASSES + 2])
        counts = sb("counts", [P, 8])
        fuller = sb("fuller", [P, PAIRS])
        two_blocks = sb("two_blocks", [P, PAIRS * PASSES], I32)
        bodies = sb("bodies", [P, 1], I32)
        dram_toe = nc.dram_tensor("toeplitz_rows", (P, HEADS, NTOE), F32, kind="Internal").ap()

        ps = [ctx.enter_context(nc.psum_tensor(f"bank{i}", [P, 512], F32)) for i in range(8)]
        acc = ps[0:4]
        gate_ps, up_ps, t0_ps, t1_ps = ps[4:8]

        x_loaded = sem("x_loaded")
        vecs_loaded = sem("vecs_loaded")
        cw_loaded = sem("cw_loaded")
        rel_loaded = sem("rel_loaded")
        toe_stored = sem("toe_stored")
        toe_loaded = sem("toe_loaded")
        router_loaded = sem("router_loaded")
        ebias_loaded = sem("ebias_loaded")
        gfin_loaded = sem("gfin_loaded")
        slot_loaded = [sem(f"slot{i}_loaded") for i in range(RING)]
        unit_used = sem("unit_used")
        zeroed = sem("zeroed")
        pool_done = sem("pool_done")
        act_chain = sem("act_chain")
        dve_chain = sem("dve_chain")
        ss_ready = sem("ss_ready")
        root_ready = sem("root_ready")
        scaled_ready = sem("scaled_ready")
        vec_ps_ready = sem("vec_ps_ready")
        vec_ready = sem("vec_ready")
        xt_ready = sem("xt_ready")
        hn_act = sem("hn_act")
        hn_dve = sem("hn_dve")
        toe_ps_ready = sem("toe_ps_ready")
        toe_sb_ready = sem("toe_sb_ready")
        tile_ready = sem("tile_ready")
        tile_act = sem("tile_act")
        tile_dve = sem("tile_dve")
        iw_ps_ready = sem("iw_ps_ready")
        iw_ready = sem("iw_ready")
        idx_ready = sem("idx_ready")
        relu_ready = sem("relu_ready")
        relu_used = sem("relu_used")
        seen_ready = sem("seen_ready")
        bias_ready = sem("bias_ready")
        qk_ready = sem("qk_ready")
        logit_ready = sem("logit_ready")
        max_ready = sem("max_ready")
        exp_ready = sem("exp_ready")
        prob_ready = sem("prob_ready")
        attn_ps_ready = sem("attn_ps_ready")
        attn_copied = sem("attn_copied")
        glu_ready = sem("glu_ready")
        conv_ready = sem("conv_ready")
        mean_ready = sem("mean_ready")
        centred_ready = sem("centred_ready")
        squares_ready = sem("squares_ready")
        var_ready = sem("var_ready")
        ln_root = sem("ln_root")
        normed_ready = sem("normed_ready")
        swish_ready = sem("swish_ready")
        conv_out_ready = sem("conv_out_ready")
        merged_ready = sem("merged_ready")
        h2_ps_ready = sem("h2_ps_ready")
        h2_ready = sem("h2_ready")
        hs_ready = sem("hs_ready")
        hst_ready = sem("hst_ready")
        hf_act = sem("hf_act")
        hf_dve = sem("hf_dve")
        rlog_ready = sem("rlog_ready")
        rmax_ready = sem("rmax_ready")
        rexp_ready = sem("rexp_ready")
        choice_ready = sem("choice_ready")
        place_ps_ready = sem("place_ps_ready")
        ct_ready = sem("ct_ready")
        plan_ready = sem("plan_ready")
        pick_ready = sem("pick_ready")
        pick2_ready = sem("pick2_ready")
        gather_ready = [sem("gather_ready"), sem("gather_ready_2")]
        picked_ready = [sem("picked_ready"), sem("picked_ready_2")]
        gate_read = [sem("gate_read"), sem("gate_read_2")]
        clipped = [sem("clipped"), sem("clipped_2")]
        sig_ready = [sem("sig_ready"), sem("sig_ready_2")]
        act_ready = [sem("act_ready"), sem("act_ready_2")]
        actt_ps_ready = [sem("actt_ps_ready"), sem("actt_ps_ready_2")]
        actt_ready = [sem("actt_ready"), sem("actt_ready_2")]
        givet_ps_ready = [sem("givet_ps_ready"), sem("givet_ps_ready_2")]
        givet_ready = [sem("givet_ready"), sem("givet_ready_2")]
        y_act = [sem("y_act"), sem("y_act_2")]
        y_dve = [sem("y_dve"), sem("y_dve_2")]
        combined = [sem("combined"), sem("combined_2")]
        sum_ready = sem("sum_ready")
        fin_ss = sem("fin_ss")
        fin_root = sem("fin_root")
        fin_ready = sem("fin_ready")
        stored = sem("stored")

        tiles = []
        for i in range(2):
            tiles += [("g", 2 * i, 2 * i, 0), ("g", 2 * i + 1, 2 * i, P),
                      ("a", 2 * i, 2 * i + 1, 0), ("a", 2 * i + 1, 2 * i + 1, P)]
        tiles += [("iq", i, 4 + i // 2, P * (i % 2)) for i in range(4)]
        tiles += [("ik", 0, 6, 0), ("ik", 1, 6, 0)]
        tiles += [("q", i, 7 + i // 2, P * (i % 2)) for i in range(4)]
        tiles += [("k", i, 9 + i // 2, P * (i % 2)) for i in range(4)]
        tiles += [("v", i, 11, 0) for i in range(3)]
        tiles += [("gate", i, 13 + i // 2, P * (i % 2)) for i in range(16)]
        first = {}
        for n, (kind, *_) in enumerate(tiles):
            first.setdefault(kind, n)
        NT = len(tiles)
        U_AO, U_CO, U_WO = 21, 23, 25

        def read_by(n):
            if n >= NT:
                return tile_dve, 4 + n - NT + 1
            dve = sum(k == "a" for k, *_ in tiles[:n + 1])
            return (tile_dve, dve) if tiles[n][0] == "a" else (tile_act, n + 1 - dve)

        block = ctx.enter_context(nc.Block())

        @block.sync
        def _(sp):
            with nc.allow_non_contiguous_dma(reason="rows of the packed vectors and of the weights"):
                for u, (kind, c) in enumerate(FRONT):
                    if u >= RING:
                        sp.wait_ge(unit_used, u - RING + 1)
                    dst = ring[:, slot_of(u), :]
                    if kind == "in" or kind == "ik":
                        n = UNIT_COLS if kind == "in" else C_GLU - C_IK
                        dst = dst[:, 0:KD * n].rearrange("p (k n) -> p k n", k=KD)
                        src = w_in.rearrange("(k p) n -> p k n", p=P)[:, :, c:c + n]
                    else:
                        w = {"ao": w_attn_out, "co": w_conv_out, "wo": w_out}[kind]
                        dst = dst.rearrange("p (k n) -> p k n", k=2)
                        src = w.rearrange("(k p) n -> p k n", p=P)[:, c:c + 2, :]
                    sp.dma_start(dst, src).then_inc(slot_loaded[slot_of(u)], 16)

                def experts(first_body, i):
                    for j in range(BODY_UNITS):
                        pair, r = divmod(j, PAIR_UNITS)
                        u = NF + j
                        sp.wait_ge(unit_used, (first_body + i) * BODY_UNITS + (u - RING + 1))
                        dst = ring[:, slot_of(u), :]
                        if r < 2 * UP_UNITS:
                            e, k = divmod(r, UP_UNITS)
                            src = w_ug[bass.ds(4 * i + (2 * pair + e), 1), k * P:(k + 1) * P, :].rearrange(
                                "e p n -> p (e n)")
                        else:
                            f = r - 2 * UP_UNITS
                            dst = dst.rearrange("p (e n) -> p e n", e=2)
                            src = w_down[bass.ds(4 * i + 2 * pair, 2), f * P:(f + 1) * P, :].rearrange(
                                "e p n -> p e n")
                        sp.dma_start(dst, src).then_inc(slot_loaded[slot_of(u)], 16)

                with sp.Fori(0, PAIRS // 2) as i:
                    experts(0, i)
                sp.wait_ge(plan_ready, 1)
                n_bodies = sp.value_load(bodies[0:1, 0:1], min_val=PAIRS // 2,
                                         max_val=PASSES * PAIRS // 2)
                with sp.If(n_bodies > PAIRS // 2):
                    with sp.Fori(PAIRS // 2, n_bodies, PAIRS // 2) as done:
                        with sp.Fori(0, PAIRS // 2) as i:
                            experts(done, i)
            for i in range(QT):
                sp.wait_ge(fin_ready, i + 1)
                sp.dma_start(out[i * P:(i + 1) * P, :], x_nat[:, i, :]).then_inc(stored, 16)
            sp.wait_ge(stored, 16 * QT)

        @block.gpsimd
        def _(pool):
            nc.gpsimd.memset(ident[:], 0.0).then_inc(zeroed, 1)
            nc.gpsimd.memset(ones[:], 1.0).then_inc(zeroed, 1)
            nc.gpsimd.memset(before[:], 1.0).then_inc(zeroed, 1)
            nc.gpsimd.memset(seen_bias[:], 0.0).then_inc(zeroed, 1)
            nc.gpsimd.memset(rel_sb[:], 1.0).then_inc(zeroed, 1)
            nc.gpsimd.memset(eps_col[:], EPS).then_inc(zeroed, 1)
            pool.wait_ge(zeroed, 6)
            nc.gpsimd.affine_select(out=ident[:], in_=ident[:], compare_op=ALU.not_equal, fill=1.0,
                                    base=0, pattern=[[-1, P]], channel_multiplier=1).then_inc(pool_done, 1)
            nc.gpsimd.affine_select(out=before[:], in_=before[:], compare_op=ALU.is_gt, fill=0.0,
                                    base=0, pattern=[[1, P]], channel_multiplier=-1).then_inc(pool_done, 1)
            for i in range(QT):
                nc.gpsimd.affine_select(out=seen_bias[:, i, :], in_=seen_bias[:, i, :],
                                        compare_op=ALU.is_ge, fill=FAR, base=META + i * P,
                                        pattern=[[-1, T]], channel_multiplier=1).then_inc(pool_done, 1)
            nc.gpsimd.memset(mean_w[:], 1.0 / CH).then_inc(pool_done, 1)
            nc.gpsimd.iota(number[:], pattern=[[1, P]], base=0, channel_multiplier=0,
                           allow_small_or_imprecise_dtypes=True).then_inc(pool_done, 1)
            nc.gpsimd.memset(glu[:, :, 0:TAPS - 1], 0.0).then_inc(pool_done, 1)
            pool.wait_ge(pool_done, 7)
            nc.gpsimd.memset(ik_half[64:128, 0, :], 0.0).then_inc(pool_done, 1)
            nc.gpsimd.memset(k_half[64:128, 0:HEADS:2, :], 0.0).then_inc(pool_done, 1)
            pool.wait_ge(pool_done, 9)
            nc.gpsimd.memset(ik_half[0:64, 1, :], 0.0).then_inc(pool_done, 1)
            nc.gpsimd.memset(k_half[0:64, 1:HEADS:2, :], 0.0).then_inc(pool_done, 1)
            nc.gpsimd.memset(place[:], -1.0).then_inc(pool_done, 1)
            nc.gpsimd.memset(weight[:], 0.0).then_inc(pool_done, 1)
            for i in range(QT):
                pool.wait_ge(toe_loaded, 32)
                pool.wait_ge(seen_ready, i + 1)
                w = SEEN[i]
                left_out = seen_bias[:, i, 0:w].unsqueeze(1).broadcast_to([P, HEADS, w])
                nc.gpsimd.tensor_tensor(probs[i], probs[i], left_out, ALU.add).then_inc(bias_ready, 1)

        CONSTS = 13

        @block.scalar
        def _(act):
            chain = [0]

            def link(ins):
                chain[0] += 1
                ins.then_inc(act_chain, 1)
                act.wait_ge(act_chain, chain[0])

            with nc.allow_non_contiguous_dma(reason="small vectors"):
                for i in range(QT):
                    act.dma_start(x_nat[:, i, :], x[i * P:(i + 1) * P, :]).then_inc(x_loaded, 16)
                act.dma_start(meta_nat[0:META, :], meta).then_inc(x_loaded, 16)
                for r, n, v in ((V_MIX, 8, norm_mix), (V_FFN, 8, norm_ffn), (V_CB, 4, conv_b),
                                (V_LG, 4, ln_g), (V_LB, 4, ln_b), (V_BG, 16, b_gate)):
                    act.dma_start(vec_rows[r:r + n, :], v.rearrange("(k p) -> k p", p=P)).then_inc(vecs_loaded, 16)
                act.dma_start(cw_rows, conv_w).then_inc(cw_loaded, 16)
                act.wait_ge(zeroed, 6)
                act.dma_start(rel_sb[0:NB, :], rel_bias).then_inc(rel_loaded, 16)
                act.dma_start(bucket_sb, bucket_rows).then_inc(rel_loaded, 16)
                act.dma_start(wr_sb[:], w_router.rearrange("(k p) n -> p k n", p=P)).then_inc(router_loaded, 16)
                act.dma_start(br_sb[:], b_router.rearrange("(a n) -> a n", a=1)).then_inc(router_loaded, 16)

            act.wait_ge(x_loaded, 48)
            for i in range(3):
                rows = x_nat[:, i, :] if i < QT else meta_nat[0:META, :]
                n = P if i < QT else META
                nc.scalar.activation(x_scaled[0:n, i, :], rows, ACT.Square,
                                     accum_out=stat[0:n, i:i + 1]).then_inc(ss_ready, 1)
            act.wait_ge(ss_ready, 3)
            act.wait_ge(zeroed, 6)
            nc.scalar.activation(stat[:, 3:5], stat[:, 0:2], ACT.Sqrt, scale=1.0 / D,
                                 bias=eps_col[:]).then_inc(root_ready, 1)
            nc.scalar.activation(stat[0:META, 5:6], stat[0:META, 2:3], ACT.Sqrt, scale=1.0 / D,
                                 bias=eps_col[0:META]).then_inc(root_ready, 1)
            act.wait_ge(vec_ready, 2)
            for k in range(4):
                act.wait_ge(xt_ready, k + 1)
                nc.scalar.activation(hn[:, k, :], ps[k][:, 0:T], ACT.Copy,
                                     scale=vec[:, V_MIX + k:V_MIX + k + 1]).then_inc(hn_act, 1)

            act.wait_ge(toe_ps_ready, 1)
            link(nc.scalar.copy(toe_sb[:, 0:512], ps[4][0:HEADS, :]))
            link(nc.scalar.copy(toe_sb[:, 512:NTOE], ps[5][0:HEADS, 0:NTOE - 512]))
            with nc.allow_non_contiguous_dma(reason="Toeplitz rows"):
                act.dma_start(dram_toe.rearrange("p h j -> h p j"),
                              toe_sb.unsqueeze(1).broadcast_to([HEADS, P, NTOE])).then_inc(toe_stored, 16)
                act.wait_ge(toe_stored, 16)
                for i in range(QT):
                    w = SEEN[i]
                    rows = bass.AP(dram_toe.tensor, T - 1 - META - i * P,
                                   [[HEADS * NTOE - 1, P], [NTOE, HEADS], [1, w]])
                    act.dma_start(probs[i], rows).then_inc(toe_loaded, 16)

            def read_tile(n):
                kind, i, _, _ = tiles[n]
                bank = ps[n % 4]
                act.wait_ge(tile_ready, n + 1)
                if kind == "g":
                    if i >= 2:
                        act.wait_ge(tile_dve, i - 1)
                    ins = nc.scalar.activation(glu_sig[:, i % 2, :], bank[:, 0:T], ACT.Sigmoid)
                elif kind == "iq":
                    ins = nc.scalar.copy(iq[:, i, :], bank[:, 0:SEQ])
                elif kind == "ik" and i == 0:
                    act.wait_ge(pool_done, CONSTS)
                    nc.scalar.copy(ik_half[0:64, 0, :], bank[0:64, 0:T]).then_inc(idx_ready, 1)
                    ins = nc.scalar.copy(iw_t[64:72, :], bank[64:72, META:T])
                elif kind == "ik":
                    ins = nc.scalar.copy(ik_half[64:128, 1, :], bank[64:128, 0:T])
                elif kind == "q":
                    ins = nc.scalar.copy(q_t[:, i, :], bank[:, 0:SEQ])
                elif kind == "k":
                    nc.scalar.copy(k_half[0:64, 2 * i, :], bank[0:64, 0:T]).then_inc(idx_ready, 1)
                    ins = nc.scalar.copy(k_half[64:128, 2 * i + 1, :], bank[64:128, 0:T])
                elif kind == "v":
                    ins = nc.scalar.copy(v_sb[0:KEYN[i], i, :], bank[0:KEYN[i], :])
                else:
                    if i == 0:
                        act.wait_ge(hn_dve, 4)
                    ins = nc.scalar.activation(gates[:, i, :], bank[:, 0:SEQ], ACT.Sigmoid,
                                               bias=vec[:, V_BG + i:V_BG + i + 1])
                ins.then_inc(tile_act, 1)

            for n in range(first["ik"] + 2):
                if tiles[n][0] != "a":
                    read_tile(n)
            act.wait_ge(iw_ps_ready, 1)
            nc.scalar.mul(iw[:], ps[4][:, 0:QT * HEADS].rearrange("p (i h) -> p i h", i=QT),
                          IDX_SCALE).then_inc(iw_ready, 1)
            for m in range(QT * HEADS):
                w = SEEN[m // HEADS]
                act.wait_ge(qk_ready, m + 1)
                if m >= 2:
                    act.wait_ge(relu_used, m - 1)
                nc.scalar.activation(relu[:, m % 2, 0:w], ps[4 + m % 4][:, 0:w], ACT.Relu).then_inc(relu_ready, 1)
            for n in range(first["q"], first["gate"]):
                read_tile(n)

            def softmax_exp(i):
                act.wait_ge(max_ready, i + 1)
                for h in range(HEADS):
                    nc.scalar.activation(probs[i][:, h, :], probs[i][:, h, :], ACT.Exp,
                                         bias=sneg[:, i, h:h + 1],
                                         accum_out=ssum[:, i, h:h + 1]).then_inc(exp_ready, 1)

            def copy_probs(i):
                r0 = 0 if i == 0 else 5
                groups = [(s, g) for s in range(2 + i) for g in range(2)]
                if i == 0:
                    act.wait_ge(conv_out_ready, 1)
                for r, (s, g) in enumerate(groups):
                    act.wait_ge(attn_ps_ready, r0 + r + 1)
                    nc.scalar.copy(probs_t[0:KEYN[s], s, 4 * g:4 * g + 4, :],
                                   ps[4 + (r0 + r) % 4][0:KEYN[s], :].rearrange("p (h q) -> p h q", h=4)
                                   ).then_inc(attn_copied, 1)
                r = r0 + len(groups)
                act.wait_ge(attn_ps_ready, r + 1)
                nc.scalar.copy(attn[:, :, i * P:(i + 1) * P],
                               ps[4 + r % 4][:, :].rearrange("p (c q) -> p c q", c=HP)).then_inc(attn_copied, 1)

            for n in range(first["gate"], first["gate"] + 4):
                read_tile(n)
            softmax_exp(0)
            for n in range(first["gate"] + 4, first["gate"] + 8):
                read_tile(n)
            softmax_exp(1)
            for n in range(first["gate"] + 8, first["gate"] + 12):
                read_tile(n)

            act.wait_ge(centred_ready, 1)
            nc.scalar.activation(squares, centred, ACT.Square).then_inc(squares_ready, 1)
            read_tile(first["gate"] + 12)
            act.wait_ge(var_ready, 1)
            nc.scalar.activation(ln_rows[:, 0, :], ps[5][:, 0:SEQ], ACT.Sqrt,
                                 bias=eps_col[:]).then_inc(ln_root, 1)
            act.wait_ge(normed_ready, 1)
            for c in range(CT):
                nc.scalar.activation(swish[:, c, :], centred[:, c, :], ACT.Sigmoid,
                                     scale=vec[:, V_LG + c:V_LG + c + 1],
                                     bias=vec[:, V_LB + c:V_LB + c + 1]).then_inc(swish_ready, 1)
            for n in range(first["gate"] + 13, NT):
                read_tile(n)
            copy_probs(0)
            copy_probs(1)

            act.wait_ge(logit_ready, QT * HEADS)
            act.dma_start(bu_sb, b_ug).then_inc(ebias_loaded, 16)
            act.dma_start(bd_sb, b_down).then_inc(ebias_loaded, 16)

            for i in range(QT):
                act.wait_ge(h2_ready, 2 * i + 2)
                if i == 0:
                    act.wait_ge(merged_ready, 2 * KD)
                nc.scalar.activation(h_scaled[:, i, :], h2[:, i, :], ACT.Square,
                                     accum_out=stat[:, 6 + i:7 + i]).then_inc(ss_ready, 1)
            act.wait_ge(ss_ready, 5)
            nc.scalar.activation(stat[:, 8:10], stat[:, 6:8], ACT.Sqrt, scale=1.0 / D,
                                 bias=eps_col[:]).then_inc(root_ready, 1)
            for k in range(0, KD, 2):
                act.wait_ge(hst_ready, k // 2 + 1)
                nc.scalar.activation(hf[:, k, :], ps[k // 2][:, 0:SEQ], ACT.Copy,
                                     scale=vec[:, V_FFN + k:V_FFN + k + 1]).then_inc(hf_act, 1)
            act.wait_ge(rmax_ready, 1)
            for i in range(QT):
                nc.scalar.activation(rexp[:, i, :], top8[:, i, 0:4], ACT.Exp, bias=stat[:, 10 + i:11 + i],
                                     accum_out=stat[:, 12 + i:13 + i]).then_inc(rexp_ready, 1)
            act.wait_ge(ct_ready, 1)
            with nc.allow_non_contiguous_dma(reason="one row for every partition"):
                act.dma_start(gfin, norm_final.rearrange("(a n) -> a n", a=1).broadcast_to([P, D])
                              ).then_inc(gfin_loaded, 16)

            act.wait_ge(plan_ready, 1)
            n_bodies = act.value_load(bodies[0:1, 0:1], min_val=PAIRS // 2,
                                      max_val=PASSES * PAIRS // 2)
            for signal in (sig_ready[1], actt_ready[1], givet_ready[1], y_act[1], y_act[0]):
                act.sem_inc(signal, 1)

            def pair(g, b, blocks):
                def sigmoid(e, q):
                    act.wait_ge(gate_read[q], 4 * g + (2 * b + e + 1 + q))
                    act.wait_ge(act_ready[0], 4 * g + (2 * b + e + 1 + q))
                    if q == 0 and (blocks == 2 or e == 0):
                        act.wait_ge(act_ready[1], 4 * g + (2 * b + e + 1))
                    nc.scalar.activation(glu_steps[:, 1, :], glu_steps[:, 0, :], ACT.Sigmoid,
                                         scale=1.702).then_inc(sig_ready[q], 1)

                def copy_act(e, q):
                    act.wait_ge(actt_ps_ready[q], 4 * g + (2 * b + e + 1 + q))
                    nc.scalar.copy(act_t[q][:, e].rearrange("p (h j) n -> p j h n", h=2),
                                   (gate_ps, t0_ps)[q][:, :].rearrange("p (j h n) -> p j h n", j=4, h=2)
                                   ).then_inc(actt_ready[q], 1)

                for e in range(2):
                    for q in range(blocks):
                        sigmoid(e, q)
                        copy_act(e, q)
                for q in range(blocks):
                    act.wait_ge(givet_ps_ready[q], 2 * g + (b + 1 + q))
                    nc.scalar.copy(give_t[q], t1_ps[:, q * SEQ:(q + 1) * SEQ]).then_inc(givet_ready[q], 1)
                act.wait_ge(unit_used, g * BODY_UNITS + (NF + (b + 1) * PAIR_UNITS))
                for q in range(blocks):
                    nc.scalar.copy(y_pair[q][:, 0:512], (t0_ps, gate_ps)[q][:, :]).then_inc(y_act[q], 1)
                if blocks == 1:
                    for signal, n in ((sig_ready[1], 2), (actt_ready[1], 2), (givet_ready[1], 1), (y_act[1], 1)):
                        act.wait_ge(signal, 2 * n * g + (n * b + 1))
                        act.sem_inc(signal, n)

            with act.Fori(0, n_bodies) as g:
                for b in range(2):
                    two = act.value_load(two_blocks[0:1, bass.ds(2 * g + b, 1)], min_val=0, max_val=1)
                    with act.If(two > 0):
                        pair(g, b, 2)
                    with act.Else():
                        pair(g, b, 1)

            for i in range(QT):
                act.wait_ge(sum_ready, 2 * i + 2)
                nc.scalar.activation(h_scaled[:, i, :], h2[:, i, :], ACT.Square,
                                     accum_out=stat[:, 6 + i:7 + i]).then_inc(fin_ss, 1)
            act.wait_ge(fin_ss, 2)
            nc.scalar.activation(stat[:, 8:10], stat[:, 6:8], ACT.Sqrt, scale=1.0 / D,
                                 bias=eps_col[:]).then_inc(fin_root, 1)

        @block.vector
        def _(dve):
            chain = [0]

            def link(ins, behind=0):
                chain[0] += 1
                ins.then_inc(dve_chain, 1)
                if chain[0] > behind:
                    dve.wait_ge(dve_chain, chain[0] - behind)

            dve.wait_ge(vec_ps_ready, 1)
            nc.vector.tensor_copy(vec[:], ps[7][:, 0:V_ROWS]).then_inc(vec_ready, 1)
            nc.vector.tensor_copy(cw[:], ps[6][:, 0:CT * TAPS].rearrange("p (c j) -> p c j", c=CT)
                                  ).then_inc(vec_ready, 1)
            dve.wait_ge(root_ready, 2)
            link(nc.vector.reciprocal(stat[:, 6:8], stat[:, 3:5]))
            link(nc.vector.reciprocal(stat[0:META, 8:9], stat[0:META, 5:6]))
            for i in range(3):
                n = P if i < QT else META
                rows = x_nat[:, i, :] if i < QT else meta_nat[0:META, :]
                nc.vector.tensor_scalar(x_scaled[0:n, i, :], rows, stat[0:n, 6 + i:7 + i], None,
                                        ALU.mult).then_inc(scaled_ready, 1)
            for k in range(4, KD):
                dve.wait_ge(xt_ready, k + 1)
                nc.vector.tensor_scalar(hn[:, k, :], ps[k][:, 0:T], vec[:, V_MIX + k:V_MIX + k + 1], None,
                                        ALU.mult).then_inc(hn_dve, 1)
            dve.wait_ge(pool_done, CONSTS)
            for n, (kind, i, _, _) in enumerate(tiles):
                if kind == "a":
                    dve.wait_ge(tile_ready, n + 1)
                    dve.wait_ge(tile_act, i + 1)
                    nc.vector.tensor_tensor(glu[:, i, TAPS - 1:], ps[n % 4][:, 0:T], glu_sig[:, i % 2, :],
                                            ALU.mult).then_inc(tile_dve, 1)

            dve.wait_ge(iw_ready, 1)
            for m in range(QT * HEADS):
                i, h = divmod(m, HEADS)
                w = SEEN[i]
                dve.wait_ge(relu_ready, m + 1)
                if h:
                    dve.wait_ge(relu_used, m)
                nc.vector.scalar_tensor_tensor(
                    out=score[:, i, 0:w], in0=relu[:, m % 2, 0:w], scalar=iw[:, i, h:h + 1],
                    in1=(score if h else seen_bias)[:, i, 0:w], op0=ALU.mult,
                    op1=ALU.add).then_inc(relu_used, 1)
            dve.wait_ge(relu_used, QT * HEADS)
            for r in range(TOPK // 8):
                for i in range(QT):
                    link(nc.vector.max(top8[:, i, :], score[:, i, 0:SEEN[i]]), behind=1)
                for i in range(QT):
                    link(nc.vector.match_replace(score[:, i, 0:SEEN[i]], top8[:, i, :],
                                                 score[:, i, 0:SEEN[i]], TAKEN), behind=1)
            link(nc.vector.tensor_scalar(ssum[:, 0, :], iw[:, 0, :], 0.0, None, ALU.mult))
            for i in range(QT):
                nc.vector.tensor_scalar(seen_bias[:, i, 0:SEEN[i]], score[:, i, 0:SEEN[i]],
                                        0.5 * TAKEN, FAR, ALU.is_gt, ALU.mult).then_inc(seen_ready, 1)

            def convolve(c0, c1):
                n = c1 - c0
                link(nc.vector.memset(stat[:, 15:16], 0.0))
                for j in range(TAPS):
                    for c in range(c0, c1):
                        src = glu[:, c, META + j:META + j + SEQ]
                        if j == 0:
                            ins = nc.vector.tensor_scalar(conv[:, c, :], src, cw[:, c, 0:1],
                                                          vec[:, V_CB + c:V_CB + c + 1], ALU.mult, ALU.add)
                        else:
                            ins = nc.vector.scalar_tensor_tensor(
                                out=conv[:, c, :], in0=src, scalar=cw[:, c, j:j + 1],
                                in1=conv[:, c, :], op0=ALU.mult, op1=ALU.add)
                        link(ins, behind=n - 1)

            def softmax_logits(i):
                w = SEEN[i]
                dve.wait_ge(bias_ready, i + 1)
                for h in range(HEADS):
                    m = QT * HEADS + i * HEADS + h
                    dve.wait_ge(qk_ready, m + 1)
                    nc.vector.scalar_tensor_tensor(
                        out=probs[i][:, h, :], in0=ps[4 + m % 4][:, 0:w], scalar=DH ** -0.5,
                        in1=probs[i][:, h, :], op0=ALU.mult, op1=ALU.add).then_inc(logit_ready, 1)
                dve.wait_ge(logit_ready, HEADS * (i + 1))
                link(nc.vector.tensor_reduce(smax[:, i, :], probs[i], AX_X, ALU.max))
                nc.vector.tensor_scalar(sneg[:, i, :], smax[:, i, :], -1.0, None, ALU.mult).then_inc(max_ready, 1)

            def softmax_scale(i):
                dve.wait_ge(exp_ready, HEADS * (i + 1))
                link(nc.vector.reciprocal(srec[:, i, :], ssum[:, i, :]))
                nc.vector.tensor_tensor(probs[i], probs[i],
                                        srec[:, i, :].unsqueeze(2).broadcast_to([P, HEADS, SEEN[i]]),
                                        ALU.mult).then_inc(prob_ready, 1)

            convolve(0, 2)
            softmax_logits(0)
            softmax_logits(1)
            convolve(2, 4)
            link(nc.vector.memset(stat[:, 15:16], 0.0))
            nc.vector.memset(stat[:, 15:16], 0.0).then_inc(conv_ready, 1)
            softmax_scale(0)
            softmax_scale(1)
            dve.wait_ge(mean_ready, 1)
            nc.vector.tensor_tensor(centred, conv, ps[4][:, 0:SEQ].unsqueeze(1).broadcast_to([P, CT, SEQ]),
                                    ALU.subtract).then_inc(centred_ready, 1)
            dve.wait_ge(ln_root, 1)
            link(nc.vector.reciprocal(ln_rows[:, 1, :], ln_rows[:, 0, :]))
            nc.vector.tensor_tensor(centred, centred, ln_rows[:, 1, :].unsqueeze(1).broadcast_to([P, CT, SEQ]),
                                    ALU.mult).then_inc(normed_ready, 1)
            dve.wait_ge(normed_ready, 1)
            for c in range(CT):
                link(nc.vector.tensor_scalar(conv[:, c, :], centred[:, c, :], vec[:, V_LG + c:V_LG + c + 1],
                                             vec[:, V_LB + c:V_LB + c + 1], ALU.mult, ALU.add))
            dve.wait_ge(swish_ready, CT)
            nc.vector.tensor_tensor(conv, conv, swish, ALU.mult).then_inc(conv_out_ready, 1)

            for half in range(2):
                for k in range(KD):
                    n = NT + half * KD + k
                    dve.wait_ge(tile_ready, n + 1)
                    if half == 0:
                        dve.wait_ge(tile_act, NT - 4)
                        nc.vector.tensor_tensor(merged[:, k, :], ps[n % 4][:, 0:SEQ], gates[:, k, :],
                                                ALU.mult).then_inc(tile_dve, 1)
                    else:
                        nc.vector.tensor_tensor(gates[:, KD + k, :], ps[n % 4][:, 0:SEQ],
                                                gates[:, KD + k, :], ALU.mult).then_inc(tile_dve, 1)
                        dve.wait_ge(tile_dve, 4 + KD + k + 1)
                        nc.vector.tensor_tensor(merged[:, k, :], merged[:, k, :], gates[:, KD + k, :],
                                                ALU.add).then_inc(merged_ready, 2)
            dve.wait_ge(attn_copied, 12)
            dve.wait_ge(h2_ps_ready, 1)
            for i in range(QT):
                for c in range(2):
                    nc.vector.tensor_tensor(h2[:, i, c * 512:(c + 1) * 512], ps[4 + 2 * i + c][:, :],
                                            x_nat[:, i, c * 512:(c + 1) * 512], ALU.add).then_inc(h2_ready, 1)
            dve.wait_ge(root_ready, 3)
            link(nc.vector.reciprocal(stat[:, 6:8], stat[:, 8:10]))
            for i in range(QT):
                nc.vector.tensor_scalar(h_scaled[:, i, :], h2[:, i, :], stat[:, 6 + i:7 + i], None,
                                        ALU.mult).then_inc(hs_ready, 1)
            for k in range(1, KD, 2):
                dve.wait_ge(hst_ready, k // 2 + 1)
                dve.wait_ge(hf_act, k // 2 + 1)
                nc.vector.tensor_scalar(hf[:, k, :], ps[k // 2][:, SEQ:2 * SEQ],
                                        vec[:, V_FFN + k:V_FFN + k + 1], None, ALU.mult).then_inc(hf_dve, 1)

            dve.wait_ge(rlog_ready, 1)
            link(nc.vector.tensor_copy(rlog[:], ps[4][:, 0:QT * E].rearrange("p (i e) -> p i e", i=QT)))
            for i in range(QT):
                link(nc.vector.max(top8[:, i, :], rlog[:, i, :]))
                link(nc.vector.max_index(ridx[:, i, :], top8[:, i, :], rlog[:, i, :]))
                link(nc.vector.tensor_scalar(stat[:, 10 + i:11 + i], top8[:, i, 0:1], -1.0, None, ALU.mult))
            nc.vector.tensor_copy(ridxf[:], ridx[:]).then_inc(rmax_ready, 1)
            dve.wait_ge(rmax_ready, 1)
            dve.wait_ge(rexp_ready, QT)
            link(nc.vector.reciprocal(stat[:, 14:16], stat[:, 12:14]))
            for i in range(QT):
                for j in range(4):
                    link(nc.vector.tensor_scalar(hot[:, i, j, :], number[:, 0:E], ridxf[:, i, j:j + 1], None,
                                                 ALU.is_equal), behind=3)
            link(nc.vector.memset(counts[:, 7:8], 0.0))
            for i in range(QT):
                link(nc.vector.tensor_scalar(rexp[:, i, :], rexp[:, i, :], stat[:, 14 + i:15 + i], None, ALU.mult))
                link(nc.vector.tensor_reduce(chosen[:, i, :], hot[:, i].rearrange("p j e -> p e j"), AX_X, ALU.add))
                link(nc.vector.tensor_scalar(combine_w[:, i, :], hot[:, i, 0, :], rexp[:, i, 0:1], None, ALU.mult))
                for j in range(1, 4):
                    link(nc.vector.scalar_tensor_tensor(
                        out=combine_w[:, i, :], in0=hot[:, i, j, :], scalar=rexp[:, i, j:j + 1],
                        in1=combine_w[:, i, :], op0=ALU.mult, op1=ALU.add))
            nc.vector.memset(counts[:, 6:7], 0.0).then_inc(choice_ready, 1)

            dve.wait_ge(place_ps_ready, 1)
            link(nc.vector.tensor_copy(combine_t[:], ps[6][0:E, 0:SEQ]))
            nc.vector.memset(counts[:, 6:7], 0.0).then_inc(ct_ready, 1)
            where = ps[5][:, 0:QT * E].rearrange("p (i e) -> p i e", i=QT)
            link(nc.vector.scalar_tensor_tensor(out=place[:, :, 0:E], in0=where, scalar=1.0, in1=chosen[:],
                                                op0=ALU.add, op1=ALU.mult))
            link(nc.vector.tensor_scalar(place[:, :, 0:E], place[:, :, 0:E], -1.0, None, ALU.add))
            for q in range(1, PASSES):
                link(nc.vector.tensor_scalar(place[:, :, q * E:(q + 1) * E], place[:, :, 0:E],
                                             -float(q * PASS_CAP), None, ALU.add))
            for q in range(PASSES):
                link(nc.vector.tensor_copy(weight[:, :, q * E:(q + 1) * E], combine_w[:]))
            per_expert = ps[5][:, QT * E:(QT + 1) * E]
            link(nc.vector.tensor_reduce(counts[:, 0:1], per_expert, AX_X, ALU.max))
            link(nc.vector.tensor_scalar(counts[:, 4:5], counts[:, 0:1], float(PASS_CAP),
                                         float(PAIRS // 2), ALU.is_gt, ALU.mult))
            link(nc.vector.tensor_reduce(fuller[:], per_expert.rearrange("p (i e) -> p i e", e=2), AX_X, ALU.max))
            for q in range(PASSES):
                link(nc.vector.tensor_scalar(two_blocks[:, q * PAIRS:(q + 1) * PAIRS], fuller[:],
                                             float(q * PASS_CAP + CAP), None, ALU.is_gt))
            link(nc.vector.tensor_scalar(bodies[:], counts[:, 4:5], float(PAIRS // 2), None, ALU.add))
            dve.wait_ge(gfin_loaded, 16)
            nc.vector.memset(counts[:, 6:7], 0.0).then_inc(plan_ready, 1)
            dve.wait_ge(plan_ready, 1)

            def one_hot(pair_expert, q, dst, weighted, signal):
                for i in range(QT):
                    for e in range(2):
                        nc.vector.tensor_scalar(
                            dst[:, i, e * CAP:(e + 1) * CAP], number[:, q * CAP:(q + 1) * CAP],
                            place[:, i, bass.ds(pair_expert + e, 1)],
                            weight[:, i, bass.ds(pair_expert + e, 1)] if weighted else None,
                            ALU.is_equal, *([ALU.mult] if weighted else [])).then_inc(signal, 1)

            def plan_pick(pair_expert, bank, expert_mod):
                one_hot(pair_expert, 0, pick[0], False, pick_ready)
                for e in range(2):
                    nc.vector.tensor_copy(choose[0:E, bank, e * CAP:(e + 1) * CAP],
                                          ident[0:E, bass.ds(expert_mod + e, 1)].broadcast_to([E, CAP])
                                          ).then_inc(pick_ready, 1)

            def copy_picked(dst, q, value):
                dve.wait_ge(gather_ready[q], value)
                for j, src in enumerate((t0_ps, t1_ps)):
                    g_ffn = vec[:, V_FFN + 4 * j:V_FFN + 4 * j + 4].unsqueeze(2).broadcast_to([P, 4, P])
                    nc.vector.tensor_tensor(dst[:, 4 * j:4 * j + 4, :],
                                            src[:, :].rearrange("p (k n) -> p k n", k=4), g_ffn,
                                            ALU.mult).then_inc(picked_ready[q], 1)

            plan_pick(0, 0, 0)
            copy_picked(picked[:, 0], 0, 1)
            for signal, n in ((pick2_ready, 1), (picked_ready[1], 1), (gate_read[1], 1), (clipped[0], 2),
                              (clipped[1], 2), (act_ready[0], 1), (act_ready[1], 1), (y_dve[0], 1), (y_dve[1], 1)):
                dve.sem_inc(signal, n)
            n_bodies = dve.value_load(bodies[0:1, 0:1], min_val=PAIRS // 2,
                                      max_val=PASSES * PAIRS // 2)

            def pair(g, b, blocks):
                def swiglu(e, q):
                    dve.wait_ge(unit_used, g * BODY_UNITS + (NF + b * PAIR_UNITS + (e + 1) * UP_UNITS))
                    n = 4 * g + (2 * b + e + 1)
                    gate, lin = ((gate_ps, up_ps), (t0_ps, t1_ps))[q]
                    nc.vector.tensor_scalar(glu_steps[:, 0, :], gate[:, :], 7.0, None,
                                            ALU.min).then_inc(gate_read[q], 1)
                    dve.wait_ge(act_ready[0], n + (1 if q else 0))
                    if q == 0 and (blocks == 2 or e == 0):
                        dve.wait_ge(act_ready[1], n)
                    nc.vector.tensor_scalar(glu_steps[:, 2, :], lin[:, :], 7.0, -7.0, ALU.min,
                                            ALU.max).then_inc(clipped[q], 1)
                    dve.wait_ge(clipped[q], 2 * n + 1)
                    nc.vector.scalar_tensor_tensor(
                        out=glu_steps[:, 2, :], in0=glu_steps[:, 2, :], scalar=1.0, in1=glu_steps[:, 0, :],
                        op0=ALU.add, op1=ALU.mult).then_inc(clipped[q], 1)
                    dve.wait_ge(clipped[q], 2 * n + 2)
                    dve.wait_ge(sig_ready[q], n + q)
                    nc.vector.tensor_tensor(glu_steps[:, 3, :], glu_steps[:, 2, :], glu_steps[:, 1, :],
                                            ALU.mult).then_inc(act_ready[q], 1)

                if blocks == 2:
                    one_hot(4 * g + 2 * b, 1, pick[1], False, pick2_ready)
                    one_hot(4 * g + 2 * b, 1, give[1], True, pick2_ready)
                    copy_picked(picked2, 1, 2 * g + (b + 2))
                one_hot(4 * g + 2 * b, 0, give[0], True, pick_ready)
                plan_pick(4 * g + (2 * b + 2), 1 - b, (4 * g + (2 * b + 2)) % E)
                swiglu(0, 0)
                if blocks == 2:
                    swiglu(0, 1)
                copy_picked(picked[:, 1 - b], 0, 2 * g + (b + 2))
                for q in range(blocks):
                    swiglu(1, q)
                dve.wait_ge(unit_used, g * BODY_UNITS + (NF + (b + 1) * PAIR_UNITS))
                for q in range(blocks):
                    nc.vector.tensor_copy(y_pair[q][:, 512:1024], (t1_ps, up_ps)[q][:, :]).then_inc(y_dve[q], 1)
                if blocks == 1:
                    for signal, n, n0 in ((pick2_ready, 8, 1), (picked_ready[1], 2, 1), (gate_read[1], 2, 1),
                                          (clipped[1], 4, 2), (act_ready[1], 2, 1), (y_dve[1], 1, 1)):
                        dve.wait_ge(signal, 2 * n * g + (n * b + n0))
                        dve.sem_inc(signal, n)

            with dve.Fori(0, n_bodies) as g:
                for b in range(2):
                    two = dve.value_load(two_blocks[0:1, bass.ds(2 * g + b, 1)], min_val=0, max_val=1)
                    with dve.If(two > 0):
                        pair(g, b, 2)
                    with dve.Else():
                        pair(g, b, 1)

            dve.wait_ge(combined[0], n_bodies * 2)
            dve.wait_ge(combined[1], n_bodies * 2 + 1)
            for i in range(QT):
                for c in range(2):
                    part = h2[:, i, c * 512:(c + 1) * 512]
                    nc.vector.tensor_tensor(part, acc[2 * i + c][:, :], part, ALU.add).then_inc(sum_ready, 1)
            dve.wait_ge(fin_root, 1)
            nc.vector.reciprocal(stat[:, 6:8], stat[:, 8:10]).then_inc(sum_ready, 1)
            dve.wait_ge(sum_ready, 5)
            for i in range(QT):
                nc.vector.scalar_tensor_tensor(out=x_nat[:, i, :], in0=h2[:, i, :], scalar=stat[:, 6 + i:7 + i],
                                               in1=gfin, op0=ALU.mult, op1=ALU.mult).then_inc(fin_ready, 1)

        @block.tensor
        def _(pe):
            mm = nc.tensor.matmul

            pe.wait_ge(pool_done, 1)
            pe.wait_ge(vecs_loaded, 96)
            pe.wait_ge(cw_loaded, 16)
            for c in range(CT):
                nc.tensor.transpose(ps[6][:, c * TAPS:(c + 1) * TAPS], cw_rows[:, c * P:(c + 1) * P],
                                    ident[0:TAPS, 0:TAPS])
            nc.tensor.transpose(ps[7][:, 0:V_ROWS], vec_rows, ident[0:V_ROWS, 0:V_ROWS]).then_inc(vec_ps_ready, 1)

            pe.wait_ge(scaled_ready, 3)
            for k in range(KD):
                if k >= 6:
                    pe.wait_ge(vec_ready, 2)
                for i, (t0, n) in enumerate(((META, P), (META + P, P), (0, META))):
                    ins = nc.tensor.transpose(ps[k][:, t0:t0 + n], x_scaled[0:n, i, k * P:(k + 1) * P],
                                              ident[0:n, 0:n])
                ins.then_inc(xt_ready, 1)
            pe.wait_ge(rel_loaded, 32)
            pe.wait_ge(hn_dve, 2)
            mm(ps[4][0:HEADS, :], rel_sb[:], bucket_sb[:, 0:512], start=True, stop=True)
            mm(ps[5][0:HEADS, 0:NTOE - 512], rel_sb[:], bucket_sb[:, 512:NTOE], start=True,
               stop=True).then_inc(toe_ps_ready, 1)
            pe.wait_ge(hn_act, 4)
            pe.wait_ge(hn_dve, 4)

            def front_unit(u, n, kk=KD):
                pe.wait_ge(slot_loaded[slot_of(u)], 16 * (loads_before(u) + 1))
                return ring[:, slot_of(u), 0:kk * n].rearrange("p (k n) -> p k n", k=kk)

            used = [0]

            def project(n):
                kind, i, u, c = tiles[n]
                if n >= 4:
                    pe.wait_ge(*read_by(n - 4))
                bank = ps[n % 4]
                if kind == "v":
                    ws = [front_unit(u + j, UNIT_COLS) for j in range(2)]
                    for j, w in enumerate(ws):
                        for k in range(KD):
                            ins = mm(bank[0:KEYN[i], j * UNIT_COLS:(j + 1) * UNIT_COLS],
                                     hn[:, k, KEY0[i]:KEY0[i] + KEYN[i]], w[:, k, :],
                                     start=(k == 0), stop=(k == KD - 1))
                elif kind == "ik":
                    w = front_unit(u, C_GLU - C_IK)
                    rows = slice(0, 72) if i == 0 else slice(64, 128)
                    cols = slice(0, 72) if i == 0 else slice(0, 64)
                    for k in range(KD):
                        ins = mm(bank[rows, 0:T], w[:, k, cols], hn[:, k, :], start=(k == 0), stop=(k == KD - 1))
                else:
                    w = front_unit(u, UNIT_COLS)
                    t0 = 0 if kind in ("g", "a", "k") else META
                    for k in range(KD):
                        ins = mm(bank[:, 0:T - t0], w[:, k, c:c + P], hn[:, k, t0:T],
                                 start=(k == 0), stop=(k == KD - 1))
                ins.then_inc(tile_ready, 1)
                nxt = tiles[n + 1][2] if n + 1 < NT else U_AO
                if nxt != u:
                    pe.wait_ge(tile_ready, n + 1)
                    pe.sem_inc(unit_used, nxt - u)

            for n in range(first["ik"] + 2):
                project(n)
            pe.wait_ge(tile_act, first["ik"] + 1 - 4 + 1)
            for i in range(QT):
                ins = nc.tensor.transpose(ps[4][:, i * HEADS:(i + 1) * HEADS], iw_t[64:72, i * P:(i + 1) * P],
                                          ident[64:72, 64:72])
            ins.then_inc(iw_ps_ready, 1)
            pe.wait_ge(iw_ready, 1)
            pe.wait_ge(idx_ready, 1)
            for m in range(QT * HEADS):
                i, h = divmod(m, HEADS)
                if m >= 4:
                    pe.wait_ge(relu_ready, m - 3)
                mm(ps[4 + m % 4][:, 0:SEEN[i]], iq[:, h // 2, i * P:(i + 1) * P], ik_half[:, h % 2, 0:SEEN[i]],
                   start=True, stop=True).then_inc(qk_ready, 1)
            for n in range(first["q"], first["gate"]):
                project(n)
            pe.wait_ge(tile_act, first["k"] + 4 - 4)
            pe.wait_ge(idx_ready, 5)
            for j in range(QT * HEADS):
                m = QT * HEADS + j
                i, h = divmod(j, HEADS)
                if j < 4:
                    pe.wait_ge(relu_ready, m - 3)
                else:
                    pe.wait_ge(logit_ready, j - 3)
                mm(ps[4 + m % 4][:, 0:SEEN[i]], q_t[:, h // 2, i * P:(i + 1) * P], k_half[:, h, 0:SEEN[i]],
                   start=True, stop=True).then_inc(qk_ready, 1)
                if j % 2:
                    project(first["gate"] + j // 2)
            for n in range(first["gate"] + 8, first["gate"] + 12):
                project(n)
            pe.wait_ge(conv_ready, 1)
            pe.wait_ge(logit_ready, QT * HEADS)
            for c in range(CT):
                ins = mm(ps[4][:, 0:SEQ], mean_w[:], conv[:, c, :], start=(c == 0), stop=(c == CT - 1))
            ins.then_inc(mean_ready, 1)
            project(first["gate"] + 12)
            pe.wait_ge(squares_ready, 1)
            for c in range(CT):
                ins = mm(ps[5][:, 0:SEQ], mean_w[:], squares[:, c, :], start=(c == 0), stop=(c == CT - 1))
            ins.then_inc(var_ready, 1)
            for n in range(first["gate"] + 13, NT):
                project(n)

            def attend(i):
                r0 = 0 if i == 0 else 5
                pe.wait_ge(prob_ready, i + 1)
                if i == 0:
                    pe.wait_ge(ln_root, 1)
                    pe.wait_ge(centred_ready, 1)
                r = r0
                for s in range(2 + i):
                    for half in range(2):
                        if r >= 4:
                            pe.wait_ge(attn_copied, r - 3)
                        for j in range(4):
                            ins = nc.tensor.transpose(
                                ps[4 + r % 4][0:KEYN[s], j * P:(j + 1) * P],
                                probs[i][:, 4 * half + j, KEY0[s]:KEY0[s] + KEYN[s]], ident[:])
                        ins.then_inc(attn_ps_ready, 1)
                        r += 1
                pe.wait_ge(attn_copied, r)
                bank = ps[4 + r % 4]
                for h in range(HEADS):
                    for s in range(2 + i):
                        ins = mm(bank[(h % 2) * DH:(h % 2 + 1) * DH, (h // 2) * P:(h // 2 + 1) * P],
                                 v_sb[0:KEYN[s], s, h * DH:(h + 1) * DH], probs_t[0:KEYN[s], s, h, :],
                                 start=(s == 0), stop=(s == 1 + i))
                ins.then_inc(attn_ps_ready, 1)

            attend(0)
            attend(1)

            for half, (u, src) in enumerate(((U_AO, attn), (U_CO, conv))):
                ws = [front_unit(u + j, D, 2) for j in range(2)]
                if half == 0:
                    pe.wait_ge(attn_copied, 12)
                else:
                    pe.wait_ge(conv_out_ready, 1)
                for k in range(KD):
                    n = NT + half * KD + k
                    pe.wait_ge(*read_by(n - 4))
                    for q in range(4):
                        ins = mm(ps[n % 4][:, 0:SEQ], ws[q // 2][:, q % 2, k * P:(k + 1) * P], src[:, q, :],
                                 start=(q == 0), stop=(q == 3))
                    ins.then_inc(tile_ready, 1)
                pe.wait_ge(tile_ready, NT + (half + 1) * KD)
                pe.sem_inc(unit_used, 2)
            for k in range(KD):
                w = front_unit(U_WO + k // 2, D, 2)
                pe.wait_ge(merged_ready, 2 * (k + 1))
                for i in range(QT):
                    for c in range(2):
                        ins = mm(ps[4 + 2 * i + c][:, :], merged[:, k, i * P:(i + 1) * P],
                                 w[:, k % 2, c * 512:(c + 1) * 512], start=(k == 0), stop=(k == KD - 1))
                if k % 2:
                    ins.then_inc(unit_used, 1)
            pe.wait_ge(unit_used, NF)
            pe.sem_inc(h2_ps_ready, 1)

            pe.wait_ge(hs_ready, QT)
            for k in range(0, KD, 2):
                for kk in range(2):
                    for i in range(QT):
                        c0 = kk * SEQ + i * P
                        ins = nc.tensor.transpose(ps[k // 2][:, c0:c0 + P],
                                                  h_scaled[:, i, (k + kk) * P:(k + kk + 1) * P], ident[:])
                ins.then_inc(hst_ready, 1)
            pe.wait_ge(router_loaded, 32)
            pe.wait_ge(hf_act, 4)
            pe.wait_ge(hf_dve, 4)
            for i in range(QT):
                o = ps[4][:, i * E:(i + 1) * E]
                mm(o, ones[0:1, :], br_sb[:], start=True, stop=False)
                for k in range(KD):
                    ins = mm(o, hf[:, k, i * P:(i + 1) * P], wr_sb[:, k, :], start=False, stop=(k == KD - 1))
            ins.then_inc(rlog_ready, 1)
            pe.wait_ge(choice_ready, 1)
            mm(ps[5][:, 0:E], before[:], chosen[:, 0, :], start=True, stop=True)
            mm(ps[5][:, E:2 * E], ones[:], chosen[:, 0, :], start=True, stop=False)
            mm(ps[5][:, E:2 * E], before[:], chosen[:, 1, :], start=False, stop=True)
            mm(ps[5][:, 2 * E:3 * E], ones[:], chosen[:, 0, :], start=True, stop=False)
            mm(ps[5][:, 2 * E:3 * E], ones[:], chosen[:, 1, :], start=False, stop=True)
            for i in range(QT):
                ins = nc.tensor.transpose(ps[6][0:E, i * P:(i + 1) * P], combine_w[:, i, :], ident[:])
            ins.then_inc(place_ps_ready, 1)
            pe.wait_ge(ct_ready, 1)
            pe.wait_ge(ebias_loaded, 32)
            for i in range(QT):
                for c in range(2):
                    mm(acc[2 * i + c][:, :], combine_t[:, i * P:(i + 1) * P], bd_sb[:, c * 512:(c + 1) * 512],
                       start=True, stop=False, skip_group_check=True)

            def gather(q):
                for k in range(KD):
                    for i in range(QT):
                        ins = mm((t0_ps, t1_ps)[k // 4][:, (k % 4) * P:(k % 4 + 1) * P],
                                 h_scaled[:, i, k * P:(k + 1) * P], pick[q][:, i, :],
                                 start=(i == 0), stop=(i == QT - 1))
                ins.then_inc(gather_ready[q], 1)

            pe.wait_ge(pick_ready, 6)
            gather(0)
            for signal in (gather_ready[1], actt_ps_ready[1], givet_ps_ready[1], combined[1]):
                pe.sem_inc(signal, 1)
            n_bodies = pe.value_load(bodies[0:1, 0:1], min_val=PAIRS // 2,
                                     max_val=PASSES * PAIRS // 2)
            def pair(g, b, blocks):
                def unit(j):
                    u = NF + b * PAIR_UNITS + j
                    pe.wait_ge(slot_loaded[slot_of(u)], g * (16 * TURNS) + 16 * (loads_before(u) + 1))
                    return ring[:, slot_of(u), :]

                def up(e):
                    pe.wait_ge(clipped[0], 8 * g + (2 * (2 * b + e) + 2))
                    outs = [(q, c, bank, half) for q in range(blocks)
                            for c, (bank, half) in enumerate([(((gate_ps, up_ps), (t0_ps, t1_ps))[q][w], half)
                                                              for w in range(2) for half in range(2)])]
                    for q, c, bank, half in outs[::-1]:
                        if e == 1 and (q, c) == (0, 1):
                            pe.wait_ge(actt_ready[0], 4 * g + (2 * b + 1))
                        mm(bank[half * CAP:(half + 1) * CAP, :], choose[0:E, b, e * CAP:(e + 1) * CAP],
                           bu_sb[:, c * 512:(c + 1) * 512], start=True, stop=False)
                    for k in range(UP_UNITS):
                        w = unit(e * UP_UNITS + k)
                        for q, c, bank, half in outs:
                            tokens = (picked[:, b], picked2)[q]
                            ins = mm(bank[half * CAP:(half + 1) * CAP, :], tokens[:, k, e * CAP:(e + 1) * CAP],
                                     w[:, c * 512:(c + 1) * 512], start=False, stop=(k == UP_UNITS - 1))
                        ins.then_inc(unit_used, 1)

                def transpose_act(e, q):
                    pe.wait_ge(act_ready[q], 4 * g + (2 * b + e + 2))
                    for j in range(4):
                        ins = nc.tensor.transpose((gate_ps, t0_ps)[q][:, j * P:(j + 1) * P],
                                                  glu_steps[:, 3, j * P:(j + 1) * P], ident[:])
                    ins.then_inc(actt_ps_ready[q], 1)

                for q in range(2):
                    pe.wait_ge(y_act[q], 2 * g + (b + 1))
                    pe.wait_ge(y_dve[q], 2 * g + (b + 1))
                if blocks == 2:
                    pe.wait_ge(pick2_ready, 16 * g + (8 * b + 9))
                    gather(1)
                    pe.wait_ge(picked_ready[1], 4 * g + (2 * b + 3))
                pe.wait_ge(picked_ready[0], 4 * g + (2 * b + 2))
                up(0)
                if blocks == 2:
                    transpose_act(0, 0)
                    pe.wait_ge(clipped[1], 8 * g + (4 * b + 4))
                pe.wait_ge(pick_ready, 20 * g + (6 + 10 * (b + 1)))
                gather(0)
                if blocks == 1:
                    transpose_act(0, 0)
                else:
                    pe.wait_ge(picked_ready[0], 4 * g + (2 * b + 4))
                    transpose_act(0, 1)
                    pe.wait_ge(actt_ready[1], 4 * g + (2 * b + 2))
                up(1)
                if blocks == 2:
                    transpose_act(1, 0)
                    pe.wait_ge(clipped[1], 8 * g + (4 * b + 6))
                else:
                    pe.wait_ge(picked_ready[0], 4 * g + (2 * b + 4))
                for q in range(blocks):
                    for i in range(QT):
                        ins = nc.tensor.transpose(t1_ps[:, q * SEQ + i * P:q * SEQ + (i + 1) * P],
                                                  give[q][:, i, :], ident[:])
                    ins.then_inc(givet_ps_ready[q], 1)
                transpose_act(1, blocks - 1)
                for q in range(blocks):
                    pe.wait_ge(actt_ready[q], 4 * g + (2 * b + 2 + q))
                for q in range(blocks):
                    pe.wait_ge(givet_ready[q], 2 * g + (b + 1 + q))
                for f in range(DOWN_UNITS):
                    w = unit(2 * UP_UNITS + f)
                    for q in range(blocks):
                        for c in range(2):
                            bank = ((t0_ps, t1_ps), (gate_ps, up_ps))[q][c]
                            for e in range(2):
                                ins = mm(bank[e * CAP:(e + 1) * CAP, :], act_t[q][:, e, f, :],
                                         w[:, e * D + c * 512:e * D + (c + 1) * 512],
                                         start=(f == 0), stop=(f == DOWN_UNITS - 1))
                    ins.then_inc(unit_used, 1)
                for q in range(blocks):
                    pe.wait_ge(y_act[q], 2 * g + (b + 2))
                    pe.wait_ge(y_dve[q], 2 * g + (b + 2))
                    for i in range(QT):
                        for c in range(2):
                            ins = mm(acc[2 * i + c][:, :], give_t[q][:, i * P:(i + 1) * P],
                                     y_pair[q][:, c * 512:(c + 1) * 512], start=False, stop=False,
                                     skip_group_check=True)
                    ins.then_inc(combined[q], 1)
                if blocks == 1:
                    for signal, n in ((gather_ready[1], 1), (actt_ps_ready[1], 2), (givet_ps_ready[1], 1),
                                      (combined[1], 1)):
                        pe.wait_ge(signal, 2 * n * g + (n * b + 1))
                        pe.sem_inc(signal, n)

            with pe.Fori(0, n_bodies) as g:
                for b in range(2):
                    two = pe.value_load(two_blocks[0:1, bass.ds(2 * g + b, 1)], min_val=0, max_val=1)
                    with pe.If(two > 0):
                        pair(g, b, 2)
                    with pe.Else():
                        pair(g, b, 1)


def bucket_rows():
    j = np.arange(NTOE)
    dist = T - 1 - j
    n = np.maximum(dist, 0)
    exact = NB // 2
    large = exact + (np.log(np.maximum(n, 1) / exact) / np.log(128 / exact) * (NB - exact)).astype(np.int32)
    bucket = np.where(n < exact, n, np.minimum(large, NB - 1))
    rows = np.zeros((NB + 1, NTOE), np.float32)
    rows[bucket[dist >= 0], j[dist >= 0]] = 1.0
    rows[NB, dist < 0] = FAR
    return rows


def kernel(**inputs):
    import concourse.bacc as bacc
    from concourse.bass_utils import run_bass_kernel_spmd

    a = {k: np.ascontiguousarray(v) for k, v in inputs.items()}
    order = ["x", "meta_tokens", "rel_bias", "norm_mix", "w_in", "b_gate", "w_attn_out", "conv_w", "conv_b",
             "conv_ln_g", "conv_ln_b", "w_conv_out", "w_out", "norm_ffn", "w_router", "b_router",
             "w_up_gate", "b_up_gate", "w_down", "b_down", "norm_final"]
    whole = ("meta_tokens", "rel_bias", "norm_final")
    nc = bacc.Bacc("TRN2", target_bir_lowering=False, num_devices=1)
    arrays, args = {}, []
    for name in order:
        v = a[name] if name in whole else a[name][0]
        arrays["in_" + name] = v
        args.append(nc.dram_tensor("in_" + name, v.shape, F32, kind="ExternalInput").ap())
    arrays["in_bucket_rows"] = bucket_rows()
    args.append(nc.dram_tensor("in_bucket_rows", (NB + 1, NTOE), F32, kind="ExternalInput").ap())
    args.append(nc.dram_tensor("out", (SEQ, D), F32, kind="ExternalOutput").ap())
    layer(nc, *args)
    r = run_bass_kernel_spmd(nc, [arrays], core_ids=[0])
    return r.results[0]["out"].reshape(1, SEQ, D)
```

```python
from contextlib import ExitStack

import numpy as np

import concourse.bass as bass
from concourse import mybir

F32 = mybir.dt.float32
I32 = mybir.dt.int32
U32 = mybir.dt.uint32
ALU = mybir.AluOpType
ACT = mybir.ActivationFunctionType
AX_X = mybir.AxisListType.X

P = 128
META = 16
D = 1024
KD = D // P
SEQ = 256
QT = SEQ // P
T = META + SEQ
HEADS = 8
DH = 64
HP = HEADS // 2
TOPK = 64
IDX_SCALE = (64 ** -0.5) * (8 ** -0.5)
CH = 512
CT = CH // P
TAPS = 31
NB = 32
E = 32
FF = 1024
CAP = 64
PASS_CAP = 2 * CAP
PASSES = SEQ // PASS_CAP
PAIRS = E // 2
EPS = 1e-6
FAR = -1.0e30
TAKEN = -3.0e38
NTOE = 2 * T - 1

C_Q, C_K, C_V, C_IQ, C_IK, C_IW, C_GLU, C_GATE = 0, 512, 1024, 1536, 2048, 2112, 2120, 3144
UNIT_COLS = 256
SLOT = 2048

KEY0 = [0, META, META + P]
KEYN = [META, P, P]
SEEN = [META + P, T]

FRONT = [("in", C_GLU + CH), ("in", C_GLU), ("in", C_GLU + CH + UNIT_COLS), ("in", C_GLU + UNIT_COLS),
         ("in", C_IQ), ("in", C_IQ + UNIT_COLS), ("ik", C_IK),
         ("in", C_Q), ("in", C_Q + UNIT_COLS), ("in", C_K), ("in", C_K + UNIT_COLS),
         ("in", C_V), ("in", C_V + UNIT_COLS)]
FRONT += [("in", C_GATE + UNIT_COLS * i) for i in range(8)]
FRONT += [("ao", 0), ("ao", 2), ("co", 0), ("co", 2)] + [("wo", 2 * i) for i in range(4)]
NF = len(FRONT)
UP_UNITS, DOWN_UNITS = KD, FF // P
PAIR_UNITS = 2 * UP_UNITS + DOWN_UNITS
BODY_UNITS = 2 * PAIR_UNITS
RING = 12
assert BODY_UNITS % RING == 0
TURNS = BODY_UNITS // RING

V_MIX, V_FFN, V_CB, V_LG, V_LB, V_BG = 0, 8, 16, 20, 24, 28
V_ROWS = 44


def slot_of(u):
    return u % RING


def loads_before(u):
    return u // RING


def layer(nc, x, meta, rel_bias, norm_mix, w_in, b_gate, w_attn_out, conv_w, conv_b, ln_g, ln_b,
          w_conv_out, w_out, norm_ffn, w_router, b_router, w_ug, b_ug, w_down, b_down, norm_final,
          bucket_rows, out):
    with ExitStack() as ctx:
        def sb(name, shape, dt=F32):
            return ctx.enter_context(nc.sbuf_tensor(name, shape, dt))

        def sem(name):
            return ctx.enter_context(nc.semaphore(name))

        ring = sb("ring", [P, RING, SLOT])
        x_nat = sb("x_nat", [P, QT, D])
        gate_region = sb("gate_region", [P, 16 * SEQ])
        x_scaled = gate_region[:, 0:3 * D].rearrange("p (i n) -> p i n", i=3)
        meta_nat = gate_region[:, 3 * D:4 * D]
        gates = gate_region[:, :].rearrange("p (i n) -> p i n", i=16)
        h_scaled = gate_region[:, 0:2 * D].rearrange("p (i n) -> p i n", i=2)
        picked = gate_region[:, 2 * D:4 * D].rearrange("p (b k n) -> p b k n", b=2, k=KD)
        hn_region = sb("hn_region", [P, KD * T])
        hn = hn_region[:, :].rearrange("p (k t) -> p k t", k=KD)
        merged = hn_region[:, 0:KD * SEQ].rearrange("p (k t) -> p k t", k=KD)
        glu_steps = hn_region[:, 0:4 * 512].rearrange("p (i n) -> p i n", i=4)
        iq_region = sb("iq_region", [P, 4 * SEQ + 2 * T])
        iq = iq_region[:, 0:4 * SEQ].rearrange("p (k t) -> p k t", k=4)
        ik_half = iq_region[:, 4 * SEQ:].rearrange("p (k t) -> p k t", k=2)
        attn = iq_region[:, 0:4 * SEQ].rearrange("p (k t) -> p k t", k=4)
        pick0 = iq_region[:, 0:512].rearrange("p (i n) -> p i n", i=QT)[:, :, 0:P]
        give0 = iq_region[:, 512:1024].rearrange("p (i n) -> p i n", i=QT)[:, :, 0:P]
        choose = iq_region[:, 1280:1536].rearrange("p (b n) -> p b n", b=2)
        qk_region = sb("qk_region", [P, 4 * SEQ + HEADS * T])
        q_t = qk_region[:, 0:4 * SEQ].rearrange("p (k t) -> p k t", k=4)
        k_half = qk_region[:, 4 * SEQ:].rearrange("p (h t) -> p h t", h=HEADS)
        bu_sb = qk_region[0:E, 0:2 * FF]
        bd_sb = qk_region[0:E, 2 * FF:2 * FF + D]
        prob_region = sb("prob_region", [P, HEADS * (SEEN[0] + SEEN[1])])
        probs = [prob_region[:, 0:HEADS * SEEN[0]].rearrange("p (h s) -> p h s", h=HEADS),
                 prob_region[:, HEADS * SEEN[0]:].rearrange("p (h s) -> p h s", h=HEADS)]
        h2 = prob_region[:, 0:2 * D].rearrange("p (i n) -> p i n", i=2)
        pt_region = sb("pt_region", [P, 3 * HEADS * P])
        probs_t = pt_region[:, :].rearrange("p (i h q) -> p i h q", i=3, h=HEADS)
        centred = pt_region[:, 0:CT * SEQ].rearrange("p (c t) -> p c t", c=CT)
        squares = pt_region[:, CT * SEQ:2 * CT * SEQ].rearrange("p (c t) -> p c t", c=CT)
        swish = pt_region[:, 2 * CT * SEQ:3 * CT * SEQ].rearrange("p (c t) -> p c t", c=CT)
        hf = pt_region[:, 0:KD * SEQ].rearrange("p (k t) -> p k t", k=KD)
        gfin = pt_region[:, 2 * D:3 * D]
        v_region = sb("v_region", [P, 3 * 512])
        v_sb = v_region[:, :].rearrange("p (i n) -> p i n", i=3)
        glu_region = sb("glu_region", [P, CT * (TAPS - 1 + T)])
        glu = glu_region[:, :].rearrange("p (c t) -> p c t", c=CT)
        conv_region = sb("conv_region", [P, CT * SEQ])
        conv = conv_region[:, :].rearrange("p (c t) -> p c t", c=CT)
        picked2 = pt_region[:, 0:D].rearrange("p (k n) -> p k n", k=KD)
        act_t = [conv_region[:, :].rearrange("p (e f n) -> p e f n", e=2, f=8),
                 prob_region[:, 2 * D:3 * D].rearrange("p (e f n) -> p e f n", e=2, f=8)]
        y_pair = glu_region[:, 0:D]
        y_more = v_region[:, 0:D].rearrange("p (e n) -> p e n", e=2)
        glu_sig = sb("glu_sig", [P, 2, T])
        score = sb("score", [P, QT, T])
        seen_bias = sb("seen_bias", [P, QT, T])
        relu = glu_sig
        pick = [pick0, seen_bias[:, :, 0:P]]
        give = give0
        give_t = iq_region[:, 1024:1280]
        give_more = [v_region[:, D:D + 2 * SEQ].rearrange("p (i n) -> p i n", i=QT), score[:, :, 0:SEQ]]
        give_more_t = pt_region[:, D:2 * D].rearrange("p (e c t) -> p e c t", e=2, c=2)
        ln_rows = glu_region[:, 0:2 * SEQ].rearrange("p (i t) -> p i t", i=2)
        ident = sb("ident", [P, P])
        ones = sb("ones", [P, P])
        mean_w = sb("mean_w", [P, P])
        before = sb("before", [P, P])
        number = sb("number", [P, P])
        eps_col = sb("eps_col", [P, 1])
        vec_rows = pt_region[0:V_ROWS, 1600:1600 + P]
        vec = sb("vec", [P, V_ROWS])
        cw_rows = pt_region[0:TAPS, 1088:1088 + CH]
        cw = sb("cw", [P, CT, TAPS])
        rel_sb = sb("rel_sb", [NB + 1, HEADS])
        bucket_sb = pt_region[0:NB + 1, 0:NTOE]
        toe_sb = pt_region[0:HEADS, 544:544 + NTOE]
        iw_t = pt_region[0:72, 1728:1728 + SEQ]
        iw = sb("iw", [P, QT, HEADS])
        stat = sb("stat", [P, 16])
        top8 = sb("top8", [P, QT, 8])
        smax = sb("smax", [P, QT, HEADS])
        sneg = sb("sneg", [P, QT, HEADS])
        ssum = sb("ssum", [P, QT, HEADS])
        srec = sb("srec", [P, QT, HEADS])
        wr_sb = sb("wr_sb", [P, KD, E])
        br_sb = sb("br_sb", [1, E])
        rlog = sb("rlog", [P, QT, E])
        ridx = sb("ridx", [P, QT, 8], U32)
        ridxf = sb("ridxf", [P, QT, 8])
        rexp = sb("rexp", [P, QT, 4])
        hot = sb("hot", [P, QT, 4, E])
        chosen = sb("chosen", [P, QT, E])
        combine_w = sb("combine_w", [P, QT, E])
        combine_t = sb("combine_t", [E, SEQ])
        place = sb("place", [P, QT, E * PASSES + 2])
        weight = sb("weight", [P, QT, E * PASSES + 2])
        counts = sb("counts", [P, 8])
        two_blocks = sb("two_blocks", [P, E * PASSES], I32)
        bodies = sb("bodies", [P, 1], I32)
        dram_toe = nc.dram_tensor("toeplitz_rows", (P, HEADS, NTOE), F32, kind="Internal").ap()

        ps = [ctx.enter_context(nc.psum_tensor(f"bank{i}", [P, 512], F32)) for i in range(8)]
        acc = ps[0:4]
        gate_ps, up_ps, t0_ps, t1_ps = ps[4:8]

        x_loaded = [sem(f"x{i}_loaded") for i in range(QT)]
        meta_loaded = sem("meta_loaded")
        vecs_loaded = sem("vecs_loaded")
        cw_loaded = sem("cw_loaded")
        rel_loaded = sem("rel_loaded")
        toe_stored = sem("toe_stored")
        toe_loaded = sem("toe_loaded")
        router_loaded = sem("router_loaded")
        ebias_loaded = sem("ebias_loaded")
        gfin_loaded = sem("gfin_loaded")
        slot_loaded = [sem(f"slot{i}_loaded") for i in range(RING)]
        unit_used = sem("unit_used")
        zeroed = sem("zeroed")
        pool_done = sem("pool_done")
        act_chain = sem("act_chain")
        dve_chain = sem("dve_chain")
        ss_ready = sem("ss_ready")
        root_ready = sem("root_ready")
        scaled_ready = sem("scaled_ready")
        vec_ps_ready = sem("vec_ps_ready")
        vec_ready = sem("vec_ready")
        xt_ready = sem("xt_ready")
        hn_act = sem("hn_act")
        hn_dve = sem("hn_dve")
        toe_ps_ready = sem("toe_ps_ready")
        toe_sb_ready = sem("toe_sb_ready")
        tile_ready = sem("tile_ready")
        tile_act = sem("tile_act")
        tile_dve = sem("tile_dve")
        iw_ps_ready = sem("iw_ps_ready")
        iw_ready = sem("iw_ready")
        idx_ready = sem("idx_ready")
        relu_ready = sem("relu_ready")
        relu_used = sem("relu_used")
        seen_ready = sem("seen_ready")
        bias_ready = sem("bias_ready")
        qk_ready = sem("qk_ready")
        logit_ready = sem("logit_ready")
        max_ready = sem("max_ready")
        exp_ready = sem("exp_ready")
        prob_ready = sem("prob_ready")
        attn_ps_ready = sem("attn_ps_ready")
        attn_copied = sem("attn_copied")
        glu_ready = sem("glu_ready")
        conv_ready = sem("conv_ready")
        mean_ready = sem("mean_ready")
        centred_ready = sem("centred_ready")
        squares_ready = sem("squares_ready")
        var_ready = sem("var_ready")
        ln_root = sem("ln_root")
        normed_ready = sem("normed_ready")
        swish_ready = sem("swish_ready")
        conv_out_ready = sem("conv_out_ready")
        merged_ready = sem("merged_ready")
        h2_ps_ready = sem("h2_ps_ready")
        h2_ready = sem("h2_ready")
        hs_ready = sem("hs_ready")
        hst_ready = sem("hst_ready")
        hf_act = sem("hf_act")
        hf_dve = sem("hf_dve")
        rlog_ready = sem("rlog_ready")
        rmax_ready = sem("rmax_ready")
        rexp_ready = sem("rexp_ready")
        choice_ready = sem("choice_ready")
        weight_ready = sem("weight_ready")
        weight_ps_ready = sem("weight_ps_ready")
        give_zeroed = sem("give_zeroed")
        place_ps_ready = sem("place_ps_ready")
        ct_ready = sem("ct_ready")
        plan_ready = sem("plan_ready")
        pick_ready = sem("pick_ready")
        pick2_ready = sem("pick2_ready")
        give2_ready = sem("give2_ready")
        y_more_act = sem("y_more_act")
        y_more_dve = sem("y_more_dve")
        gather_ready = [sem("gather_ready"), sem("gather_ready_2")]
        picked_ready = [sem("picked_ready"), sem("picked_ready_2")]
        gate_read = [sem("gate_read"), sem("gate_read_2")]
        clipped = [sem("clipped"), sem("clipped_2")]
        sig_ready = [sem("sig_ready"), sem("sig_ready_2")]
        act_ready = [sem("act_ready"), sem("act_ready_2")]
        actt_ps_ready = [sem("actt_ps_ready"), sem("actt_ps_ready_2")]
        actt_ready = [sem("actt_ready"), sem("actt_ready_2")]
        givet_ps_ready = [sem("givet_ps_ready"), sem("givet_ps_ready_2")]
        givet_ready = [sem("givet_ready"), sem("givet_ready_2")]
        y_act = sem("y_act")
        y_dve = sem("y_dve")
        combined = sem("combined")
        sum_ready = sem("sum_ready")
        fin_ss = sem("fin_ss")
        fin_root = sem("fin_root")
        fin_ready = sem("fin_ready")
        stored = sem("stored")

        tiles = []
        for i in range(2):
            tiles += [("g", 2 * i, 2 * i, 0), ("g", 2 * i + 1, 2 * i, P),
                      ("a", 2 * i, 2 * i + 1, 0), ("a", 2 * i + 1, 2 * i + 1, P)]
        tiles += [("iq", i, 4 + i // 2, P * (i % 2)) for i in range(4)]
        tiles += [("ik", 0, 6, 0), ("ik", 1, 6, 0)]
        tiles += [("q", i, 7 + i // 2, P * (i % 2)) for i in range(4)]
        tiles += [("k", i, 9 + i // 2, P * (i % 2)) for i in range(4)]
        tiles += [("v", i, 11, 0) for i in range(3)]
        tiles += [("gate", i, 13 + i // 2, P * (i % 2)) for i in range(16)]
        first = {}
        for n, (kind, *_) in enumerate(tiles):
            first.setdefault(kind, n)
        NT = len(tiles)
        U_AO, U_CO, U_WO = 21, 23, 25

        def read_by(n):
            if n >= NT:
                return tile_dve, 4 + n - NT + 1
            dve = sum(k == "a" for k, *_ in tiles[:n + 1])
            return (tile_dve, dve) if tiles[n][0] == "a" else (tile_act, n + 1 - dve)

        block = ctx.enter_context(nc.Block())

        @block.sync
        def _(sp):
            for i in range(QT):
                sp.dma_start(x_nat[:, i, :], x[i * P:(i + 1) * P, :]).then_inc(x_loaded[i], 16)
            with nc.allow_non_contiguous_dma(reason="rows of the packed vectors and of the weights"):
                for u, (kind, c) in enumerate(FRONT):
                    if u >= RING:
                        sp.wait_ge(unit_used, u - RING + 1)
                    dst = ring[:, slot_of(u), :]
                    if kind == "in" or kind == "ik":
                        n = UNIT_COLS if kind == "in" else C_GLU - C_IK
                        dst = dst[:, 0:KD * n].rearrange("p (k n) -> p k n", k=KD)
                        src = w_in.rearrange("(k p) n -> p k n", p=P)[:, :, c:c + n]
                    else:
                        w = {"ao": w_attn_out, "co": w_conv_out, "wo": w_out}[kind]
                        dst = dst.rearrange("p (k n) -> p k n", k=2)
                        src = w.rearrange("(k p) n -> p k n", p=P)[:, c:c + 2, :]
                    sp.dma_start(dst, src).then_inc(slot_loaded[slot_of(u)], 16)

                def experts(first_body, i):
                    for j in range(BODY_UNITS):
                        pair, r = divmod(j, PAIR_UNITS)
                        u = NF + j
                        sp.wait_ge(unit_used, (first_body + i) * BODY_UNITS + (u - RING + 1))
                        dst = ring[:, slot_of(u), :]
                        if r < 2 * UP_UNITS:
                            e, k = divmod(r, UP_UNITS)
                            src = w_ug[bass.ds(4 * i + (2 * pair + e), 1), k * P:(k + 1) * P, :].rearrange(
                                "e p n -> p (e n)")
                        else:
                            f = r - 2 * UP_UNITS
                            dst = dst.rearrange("p (e n) -> p e n", e=2)
                            src = w_down[bass.ds(4 * i + 2 * pair, 2), f * P:(f + 1) * P, :].rearrange(
                                "e p n -> p e n")
                        sp.dma_start(dst, src).then_inc(slot_loaded[slot_of(u)], 16)

                with sp.Fori(0, PAIRS // 2) as i:
                    experts(0, i)
                sp.wait_ge(plan_ready, 1)
                n_bodies = sp.value_load(bodies[0:1, 0:1], min_val=PAIRS // 2,
                                         max_val=PASSES * PAIRS // 2)
                with sp.If(n_bodies > PAIRS // 2):
                    with sp.Fori(PAIRS // 2, n_bodies, PAIRS // 2) as done:
                        with sp.Fori(0, PAIRS // 2) as i:
                            experts(done, i)
            for i in range(QT):
                sp.wait_ge(fin_ready, i + 1)
                sp.dma_start(out[i * P:(i + 1) * P, :], x_nat[:, i, :]).then_inc(stored, 16)
            sp.wait_ge(stored, 16 * QT)

        @block.gpsimd
        def _(pool):
            nc.gpsimd.memset(ident[:], 0.0).then_inc(zeroed, 1)
            nc.gpsimd.memset(ones[:], 1.0).then_inc(zeroed, 1)
            nc.gpsimd.memset(before[:], 1.0).then_inc(zeroed, 1)
            nc.gpsimd.memset(seen_bias[:], 0.0).then_inc(zeroed, 1)
            nc.gpsimd.memset(rel_sb[:], 1.0).then_inc(zeroed, 1)
            nc.gpsimd.memset(eps_col[:], EPS).then_inc(zeroed, 1)
            pool.wait_ge(zeroed, 6)
            nc.gpsimd.affine_select(out=ident[:], in_=ident[:], compare_op=ALU.not_equal, fill=1.0,
                                    base=0, pattern=[[-1, P]], channel_multiplier=1).then_inc(pool_done, 1)
            nc.gpsimd.affine_select(out=before[:], in_=before[:], compare_op=ALU.is_gt, fill=0.0,
                                    base=0, pattern=[[1, P]], channel_multiplier=-1).then_inc(pool_done, 1)
            for i in range(QT):
                nc.gpsimd.affine_select(out=seen_bias[:, i, :], in_=seen_bias[:, i, :],
                                        compare_op=ALU.is_ge, fill=FAR, base=META + i * P,
                                        pattern=[[-1, T]], channel_multiplier=1).then_inc(pool_done, 1)
            nc.gpsimd.memset(mean_w[:], 1.0 / CH).then_inc(pool_done, 1)
            nc.gpsimd.iota(number[:], pattern=[[1, P]], base=0, channel_multiplier=0,
                           allow_small_or_imprecise_dtypes=True).then_inc(pool_done, 1)
            nc.gpsimd.memset(glu[:, :, 0:TAPS - 1], 0.0).then_inc(pool_done, 1)
            pool.wait_ge(pool_done, 7)
            nc.gpsimd.memset(ik_half[64:128, 0, :], 0.0).then_inc(pool_done, 1)
            nc.gpsimd.memset(k_half[64:128, 0:HEADS:2, :], 0.0).then_inc(pool_done, 1)
            pool.wait_ge(pool_done, 9)
            nc.gpsimd.memset(ik_half[0:64, 1, :], 0.0).then_inc(pool_done, 1)
            nc.gpsimd.memset(k_half[0:64, 1:HEADS:2, :], 0.0).then_inc(pool_done, 1)
            nc.gpsimd.memset(place[:], -1.0).then_inc(pool_done, 1)
            nc.gpsimd.memset(weight[:], 0.0).then_inc(pool_done, 1)
            for i in range(QT):
                pool.wait_ge(toe_loaded, 32)
                pool.wait_ge(seen_ready, i + 1)
                w = SEEN[i]
                left_out = seen_bias[:, i, 0:w].unsqueeze(1).broadcast_to([P, HEADS, w])
                nc.gpsimd.tensor_tensor(probs[i], probs[i], left_out, ALU.add).then_inc(bias_ready, 1)

        CONSTS = 13

        @block.scalar
        def _(act):
            chain = [0]

            def link(ins):
                chain[0] += 1
                ins.then_inc(act_chain, 1)
                act.wait_ge(act_chain, chain[0])

            with nc.allow_non_contiguous_dma(reason="small vectors"):
                act.dma_start(meta_nat[0:META, :], meta).then_inc(meta_loaded, 16)
                for r, n, v in ((V_MIX, 8, norm_mix), (V_FFN, 8, norm_ffn), (V_CB, 4, conv_b),
                                (V_LG, 4, ln_g), (V_LB, 4, ln_b), (V_BG, 16, b_gate)):
                    act.dma_start(vec_rows[r:r + n, :], v.rearrange("(k p) -> k p", p=P)).then_inc(vecs_loaded, 16)
                act.dma_start(cw_rows, conv_w).then_inc(cw_loaded, 16)
                act.wait_ge(zeroed, 6)
                act.dma_start(rel_sb[0:NB, :], rel_bias).then_inc(rel_loaded, 16)
                act.dma_start(bucket_sb, bucket_rows).then_inc(rel_loaded, 16)
                act.dma_start(wr_sb[:], w_router.rearrange("(k p) n -> p k n", p=P)).then_inc(router_loaded, 16)
                act.dma_start(br_sb[:], b_router.rearrange("(a n) -> a n", a=1)).then_inc(router_loaded, 16)

            for i in (2, 0, 1):
                act.wait_ge(x_loaded[i] if i < QT else meta_loaded, 16)
                rows = x_nat[:, i, :] if i < QT else meta_nat[0:META, :]
                n = P if i < QT else META
                nc.scalar.activation(x_scaled[0:n, i, :], rows, ACT.Square,
                                     accum_out=stat[0:n, i:i + 1]).then_inc(ss_ready, 1)
            act.wait_ge(ss_ready, 3)
            act.wait_ge(zeroed, 6)
            nc.scalar.activation(stat[:, 3:5], stat[:, 0:2], ACT.Sqrt, scale=1.0 / D,
                                 bias=eps_col[:]).then_inc(root_ready, 1)
            nc.scalar.activation(stat[0:META, 5:6], stat[0:META, 2:3], ACT.Sqrt, scale=1.0 / D,
                                 bias=eps_col[0:META]).then_inc(root_ready, 1)
            act.wait_ge(vec_ready, 2)
            for k in range(4):
                act.wait_ge(xt_ready, k + 1)
                nc.scalar.activation(hn[:, k, :], ps[k][:, 0:T], ACT.Copy,
                                     scale=vec[:, V_MIX + k:V_MIX + k + 1]).then_inc(hn_act, 1)

            act.wait_ge(toe_ps_ready, 1)
            link(nc.scalar.copy(toe_sb[:, 0:512], ps[4][0:HEADS, :]))
            link(nc.scalar.copy(toe_sb[:, 512:NTOE], ps[5][0:HEADS, 0:NTOE - 512]))
            with nc.allow_non_contiguous_dma(reason="Toeplitz rows"):
                act.dma_start(dram_toe.rearrange("p h j -> h p j"),
                              toe_sb.unsqueeze(1).broadcast_to([HEADS, P, NTOE])).then_inc(toe_stored, 16)
                act.wait_ge(toe_stored, 16)
                for i in range(QT):
                    w = SEEN[i]
                    rows = bass.AP(dram_toe.tensor, T - 1 - META - i * P,
                                   [[HEADS * NTOE - 1, P], [NTOE, HEADS], [1, w]])
                    act.dma_start(probs[i], rows).then_inc(toe_loaded, 16)

            def read_tile(n):
                kind, i, _, _ = tiles[n]
                bank = ps[n % 4]
                act.wait_ge(tile_ready, n + 1)
                if kind == "g":
                    if i >= 2:
                        act.wait_ge(tile_dve, i - 1)
                    ins = nc.scalar.activation(glu_sig[:, i % 2, :], bank[:, 0:T], ACT.Sigmoid)
                elif kind == "iq":
                    ins = nc.scalar.copy(iq[:, i, :], bank[:, 0:SEQ])
                elif kind == "ik" and i == 0:
                    act.wait_ge(pool_done, CONSTS)
                    nc.scalar.copy(ik_half[0:64, 0, :], bank[0:64, 0:T]).then_inc(idx_ready, 1)
                    ins = nc.scalar.copy(iw_t[64:72, :], bank[64:72, META:T])
                elif kind == "ik":
                    ins = nc.scalar.copy(ik_half[64:128, 1, :], bank[64:128, 0:T])
                elif kind == "q":
                    ins = nc.scalar.copy(q_t[:, i, :], bank[:, 0:SEQ])
                elif kind == "k":
                    nc.scalar.copy(k_half[0:64, 2 * i, :], bank[0:64, 0:T]).then_inc(idx_ready, 1)
                    ins = nc.scalar.copy(k_half[64:128, 2 * i + 1, :], bank[64:128, 0:T])
                elif kind == "v":
                    ins = nc.scalar.copy(v_sb[0:KEYN[i], i, :], bank[0:KEYN[i], :])
                else:
                    if i == 0:
                        act.wait_ge(hn_dve, 4)
                    ins = nc.scalar.activation(gates[:, i, :], bank[:, 0:SEQ], ACT.Sigmoid,
                                               bias=vec[:, V_BG + i:V_BG + i + 1])
                ins.then_inc(tile_act, 1)

            for n in range(first["ik"] + 2):
                if tiles[n][0] != "a":
                    read_tile(n)
            act.wait_ge(iw_ps_ready, 1)
            nc.scalar.mul(iw[:], ps[4][:, 0:QT * HEADS].rearrange("p (i h) -> p i h", i=QT),
                          IDX_SCALE).then_inc(iw_ready, 1)
            for m in range(QT * HEADS):
                w = SEEN[m // HEADS]
                act.wait_ge(qk_ready, m + 1)
                if m >= 2:
                    act.wait_ge(relu_used, m - 1)
                nc.scalar.activation(relu[:, m % 2, 0:w], ps[4 + m % 4][:, 0:w], ACT.Relu).then_inc(relu_ready, 1)
            for n in range(first["q"], first["gate"]):
                read_tile(n)

            def softmax_exp(i):
                act.wait_ge(max_ready, i + 1)
                for h in range(HEADS):
                    nc.scalar.activation(probs[i][:, h, :], probs[i][:, h, :], ACT.Exp,
                                         bias=sneg[:, i, h:h + 1],
                                         accum_out=ssum[:, i, h:h + 1]).then_inc(exp_ready, 1)

            def copy_probs(i):
                r0 = 0 if i == 0 else 5
                groups = [(s, g) for s in range(2 + i) for g in range(2)]
                if i == 0:
                    act.wait_ge(conv_out_ready, 1)
                for r, (s, g) in enumerate(groups):
                    act.wait_ge(attn_ps_ready, r0 + r + 1)
                    nc.scalar.copy(probs_t[0:KEYN[s], s, 4 * g:4 * g + 4, :],
                                   ps[4 + (r0 + r) % 4][0:KEYN[s], :].rearrange("p (h q) -> p h q", h=4)
                                   ).then_inc(attn_copied, 1)
                r = r0 + len(groups)
                act.wait_ge(attn_ps_ready, r + 1)
                nc.scalar.copy(attn[:, :, i * P:(i + 1) * P],
                               ps[4 + r % 4][:, :].rearrange("p (c q) -> p c q", c=HP)).then_inc(attn_copied, 1)

            def read_gates(i0, i1):
                for n in range(first["gate"] + i0, first["gate"] + i1):
                    read_tile(n)

            read_gates(0, 4)
            act.wait_ge(centred_ready, 1)
            nc.scalar.activation(squares, centred, ACT.Square).then_inc(squares_ready, 1)
            read_gates(4, 6)
            act.wait_ge(var_ready, 1)
            nc.scalar.activation(ln_rows[:, 0, :], ps[5][:, 0:SEQ], ACT.Sqrt,
                                 bias=eps_col[:]).then_inc(ln_root, 1)
            read_gates(6, 10)
            softmax_exp(0)
            act.wait_ge(normed_ready, 1)
            for c in range(CT):
                nc.scalar.activation(swish[:, c, :], centred[:, c, :], ACT.Sigmoid,
                                     scale=vec[:, V_LG + c:V_LG + c + 1],
                                     bias=vec[:, V_LB + c:V_LB + c + 1]).then_inc(swish_ready, 1)
            read_gates(10, 14)
            softmax_exp(1)
            read_gates(14, 16)
            copy_probs(0)
            copy_probs(1)

            act.wait_ge(logit_ready, QT * HEADS)
            act.dma_start(bu_sb, b_ug).then_inc(ebias_loaded, 16)
            act.dma_start(bd_sb, b_down).then_inc(ebias_loaded, 16)

            for i in range(QT):
                act.wait_ge(h2_ready, 2 * i + 2)
                if i == 0:
                    act.wait_ge(merged_ready, 2 * KD)
                nc.scalar.activation(h_scaled[:, i, :], h2[:, i, :], ACT.Square,
                                     accum_out=stat[:, 6 + i:7 + i]).then_inc(ss_ready, 1)
                act.wait_ge(ss_ready, 4 + i)
                nc.scalar.activation(stat[:, 8 + i:9 + i], stat[:, 6 + i:7 + i], ACT.Sqrt, scale=1.0 / D,
                                     bias=eps_col[:]).then_inc(root_ready, 1)
            for k in range(0, KD, 2):
                act.wait_ge(hst_ready, k // 2 + 1)
                nc.scalar.activation(hf[:, k, :], ps[k // 2][:, 0:SEQ], ACT.Copy,
                                     scale=vec[:, V_FFN + k:V_FFN + k + 1]).then_inc(hf_act, 1)
            act.wait_ge(rmax_ready, 1)
            for i in range(QT):
                nc.scalar.activation(rexp[:, i, :], top8[:, i, 0:4], ACT.Exp, bias=stat[:, 10 + i:11 + i],
                                     accum_out=stat[:, 12 + i:13 + i]).then_inc(rexp_ready, 1)
            act.wait_ge(rlog_ready, 1)
            with nc.allow_non_contiguous_dma(reason="one row for every partition"):
                act.dma_start(gfin, norm_final.rearrange("(a n) -> a n", a=1).broadcast_to([P, D])
                              ).then_inc(gfin_loaded, 16)

            act.wait_ge(plan_ready, 1)
            n_bodies = act.value_load(bodies[0:1, 0:1], min_val=PAIRS // 2,
                                      max_val=PASSES * PAIRS // 2)
            for signal in (sig_ready[1], actt_ready[1], givet_ready[1], y_act, y_more_act):
                act.sem_inc(signal, 1)

            def expert(g, b, e, blocks):
                n = 4 * g + (2 * b + e)
                for q in range(blocks):
                    act.wait_ge(gate_read[q], n + (1 + q))
                    act.wait_ge(act_ready[0], n + (1 + q))
                    act.wait_ge(act_ready[1], n + 1)
                    nc.scalar.activation(glu_steps[:, 1, :], glu_steps[:, 0, :], ACT.Sigmoid,
                                         scale=1.702).then_inc(sig_ready[q], 1)
                    act.wait_ge(actt_ps_ready[q], n + (1 + q))
                    nc.scalar.copy(act_t[q][:, e].rearrange("p (h j) n -> p j h n", h=2),
                                   (gate_ps, t0_ps)[q][:, :].rearrange("p (j h n) -> p j h n", j=4, h=2)
                                   ).then_inc(actt_ready[q], 1)
                    if (q, e) == (0, 1):
                        act.wait_ge(givet_ps_ready[0], 2 * g + (b + 1))
                        nc.scalar.copy(give_t, up_ps[:, 0:SEQ]).then_inc(givet_ready[0], 1)
                if blocks == 2:
                    act.wait_ge(givet_ps_ready[1], n + 2)
                    nc.scalar.copy(give_more_t[:, e], t1_ps[:, :].rearrange("p (c t) -> p c t", c=2)
                                   ).then_inc(givet_ready[1], 1)
                else:
                    for signal in (sig_ready[1], actt_ready[1], givet_ready[1]):
                        act.wait_ge(signal, n + 1)
                        act.sem_inc(signal, 1)

            with act.Fori(0, n_bodies) as g:
                for b in range(2):
                    two = [act.value_load(two_blocks[0:1, bass.ds(4 * g + (2 * b + e), 1)], min_val=0, max_val=1)
                           for e in range(2)]
                    for e in range(2):
                        with act.If(two[e] > 0):
                            expert(g, b, e, 2)
                        with act.Else():
                            expert(g, b, e, 1)
                    act.wait_ge(unit_used, g * BODY_UNITS + (NF + (b + 1) * PAIR_UNITS))
                    nc.scalar.copy(y_pair[:, 0:512], t0_ps[:, :]).then_inc(y_act, 1)
                    with act.If(two[0] > 0):
                        nc.scalar.copy(y_more[:, 0, :], gate_ps[:, :]).then_inc(y_more_act, 1)
                    with act.Else():
                        act.wait_ge(y_more_act, 2 * g + (b + 1))
                        act.sem_inc(y_more_act, 1)

            for i in range(QT):
                act.wait_ge(sum_ready, 2 * i + 2)
                nc.scalar.activation(h_scaled[:, i, :], h2[:, i, :], ACT.Square,
                                     accum_out=stat[:, 6 + i:7 + i]).then_inc(fin_ss, 1)
            act.wait_ge(fin_ss, 2)
            nc.scalar.activation(stat[:, 8:10], stat[:, 6:8], ACT.Sqrt, scale=1.0 / D,
                                 bias=eps_col[:]).then_inc(fin_root, 1)

        @block.vector
        def _(dve):
            chain = [0]

            def link(ins, behind=0):
                chain[0] += 1
                ins.then_inc(dve_chain, 1)
                if chain[0] > behind:
                    dve.wait_ge(dve_chain, chain[0] - behind)

            dve.wait_ge(root_ready, 2)
            for signal in (meta_loaded, *x_loaded):
                dve.wait_ge(signal, 16)
            link(nc.vector.reciprocal(stat[:, 6:8], stat[:, 3:5]))
            link(nc.vector.reciprocal(stat[0:META, 8:9], stat[0:META, 5:6]))
            for i in range(3):
                n = P if i < QT else META
                rows = x_nat[:, i, :] if i < QT else meta_nat[0:META, :]
                nc.vector.tensor_scalar(x_scaled[0:n, i, :], rows, stat[0:n, 6 + i:7 + i], None,
                                        ALU.mult).then_inc(scaled_ready, 1)
            dve.wait_ge(vec_ps_ready, 1)
            nc.vector.tensor_copy(vec[:], ps[7][:, 0:V_ROWS]).then_inc(vec_ready, 1)
            nc.vector.tensor_copy(cw[:], ps[6][:, 0:CT * TAPS].rearrange("p (c j) -> p c j", c=CT)
                                  ).then_inc(vec_ready, 1)
            dve.wait_ge(vec_ready, 2)
            for k in range(4, KD):
                dve.wait_ge(xt_ready, k + 1)
                nc.vector.tensor_scalar(hn[:, k, :], ps[k][:, 0:T], vec[:, V_MIX + k:V_MIX + k + 1], None,
                                        ALU.mult).then_inc(hn_dve, 1)
            dve.wait_ge(pool_done, CONSTS)
            for n, (kind, i, _, _) in enumerate(tiles):
                if kind == "a":
                    dve.wait_ge(tile_ready, n + 1)
                    dve.wait_ge(tile_act, i + 1)
                    nc.vector.tensor_tensor(glu[:, i, TAPS - 1:], ps[n % 4][:, 0:T], glu_sig[:, i % 2, :],
                                            ALU.mult).then_inc(tile_dve, 1)

            dve.wait_ge(iw_ready, 1)
            for m in range(QT * HEADS):
                i, h = divmod(m, HEADS)
                w = SEEN[i]
                dve.wait_ge(relu_ready, m + 1)
                if h:
                    dve.wait_ge(relu_used, m)
                nc.vector.scalar_tensor_tensor(
                    out=score[:, i, 0:w], in0=relu[:, m % 2, 0:w], scalar=iw[:, i, h:h + 1],
                    in1=(score if h else seen_bias)[:, i, 0:w], op0=ALU.mult,
                    op1=ALU.add).then_inc(relu_used, 1)
            dve.wait_ge(relu_used, QT * HEADS)
            for r in range(TOPK // 8):
                for i in range(QT):
                    link(nc.vector.max(top8[:, i, :], score[:, i, 0:SEEN[i]]), behind=1)
                for i in range(QT):
                    link(nc.vector.match_replace(score[:, i, 0:SEEN[i]], top8[:, i, :],
                                                 score[:, i, 0:SEEN[i]], TAKEN), behind=1)
            link(nc.vector.tensor_scalar(ssum[:, 0, :], iw[:, 0, :], 0.0, None, ALU.mult))
            for i in range(QT):
                nc.vector.tensor_scalar(seen_bias[:, i, 0:SEEN[i]], score[:, i, 0:SEEN[i]],
                                        0.5 * TAKEN, FAR, ALU.is_gt, ALU.mult).then_inc(seen_ready, 1)

            def convolve():
                for j in range(TAPS):
                    for c in range(CT):
                        src = glu[:, c, META + j:META + j + SEQ]
                        if j == 0:
                            ins = nc.vector.tensor_scalar(conv[:, c, :], src, cw[:, c, 0:1],
                                                          vec[:, V_CB + c:V_CB + c + 1], ALU.mult, ALU.add)
                        else:
                            ins = nc.vector.scalar_tensor_tensor(
                                out=conv[:, c, :], in0=src, scalar=cw[:, c, j:j + 1],
                                in1=conv[:, c, :], op0=ALU.mult, op1=ALU.add)
                        link(ins, behind=CT - 1)

            def softmax_logits(i):
                w = SEEN[i]
                dve.wait_ge(bias_ready, i + 1)
                for h in range(HEADS):
                    m = QT * HEADS + i * HEADS + h
                    dve.wait_ge(qk_ready, m + 1)
                    nc.vector.scalar_tensor_tensor(
                        out=probs[i][:, h, :], in0=ps[4 + m % 4][:, 0:w], scalar=DH ** -0.5,
                        in1=probs[i][:, h, :], op0=ALU.mult, op1=ALU.add).then_inc(logit_ready, 1)
                dve.wait_ge(logit_ready, HEADS * (i + 1))
                link(nc.vector.tensor_reduce(smax[:, i, :], probs[i], AX_X, ALU.max))
                nc.vector.tensor_scalar(sneg[:, i, :], smax[:, i, :], -1.0, None, ALU.mult).then_inc(max_ready, 1)

            def softmax_scale(i):
                dve.wait_ge(exp_ready, HEADS * (i + 1))
                link(nc.vector.reciprocal(srec[:, i, :], ssum[:, i, :]))
                nc.vector.tensor_tensor(probs[i], probs[i],
                                        srec[:, i, :].unsqueeze(2).broadcast_to([P, HEADS, SEEN[i]]),
                                        ALU.mult).then_inc(prob_ready, 1)

            convolve()
            nc.vector.memset(stat[:, 15:16], 0.0).then_inc(conv_ready, 1)
            dve.wait_ge(mean_ready, 1)
            dve.wait_ge(conv_ready, 1)
            dve.wait_ge(bias_ready, 1)
            nc.vector.tensor_tensor(centred, conv, ps[4][:, 0:SEQ].unsqueeze(1).broadcast_to([P, CT, SEQ]),
                                    ALU.subtract).then_inc(centred_ready, 1)
            softmax_logits(0)
            dve.wait_ge(ln_root, 1)
            link(nc.vector.reciprocal(ln_rows[:, 1, :], ln_rows[:, 0, :]))
            dve.wait_ge(squares_ready, 1)
            nc.vector.tensor_tensor(centred, centred, ln_rows[:, 1, :].unsqueeze(1).broadcast_to([P, CT, SEQ]),
                                    ALU.mult).then_inc(normed_ready, 1)
            softmax_logits(1)
            dve.wait_ge(normed_ready, 1)
            for c in range(CT):
                link(nc.vector.tensor_scalar(conv[:, c, :], centred[:, c, :], vec[:, V_LG + c:V_LG + c + 1],
                                             vec[:, V_LB + c:V_LB + c + 1], ALU.mult, ALU.add), behind=CT)
            softmax_scale(0)
            dve.wait_ge(swish_ready, CT)
            nc.vector.tensor_tensor(conv, conv, swish, ALU.mult).then_inc(conv_out_ready, 1)
            softmax_scale(1)

            for half in range(2):
                for k in range(KD):
                    n = NT + half * KD + k
                    dve.wait_ge(tile_ready, n + 1)
                    if half == 0:
                        dve.wait_ge(tile_act, NT - 4)
                        nc.vector.tensor_tensor(merged[:, k, :], ps[n % 4][:, 0:SEQ], gates[:, k, :],
                                                ALU.mult).then_inc(tile_dve, 1)
                    else:
                        nc.vector.tensor_tensor(gates[:, KD + k, :], ps[n % 4][:, 0:SEQ],
                                                gates[:, KD + k, :], ALU.mult).then_inc(tile_dve, 1)
                        dve.wait_ge(tile_dve, 4 + KD + k + 1)
                        nc.vector.tensor_tensor(merged[:, k, :], merged[:, k, :], gates[:, KD + k, :],
                                                ALU.add).then_inc(merged_ready, 2)
            dve.wait_ge(attn_copied, 12)
            for e in range(2):
                nc.vector.memset(give_more[e], 0.0).then_inc(give_zeroed, 1)
            for i in range(QT):
                if i == 0:
                    dve.wait_ge(h2_ps_ready, 1)
                else:
                    dve.wait_ge(unit_used, NF)
                for c in range(2):
                    nc.vector.tensor_tensor(h2[:, i, c * 512:(c + 1) * 512], ps[4 + 2 * i + c][:, :],
                                            x_nat[:, i, c * 512:(c + 1) * 512], ALU.add).then_inc(h2_ready, 1)
                dve.wait_ge(root_ready, 3 + i)
                link(nc.vector.reciprocal(stat[:, 6 + i:7 + i], stat[:, 8 + i:9 + i]))
                dve.wait_ge(h2_ready, 2 * i + 2)
                nc.vector.tensor_scalar(h_scaled[:, i, :], h2[:, i, :], stat[:, 6 + i:7 + i], None,
                                        ALU.mult).then_inc(hs_ready, 1)
            for k in range(1, KD, 2):
                dve.wait_ge(hst_ready, k // 2 + 1)
                dve.wait_ge(hf_act, k // 2 + 1)
                nc.vector.tensor_scalar(hf[:, k, :], ps[k // 2][:, SEQ:2 * SEQ],
                                        vec[:, V_FFN + k:V_FFN + k + 1], None, ALU.mult).then_inc(hf_dve, 1)

            dve.wait_ge(rlog_ready, 1)
            link(nc.vector.tensor_copy(rlog[:], ps[4][:, 0:QT * E].rearrange("p (i e) -> p i e", i=QT)))
            for i in range(QT):
                link(nc.vector.max(top8[:, i, :], rlog[:, i, :]), behind=1 - i)
            nc.vector.tensor_scalar(stat[:, 10:12], top8[:, :, 0], -1.0, None, ALU.mult).then_inc(rmax_ready, 1)
            for i in range(QT):
                link(nc.vector.max_index(ridx[:, i, :], top8[:, i, :], rlog[:, i, :]), behind=1 - i)
            link(nc.vector.memset(counts[:, 7:8], 0.0))
            link(nc.vector.tensor_copy(ridxf[:], ridx[:]))
            link(nc.vector.tensor_tensor(
                hot[:], number[:, 0:E].unsqueeze(1).unsqueeze(1).broadcast_to([P, QT, 4, E]),
                ridxf[:, :, 0:4].unsqueeze(3).broadcast_to([P, QT, 4, E]), ALU.is_equal))
            nc.vector.tensor_reduce(chosen[:], hot[:].rearrange("p i j e -> p i e j"), AX_X,
                                    ALU.add).then_inc(choice_ready, 1)
            dve.wait_ge(rexp_ready, QT)
            link(nc.vector.reciprocal(stat[:, 14:16], stat[:, 12:14]))
            link(nc.vector.tensor_tensor(rexp[:], rexp[:], stat[:, 14:16].unsqueeze(2).broadcast_to([P, QT, 4]),
                                         ALU.mult))
            dve.wait_ge(choice_ready, 1)
            link(nc.vector.tensor_tensor(hot[:], hot[:], rexp[:].unsqueeze(3).broadcast_to([P, QT, 4, E]),
                                         ALU.mult))
            nc.vector.tensor_reduce(combine_w[:], hot[:].rearrange("p i j e -> p i e j"), AX_X,
                                    ALU.add).then_inc(weight_ready, 1)

            dve.wait_ge(place_ps_ready, 1)
            where = ps[5][:, 0:QT * E].rearrange("p (i e) -> p i e", i=QT)
            link(nc.vector.scalar_tensor_tensor(out=place[:, :, 0:E], in0=where, scalar=1.0, in1=chosen[:],
                                                op0=ALU.add, op1=ALU.mult))
            link(nc.vector.tensor_scalar(place[:, :, 0:E], place[:, :, 0:E], -1.0, None, ALU.add))
            def one_hot(pair_expert, q, dst, weighted, signal):
                for i in range(QT):
                    for e in range(2):
                        nc.vector.tensor_scalar(
                            dst[:, i, e * CAP:(e + 1) * CAP], number[:, q * CAP:(q + 1) * CAP],
                            place[:, i, bass.ds(pair_expert + e, 1)],
                            weight[:, i, bass.ds(pair_expert + e, 1)] if weighted else None,
                            ALU.is_equal, *([ALU.mult] if weighted else [])).then_inc(signal, 1)

            def plan_pick(pair_expert, bank, expert_mod):
                one_hot(pair_expert, 0, pick[0], False, pick_ready)
                for e in range(2):
                    nc.vector.tensor_copy(choose[0:E, bank, e * CAP:(e + 1) * CAP],
                                          ident[0:E, bass.ds(expert_mod + e, 1)].broadcast_to([E, CAP])
                                          ).then_inc(pick_ready, 1)

            def copy_picked(dst, q, value):
                dve.wait_ge(gather_ready[q], value)
                for j, src in enumerate((t0_ps, t1_ps)):
                    g_ffn = vec[:, V_FFN + 4 * j:V_FFN + 4 * j + 4].unsqueeze(2).broadcast_to([P, 4, P])
                    nc.vector.tensor_tensor(dst[:, 4 * j:4 * j + 4, :],
                                            src[:, :].rearrange("p (k n) -> p k n", k=4), g_ffn,
                                            ALU.mult).then_inc(picked_ready[q], 1)

            plan_pick(0, 0, 0)
            per_expert = ps[5][:, QT * E:(QT + 1) * E]
            link(nc.vector.tensor_reduce(counts[:, 0:1], per_expert, AX_X, ALU.max))
            link(nc.vector.tensor_scalar(counts[:, 4:5], counts[:, 0:1], float(PASS_CAP),
                                         float(PAIRS // 2), ALU.is_gt, ALU.mult))
            for q in range(PASSES):
                link(nc.vector.tensor_scalar(two_blocks[:, q * E:(q + 1) * E], per_expert,
                                             float(q * PASS_CAP + CAP), None, ALU.is_gt), behind=1)
            link(nc.vector.tensor_scalar(bodies[:], counts[:, 4:5], float(PAIRS // 2), None, ALU.add))
            nc.vector.memset(counts[:, 6:7], 0.0).then_inc(plan_ready, 1)
            dve.wait_ge(weight_ps_ready, 1)
            nc.vector.tensor_copy(combine_t[:], ps[0][0:E, 0:SEQ]).then_inc(ct_ready, 1)
            copy_picked(picked[:, 0], 0, 1)
            for q in range(1, PASSES):
                link(nc.vector.tensor_scalar(place[:, :, q * E:(q + 1) * E], place[:, :, 0:E],
                                             -float(q * PASS_CAP), None, ALU.add), behind=1)
            for q in range(PASSES):
                link(nc.vector.tensor_copy(weight[:, :, q * E:(q + 1) * E], combine_w[:]), behind=1)
            link(nc.vector.memset(counts[:, 7:8], 0.0))
            dve.wait_ge(plan_ready, 1)
            for signal, n in ((pick2_ready, 1), (give2_ready, 1), (picked_ready[1], 1), (gate_read[1], 1),
                              (clipped[0], 2), (clipped[1], 2), (act_ready[0], 1), (act_ready[1], 1),
                              (y_dve, 1), (y_more_dve, 1)):
                dve.sem_inc(signal, n)
            n_bodies = dve.value_load(bodies[0:1, 0:1], min_val=PAIRS // 2,
                                      max_val=PASSES * PAIRS // 2)

            dve.wait_ge(give_zeroed, 2)

            def count_on(signal, before, n):
                dve.wait_ge(signal, before)
                dve.sem_inc(signal, n)

            def expert(g, b, e, blocks):
                if blocks == 2:
                    for i in range(QT):
                        for c in range(2):
                            at = c * P + c * CAP
                            expert_at = bass.ds(4 * g + (2 * b + e), 1)
                            nc.vector.tensor_scalar(
                                give_more[e][:, i, at:at + CAP], number[:, CAP:2 * CAP],
                                place[:, i, expert_at], weight[:, i, expert_at],
                                ALU.is_equal, ALU.mult).then_inc(give2_ready, 1)
                n = 4 * g + (2 * b + e)
                for q in range(blocks):
                    dve.wait_ge(unit_used, g * BODY_UNITS + (NF + b * PAIR_UNITS + (e + 1) * UP_UNITS))
                    gate, lin = ((gate_ps, up_ps), (t0_ps, t1_ps))[q]
                    nc.vector.tensor_scalar(glu_steps[:, 0, :], gate[:, :], 7.0, None,
                                            ALU.min).then_inc(gate_read[q], 1)
                    dve.wait_ge(act_ready[0], n + (1 + q))
                    dve.wait_ge(act_ready[1], n + 1)
                    nc.vector.tensor_scalar(glu_steps[:, 2, :], lin[:, :], 7.0, -7.0, ALU.min,
                                            ALU.max).then_inc(clipped[q], 1)
                    dve.wait_ge(clipped[q], 2 * n + 3)
                    nc.vector.scalar_tensor_tensor(
                        out=glu_steps[:, 2, :], in0=glu_steps[:, 2, :], scalar=1.0, in1=glu_steps[:, 0, :],
                        op0=ALU.add, op1=ALU.mult).then_inc(clipped[q], 1)
                    dve.wait_ge(clipped[q], 2 * n + 4)
                    dve.wait_ge(sig_ready[q], n + (1 + q))
                    nc.vector.tensor_tensor(glu_steps[:, 3, :], glu_steps[:, 2, :], glu_steps[:, 1, :],
                                            ALU.mult).then_inc(act_ready[q], 1)
                if blocks == 1:
                    count_on(give2_ready, 4 * n + 1, 4)
                    count_on(gate_read[1], n + 1, 1)
                    count_on(clipped[1], 2 * n + 2, 2)
                    count_on(act_ready[1], n + 1, 1)

            with dve.Fori(0, n_bodies) as g:
                for b in range(2):
                    two = [dve.value_load(two_blocks[0:1, bass.ds(4 * g + (2 * b + e), 1)], min_val=0, max_val=1)
                           for e in range(2)]
                    with dve.If(two[0] + two[1] > 0):
                        one_hot(4 * g + 2 * b, 1, pick[1], False, pick2_ready)
                        copy_picked(picked2, 1, 2 * g + (b + 2))
                    with dve.Else():
                        count_on(pick2_ready, 8 * g + (4 * b + 1), 4)
                        count_on(picked_ready[1], 4 * g + (2 * b + 1), 2)
                    one_hot(4 * g + 2 * b, 0, give, True, pick_ready)
                    plan_pick(4 * g + (2 * b + 2), 1 - b, (4 * g + (2 * b + 2)) % E)
                    for e in range(2):
                        with dve.If(two[e] > 0):
                            expert(g, b, e, 2)
                        with dve.Else():
                            expert(g, b, e, 1)
                        if e == 0:
                            copy_picked(picked[:, 1 - b], 0, 2 * g + (b + 2))
                    dve.wait_ge(unit_used, g * BODY_UNITS + (NF + (b + 1) * PAIR_UNITS))
                    nc.vector.tensor_copy(y_pair[:, 512:1024], t1_ps[:, :]).then_inc(y_dve, 1)
                    with dve.If(two[1] > 0):
                        nc.vector.tensor_copy(y_more[:, 1, :], up_ps[:, :]).then_inc(y_more_dve, 1)
                    with dve.Else():
                        count_on(y_more_dve, 2 * g + (b + 1), 1)

            dve.wait_ge(combined, n_bodies * 2)
            for i in range(QT):
                for c in range(2):
                    part = h2[:, i, c * 512:(c + 1) * 512]
                    nc.vector.tensor_tensor(part, acc[2 * i + c][:, :], part, ALU.add).then_inc(sum_ready, 1)
            dve.wait_ge(fin_root, 1)
            nc.vector.reciprocal(stat[:, 6:8], stat[:, 8:10]).then_inc(sum_ready, 1)
            dve.wait_ge(sum_ready, 5)
            dve.wait_ge(gfin_loaded, 16)
            for i in range(QT):
                nc.vector.scalar_tensor_tensor(out=x_nat[:, i, :], in0=h2[:, i, :], scalar=stat[:, 6 + i:7 + i],
                                               in1=gfin, op0=ALU.mult, op1=ALU.mult).then_inc(fin_ready, 1)

        @block.tensor
        def _(pe):
            mm = nc.tensor.matmul

            pe.wait_ge(pool_done, 1)
            pe.wait_ge(vecs_loaded, 96)
            pe.wait_ge(cw_loaded, 16)
            for c in range(CT):
                nc.tensor.transpose(ps[6][:, c * TAPS:(c + 1) * TAPS], cw_rows[:, c * P:(c + 1) * P],
                                    ident[0:TAPS, 0:TAPS])
            nc.tensor.transpose(ps[7][:, 0:V_ROWS], vec_rows, ident[0:V_ROWS, 0:V_ROWS]).then_inc(vec_ps_ready, 1)

            for k in range(KD):
                if k >= 6:
                    pe.wait_ge(vec_ready, 2)
                for i, (t0, n) in enumerate(((META, P), (META + P, P), (0, META))):
                    if k == 0:
                        pe.wait_ge(scaled_ready, i + 1)
                    ins = nc.tensor.transpose(ps[k][:, t0:t0 + n], x_scaled[0:n, i, k * P:(k + 1) * P],
                                              ident[0:n, 0:n])
                ins.then_inc(xt_ready, 1)
            pe.wait_ge(rel_loaded, 32)
            pe.wait_ge(hn_dve, 2)
            mm(ps[4][0:HEADS, :], rel_sb[:], bucket_sb[:, 0:512], start=True, stop=True)
            mm(ps[5][0:HEADS, 0:NTOE - 512], rel_sb[:], bucket_sb[:, 512:NTOE], start=True,
               stop=True).then_inc(toe_ps_ready, 1)
            pe.wait_ge(hn_act, 4)
            pe.wait_ge(hn_dve, 4)

            def front_unit(u, n, kk=KD):
                pe.wait_ge(slot_loaded[slot_of(u)], 16 * (loads_before(u) + 1))
                return ring[:, slot_of(u), 0:kk * n].rearrange("p (k n) -> p k n", k=kk)

            used = [0]

            def project(n):
                kind, i, u, c = tiles[n]
                if n >= 4:
                    pe.wait_ge(*read_by(n - 4))
                bank = ps[n % 4]
                if kind == "v":
                    ws = [front_unit(u + j, UNIT_COLS) for j in range(2)]
                    for j, w in enumerate(ws):
                        for k in range(KD):
                            ins = mm(bank[0:KEYN[i], j * UNIT_COLS:(j + 1) * UNIT_COLS],
                                     hn[:, k, KEY0[i]:KEY0[i] + KEYN[i]], w[:, k, :],
                                     start=(k == 0), stop=(k == KD - 1))
                elif kind == "ik":
                    w = front_unit(u, C_GLU - C_IK)
                    rows = slice(0, 72) if i == 0 else slice(64, 128)
                    cols = slice(0, 72) if i == 0 else slice(0, 64)
                    for k in range(KD):
                        ins = mm(bank[rows, 0:T], w[:, k, cols], hn[:, k, :], start=(k == 0), stop=(k == KD - 1))
                else:
                    w = front_unit(u, UNIT_COLS)
                    t0 = 0 if kind in ("g", "a", "k") else META
                    for k in range(KD):
                        ins = mm(bank[:, 0:T - t0], w[:, k, c:c + P], hn[:, k, t0:T],
                                 start=(k == 0), stop=(k == KD - 1))
                ins.then_inc(tile_ready, 1)
                nxt = tiles[n + 1][2] if n + 1 < NT else U_AO
                if nxt != u:
                    pe.wait_ge(tile_ready, n + 1)
                    pe.sem_inc(unit_used, nxt - u)

            for n in range(first["ik"] + 2):
                project(n)
            pe.wait_ge(tile_act, first["ik"] + 1 - 4 + 1)
            for i in range(QT):
                ins = nc.tensor.transpose(ps[4][:, i * HEADS:(i + 1) * HEADS], iw_t[64:72, i * P:(i + 1) * P],
                                          ident[64:72, 64:72])
            ins.then_inc(iw_ps_ready, 1)
            pe.wait_ge(iw_ready, 1)
            pe.wait_ge(idx_ready, 1)
            for m in range(QT * HEADS):
                i, h = divmod(m, HEADS)
                if m >= 4:
                    pe.wait_ge(relu_ready, m - 3)
                mm(ps[4 + m % 4][:, 0:SEEN[i]], iq[:, h // 2, i * P:(i + 1) * P], ik_half[:, h % 2, 0:SEEN[i]],
                   start=True, stop=True).then_inc(qk_ready, 1)
            for n in range(first["q"], first["gate"]):
                project(n)
            gate0 = first["gate"]
            for i in range(4):
                project(gate0 + i)
            pe.wait_ge(conv_ready, 1)
            pe.wait_ge(relu_ready, QT * HEADS)
            for c in range(CT):
                ins = mm(ps[4][:, 0:SEQ], mean_w[:], conv[:, c, :], start=(c == 0), stop=(c == CT - 1))
            ins.then_inc(mean_ready, 1)
            project(gate0 + 4)
            pe.wait_ge(squares_ready, 1)
            for c in range(CT):
                ins = mm(ps[5][:, 0:SEQ], mean_w[:], squares[:, c, :], start=(c == 0), stop=(c == CT - 1))
            ins.then_inc(var_ready, 1)
            project(gate0 + 5)
            pe.wait_ge(tile_act, first["k"] + 4 - 4)
            pe.wait_ge(idx_ready, 5)
            pe.wait_ge(centred_ready, 1)
            for j in range(QT * HEADS):
                m = QT * HEADS + j
                i, h = divmod(j, HEADS)
                if j == 1:
                    pe.wait_ge(ln_root, 1)
                if j >= 4:
                    pe.wait_ge(logit_ready, j - 3)
                mm(ps[4 + m % 4][:, 0:SEEN[i]], q_t[:, h // 2, i * P:(i + 1) * P], k_half[:, h, 0:SEEN[i]],
                   start=True, stop=True).then_inc(qk_ready, 1)
                if j % 2:
                    project(gate0 + 6 + j // 2)
            for i in range(14, 16):
                project(gate0 + i)

            def attend(i):
                r0 = 0 if i == 0 else 5
                pe.wait_ge(prob_ready, i + 1)
                pe.wait_ge(logit_ready, QT * HEADS)
                r = r0
                for s in range(2 + i):
                    for half in range(2):
                        if r >= 4:
                            pe.wait_ge(attn_copied, r - 3)
                        for j in range(4):
                            ins = nc.tensor.transpose(
                                ps[4 + r % 4][0:KEYN[s], j * P:(j + 1) * P],
                                probs[i][:, 4 * half + j, KEY0[s]:KEY0[s] + KEYN[s]], ident[:])
                        ins.then_inc(attn_ps_ready, 1)
                        r += 1
                pe.wait_ge(attn_copied, r)
                bank = ps[4 + r % 4]
                for h in range(HEADS):
                    for s in range(2 + i):
                        ins = mm(bank[(h % 2) * DH:(h % 2 + 1) * DH, (h // 2) * P:(h // 2 + 1) * P],
                                 v_sb[0:KEYN[s], s, h * DH:(h + 1) * DH], probs_t[0:KEYN[s], s, h, :],
                                 start=(s == 0), stop=(s == 1 + i))
                ins.then_inc(attn_ps_ready, 1)

            attend(0)
            attend(1)

            for half, (u, src) in enumerate(((U_AO, attn), (U_CO, conv))):
                ws = [front_unit(u + j, D, 2) for j in range(2)]
                if half == 0:
                    pe.wait_ge(attn_copied, 12)
                else:
                    pe.wait_ge(conv_out_ready, 1)
                for k in range(KD):
                    n = NT + half * KD + k
                    pe.wait_ge(*read_by(n - 4))
                    for q in range(4):
                        ins = mm(ps[n % 4][:, 0:SEQ], ws[q // 2][:, q % 2, k * P:(k + 1) * P], src[:, q, :],
                                 start=(q == 0), stop=(q == 3))
                    ins.then_inc(tile_ready, 1)
                pe.wait_ge(tile_ready, NT + (half + 1) * KD)
                pe.sem_inc(unit_used, 2)
            pe.wait_ge(attn_copied, 12)
            ws = [front_unit(U_WO + j, D, 2) for j in range(KD // 2)]
            for i in range(QT):
                for k in range(KD):
                    if i == 0:
                        pe.wait_ge(merged_ready, 2 * (k + 1))
                    for c in range(2):
                        ins = mm(ps[4 + 2 * i + c][:, :], merged[:, k, i * P:(i + 1) * P],
                                 ws[k // 2][:, k % 2, c * 512:(c + 1) * 512], start=(k == 0), stop=(k == KD - 1))
                    if i == 1 and k % 2:
                        ins.then_inc(unit_used, 1)
                    elif k == KD - 1:
                        ins.then_inc(h2_ps_ready, 1)
            for i in range(QT):
                pe.wait_ge(hs_ready, i + 1)
                if i == 0:
                    pe.wait_ge(tile_dve, 4 + 2 * KD)
                for k in range(KD):
                    c0 = (k % 2) * SEQ + i * P
                    ins = nc.tensor.transpose(ps[k // 2][:, c0:c0 + P], h_scaled[:, i, k * P:(k + 1) * P],
                                              ident[:])
                    if i == 1 and k % 2:
                        ins.then_inc(hst_ready, 1)
            pe.wait_ge(router_loaded, 32)
            pe.wait_ge(hf_act, 4)
            pe.wait_ge(hf_dve, 4)
            for i in range(QT):
                o = ps[4][:, i * E:(i + 1) * E]
                mm(o, ones[0:1, :], br_sb[:], start=True, stop=False)
                for k in range(KD):
                    ins = mm(o, hf[:, k, i * P:(i + 1) * P], wr_sb[:, k, :], start=False, stop=(k == KD - 1))
            ins.then_inc(rlog_ready, 1)
            pe.wait_ge(choice_ready, 1)
            mm(ps[5][:, 0:E], before[:], chosen[:, 0, :], start=True, stop=True)
            mm(ps[5][:, E:2 * E], ones[:], chosen[:, 0, :], start=True, stop=False)
            mm(ps[5][:, E:2 * E], before[:], chosen[:, 1, :], start=False, stop=True)
            mm(ps[5][:, 2 * E:3 * E], ones[:], chosen[:, 0, :], start=True, stop=False)
            mm(ps[5][:, 2 * E:3 * E], ones[:], chosen[:, 1, :], start=False, stop=True).then_inc(place_ps_ready, 1)
            pe.wait_ge(weight_ready, 1)
            for i in range(QT):
                ins = nc.tensor.transpose(ps[0][0:E, i * P:(i + 1) * P], combine_w[:, i, :], ident[:])
            ins.then_inc(weight_ps_ready, 1)

            def gather(q):
                for k in range(KD):
                    for i in range(QT):
                        ins = mm((t0_ps, t1_ps)[k // 4][:, (k % 4) * P:(k % 4 + 1) * P],
                                 h_scaled[:, i, k * P:(k + 1) * P], pick[q][:, i, :],
                                 start=(i == 0), stop=(i == QT - 1))
                ins.then_inc(gather_ready[q], 1)

            pe.wait_ge(pick_ready, 6)
            gather(0)
            pe.wait_ge(ct_ready, 1)
            pe.wait_ge(ebias_loaded, 32)
            for i in range(QT):
                for c in range(2):
                    mm(acc[2 * i + c][:, :], combine_t[:, i * P:(i + 1) * P], bd_sb[:, c * 512:(c + 1) * 512],
                       start=True, stop=False, skip_group_check=True)
            for signal in (gather_ready[1], actt_ps_ready[1], givet_ps_ready[1]):
                pe.sem_inc(signal, 1)
            n_bodies = pe.value_load(bodies[0:1, 0:1], min_val=PAIRS // 2,
                                     max_val=PASSES * PAIRS // 2)
            def unit(g, b, j):
                u = NF + b * PAIR_UNITS + j
                pe.wait_ge(slot_loaded[slot_of(u)], g * (16 * TURNS) + 16 * (loads_before(u) + 1))
                return ring[:, slot_of(u), :]

            def count_on(signal, before):
                pe.wait_ge(signal, before)
                pe.sem_inc(signal, 1)

            def expert(g, b, e, blocks):
                n = 4 * g + (2 * b + e)
                pe.wait_ge(clipped[0], 2 * n + 2)
                if e == 1 and blocks == 2:
                    pe.wait_ge(actt_ready[1], n + 1)
                    pe.wait_ge(givet_ready[1], n + 1)
                    pe.wait_ge(picked_ready[0], 4 * g + (2 * b + 4))
                outs = [(q, c, ((gate_ps, up_ps), (t0_ps, t1_ps))[q][c // 2], c % 2)
                        for q in range(blocks) for c in range(4)]
                for q, c, bank, half in outs[::-1]:
                    if e == 1 and (q, c) == (0, 1):
                        pe.wait_ge(actt_ready[0], n)
                    mm(bank[half * CAP:(half + 1) * CAP, :], choose[0:E, b, e * CAP:(e + 1) * CAP],
                       bu_sb[:, c * 512:(c + 1) * 512], start=True, stop=False)
                for k in range(UP_UNITS):
                    w = unit(g, b, e * UP_UNITS + k)
                    for q, c, bank, half in outs:
                        tokens = (picked[:, b], picked2)[q]
                        ins = mm(bank[half * CAP:(half + 1) * CAP, :], tokens[:, k, e * CAP:(e + 1) * CAP],
                                 w[:, c * 512:(c + 1) * 512], start=False, stop=(k == UP_UNITS - 1))
                    ins.then_inc(unit_used, 1)

                def transpose_act(q):
                    pe.wait_ge(act_ready[q], n + 2)
                    for j in range(4):
                        ins = nc.tensor.transpose((gate_ps, t0_ps)[q][:, j * P:(j + 1) * P],
                                                  glu_steps[:, 3, j * P:(j + 1) * P], ident[:])
                    ins.then_inc(actt_ps_ready[q], 1)

                def transpose_give():
                    for i in range(QT):
                        ins = nc.tensor.transpose(up_ps[:, i * P:(i + 1) * P], give[:, i, :], ident[:])
                    ins.then_inc(givet_ps_ready[0], 1)

                if blocks == 2:
                    transpose_act(0)
                    if e == 1:
                        transpose_give()
                    pe.wait_ge(clipped[1], 2 * n + 4)
                if e == 0:
                    pe.wait_ge(pick_ready, 20 * g + (6 + 10 * (b + 1)))
                    gather(0)
                if blocks == 1:
                    transpose_act(0)
                    if e == 1:
                        transpose_give()
                    count_on(actt_ps_ready[1], n + 1)
                    count_on(givet_ps_ready[1], n + 1)
                else:
                    if e == 0:
                        pe.wait_ge(picked_ready[0], 4 * g + (2 * b + 4))
                    transpose_act(1)
                    pe.wait_ge(give2_ready, 4 * n + 5)
                    for c in range(2):
                        for i in range(QT):
                            ins = nc.tensor.transpose(t1_ps[:, c * SEQ + i * P:c * SEQ + (i + 1) * P],
                                                      give_more[e][:, i, c * P:(c + 1) * P], ident[:])
                    ins.then_inc(givet_ps_ready[1], 1)

            def down(g, b, more):
                for f in range(DOWN_UNITS):
                    w = unit(g, b, 2 * UP_UNITS + f)
                    for c, bank in enumerate((t0_ps, t1_ps)):
                        for e in range(2):
                            ins = mm(bank[e * CAP:(e + 1) * CAP, :], act_t[0][:, e, f, :],
                                     w[:, e * D + c * 512:e * D + (c + 1) * 512],
                                     start=(f == 0), stop=(f == DOWN_UNITS - 1))
                    for e in more:
                        bank = (gate_ps, up_ps)[e]
                        for c in range(2):
                            ins = mm(bank[c * CAP:(c + 1) * CAP, :], act_t[1][:, e, f, :],
                                     w[:, e * D + c * 512:e * D + (c + 1) * 512],
                                     start=(f == 0), stop=(f == DOWN_UNITS - 1))
                    ins.then_inc(unit_used, 1)
                pe.wait_ge(y_act, 2 * g + (b + 2))
                pe.wait_ge(y_dve, 2 * g + (b + 2))
                for i in range(QT):
                    for c in range(2):
                        ins = mm(acc[2 * i + c][:, :], give_t[:, i * P:(i + 1) * P],
                                 y_pair[:, c * 512:(c + 1) * 512], start=False, stop=False,
                                 skip_group_check=True)
                for e in more:
                    pe.wait_ge((y_more_act, y_more_dve)[e], 2 * g + (b + 2))
                    for i in range(QT):
                        for c in range(2):
                            ins = mm(acc[2 * i + c][:, :], give_more_t[:, e, c, i * P:(i + 1) * P],
                                     y_more[:, e, :], start=False, stop=False, skip_group_check=True)
                ins.then_inc(combined, 1)

            with pe.Fori(0, n_bodies) as g:
                for b in range(2):
                    two = [pe.value_load(two_blocks[0:1, bass.ds(4 * g + (2 * b + e), 1)], min_val=0, max_val=1)
                           for e in range(2)]
                    for signal in (y_act, y_dve, y_more_act, y_more_dve):
                        pe.wait_ge(signal, 2 * g + (b + 1))
                    with pe.If(two[0] + two[1] > 0):
                        pe.wait_ge(pick2_ready, 8 * g + (4 * b + 5))
                        gather(1)
                        pe.wait_ge(picked_ready[1], 4 * g + (2 * b + 3))
                    with pe.Else():
                        count_on(gather_ready[1], 2 * g + (b + 1))
                    pe.wait_ge(picked_ready[0], 4 * g + (2 * b + 2))
                    for e in range(2):
                        with pe.If(two[e] > 0):
                            expert(g, b, e, 2)
                        with pe.Else():
                            expert(g, b, e, 1)
                    pe.wait_ge(actt_ready[0], 4 * g + (2 * b + 2))
                    pe.wait_ge(actt_ready[1], 4 * g + (2 * b + 3))
                    pe.wait_ge(givet_ready[0], 2 * g + (b + 1))
                    pe.wait_ge(givet_ready[1], 4 * g + (2 * b + 3))
                    pe.wait_ge(picked_ready[0], 4 * g + (2 * b + 4))
                    which = two[0] + 2 * two[1]
                    with pe.If(which < 2):
                        with pe.If(which < 1):
                            down(g, b, [])
                        with pe.Else():
                            down(g, b, [0])
                        pe.nop()
                    with pe.Else():
                        with pe.If(which < 3):
                            down(g, b, [1])
                        with pe.Else():
                            down(g, b, [0, 1])
                        pe.nop()


def bucket_rows():
    j = np.arange(NTOE)
    dist = T - 1 - j
    n = np.maximum(dist, 0)
    exact = NB // 2
    large = exact + (np.log(np.maximum(n, 1) / exact) / np.log(128 / exact) * (NB - exact)).astype(np.int32)
    bucket = np.where(n < exact, n, np.minimum(large, NB - 1))
    rows = np.zeros((NB + 1, NTOE), np.float32)
    rows[bucket[dist >= 0], j[dist >= 0]] = 1.0
    rows[NB, dist < 0] = FAR
    return rows


def kernel(**inputs):
    import concourse.bacc as bacc
    from concourse.bass_utils import run_bass_kernel_spmd

    a = {k: np.ascontiguousarray(v) for k, v in inputs.items()}
    order = ["x", "meta_tokens", "rel_bias", "norm_mix", "w_in", "b_gate", "w_attn_out", "conv_w", "conv_b",
             "conv_ln_g", "conv_ln_b", "w_conv_out", "w_out", "norm_ffn", "w_router", "b_router",
             "w_up_gate", "b_up_gate", "w_down", "b_down", "norm_final"]
    whole = ("meta_tokens", "rel_bias", "norm_final")
    nc = bacc.Bacc("TRN2", target_bir_lowering=False, num_devices=1)
    arrays, args = {}, []
    for name in order:
        v = a[name] if name in whole else a[name][0]
        arrays["in_" + name] = v
        args.append(nc.dram_tensor("in_" + name, v.shape, F32, kind="ExternalInput").ap())
    arrays["in_bucket_rows"] = bucket_rows()
    args.append(nc.dram_tensor("in_bucket_rows", (NB + 1, NTOE), F32, kind="ExternalInput").ap())
    args.append(nc.dram_tensor("out", (SEQ, D), F32, kind="ExternalOutput").ap())
    layer(nc, *args)
    r = run_bass_kernel_spmd(nc, [arrays], core_ids=[0])
    return r.results[0]["out"].reshape(1, SEQ, D)
```

```python
from contextlib import ExitStack

import numpy as np

import concourse.bass as bass
from concourse import mybir

F32 = mybir.dt.float32
I32 = mybir.dt.int32
U32 = mybir.dt.uint32
ALU = mybir.AluOpType
ACT = mybir.ActivationFunctionType
AX_X = mybir.AxisListType.X

P = 128
META = 16
D = 1024
KD = D // P
SEQ = 256
QT = SEQ // P
T = META + SEQ
HEADS = 8
DH = 64
HP = HEADS // 2
TOPK = 64
IDX_SCALE = (64 ** -0.5) * (8 ** -0.5)
CH = 512
CT = CH // P
TAPS = 31
NB = 32
E = 32
FF = 1024
CAP = 64
PASS_CAP = 2 * CAP
PASSES = SEQ // PASS_CAP
PAIRS = E // 2
EPS = 1e-6
FAR = -1.0e30
TAKEN = -3.0e38
NTOE = 2 * T - 1

C_Q, C_K, C_V, C_IQ, C_IK, C_IW, C_GLU, C_GATE = 0, 512, 1024, 1536, 2048, 2112, 2120, 3144
UNIT_COLS = 256
SLOT = 2048

KEY0 = [0, META, META + P]
KEYN = [META, P, P]
SEEN = [META + P, T]

FRONT = [("in", C_GLU + CH), ("in", C_GLU), ("in", C_GLU + CH + UNIT_COLS), ("in", C_GLU + UNIT_COLS),
         ("in", C_IQ), ("in", C_IQ + UNIT_COLS), ("ik", C_IK),
         ("in", C_Q), ("in", C_Q + UNIT_COLS), ("in", C_K), ("in", C_K + UNIT_COLS),
         ("in", C_V), ("in", C_V + UNIT_COLS)]
FRONT += [("in", C_GATE + UNIT_COLS * i) for i in range(8)]
FRONT += [("co", 0), ("co", 2), ("ao", 0), ("ao", 2)] + [("wo", 2 * i) for i in range(4)]
NF = len(FRONT)
UP_UNITS, DOWN_UNITS = KD, FF // P
PAIR_UNITS = 2 * UP_UNITS + DOWN_UNITS
BODY_UNITS = 2 * PAIR_UNITS
RING = 12
assert BODY_UNITS % RING == 0
TURNS = BODY_UNITS // RING

V_MIX, V_FFN, V_CB, V_LG, V_LB, V_BG = 0, 8, 16, 20, 24, 28
V_ROWS = 44


def slot_of(u):
    return u % RING


def loads_before(u):
    return u // RING


def layer(nc, x, meta, rel_bias, norm_mix, w_in, b_gate, w_attn_out, conv_w, conv_b, ln_g, ln_b,
          w_conv_out, w_out, norm_ffn, w_router, b_router, w_ug, b_ug, w_down, b_down, norm_final,
          bucket_rows, order_rows, out):
    with ExitStack() as ctx:
        def sb(name, shape, dt=F32):
            return ctx.enter_context(nc.sbuf_tensor(name, shape, dt))

        def sem(name):
            return ctx.enter_context(nc.semaphore(name))

        ring = sb("ring", [P, RING, SLOT])
        x_nat = sb("x_nat", [P, QT, D])
        gate_region = sb("gate_region", [P, 16 * SEQ])
        x_scaled = gate_region[:, 0:3 * D].rearrange("p (i n) -> p i n", i=3)
        meta_nat = gate_region[:, 3 * D:4 * D]
        gates = gate_region[:, :].rearrange("p (i n) -> p i n", i=16)
        h_scaled = gate_region[:, 0:2 * D].rearrange("p (i n) -> p i n", i=2)
        picked = gate_region[:, 2 * D:4 * D].rearrange("p (b k n) -> p b k n", b=2, k=KD)
        hn_region = sb("hn_region", [P, KD * T])
        hn = hn_region[:, :].rearrange("p (k t) -> p k t", k=KD)
        merged = hn_region[:, 0:KD * SEQ].rearrange("p (k t) -> p k t", k=KD)
        glu_steps = hn_region[:, 0:4 * 512].rearrange("p (i n) -> p i n", i=4)
        iq_region = sb("iq_region", [P, 4 * SEQ + 2 * T])
        iq = iq_region[:, 0:4 * SEQ].rearrange("p (k t) -> p k t", k=4)
        ik_half = iq_region[:, 4 * SEQ:].rearrange("p (k t) -> p k t", k=2)
        attn = iq_region[:, 0:4 * SEQ].rearrange("p (k t) -> p k t", k=4)
        pick0 = iq_region[:, 0:512].rearrange("p (i n) -> p i n", i=QT)[:, :, 0:P]
        give0 = iq_region[:, 512:1024].rearrange("p (i n) -> p i n", i=QT)[:, :, 0:P]
        choose = iq_region[:, 1280:1536].rearrange("p (b n) -> p b n", b=2)
        qk_region = sb("qk_region", [P, 4 * SEQ + HEADS * T])
        q_t = qk_region[:, 0:4 * SEQ].rearrange("p (k t) -> p k t", k=4)
        k_half = qk_region[:, 4 * SEQ:].rearrange("p (h t) -> p h t", h=HEADS)
        bu_sb = qk_region[0:E, 0:2 * FF]
        prob_region = sb("prob_region", [P, HEADS * (SEEN[0] + SEEN[1])])
        probs = [prob_region[:, 0:HEADS * SEEN[0]].rearrange("p (h s) -> p h s", h=HEADS),
                 prob_region[:, HEADS * SEEN[0]:].rearrange("p (h s) -> p h s", h=HEADS)]
        h2 = prob_region[:, 0:2 * D].rearrange("p (i n) -> p i n", i=2)
        pt_region = sb("pt_region", [P, 3 * HEADS * P])
        probs_t = pt_region[:, :].rearrange("p (i h q) -> p i h q", i=3, h=HEADS)
        centred = pt_region[:, 0:CT * SEQ].rearrange("p (c t) -> p c t", c=CT)
        squares = pt_region[:, CT * SEQ:2 * CT * SEQ].rearrange("p (c t) -> p c t", c=CT)
        swish = pt_region[:, 2 * CT * SEQ:3 * CT * SEQ].rearrange("p (c t) -> p c t", c=CT)
        hf = pt_region[:, 0:KD * SEQ].rearrange("p (k t) -> p k t", k=KD)
        gfin = pt_region[:, 2 * D:3 * D]
        rpart = pt_region[:, 2 * D:2 * D + SEQ]
        v_region = sb("v_region", [P, 3 * 512])
        v_sb = v_region[:, :].rearrange("p (i n) -> p i n", i=3)
        glu_region = sb("glu_region", [P, CT * (TAPS - 1 + T)])
        glu = glu_region[:, :].rearrange("p (c t) -> p c t", c=CT)
        conv_region = sb("conv_region", [P, CT * SEQ])
        conv = conv_region[:, :].rearrange("p (c t) -> p c t", c=CT)
        picked2 = pt_region[:, 0:D].rearrange("p (k n) -> p k n", k=KD)
        act_t = [conv_region[:, :].rearrange("p (e f n) -> p e f n", e=2, f=8),
                 prob_region[:, 2 * D:3 * D].rearrange("p (e f n) -> p e f n", e=2, f=8)]
        y_pair = glu_region[:, 0:D]
        y_more = v_region[:, 0:D].rearrange("p (e n) -> p e n", e=2)
        glu_sig = sb("glu_sig", [P, 2, T])
        score = sb("score", [P, QT, T])
        seen_bias = sb("seen_bias", [P, QT, T])
        relu = glu_sig
        pick = [pick0, seen_bias[:, :, 0:P]]
        give = give0
        give_t = iq_region[:, 1024:1280]
        give_more = [v_region[:, D:D + 2 * SEQ].rearrange("p (i n) -> p i n", i=QT), score[:, :, 0:SEQ]]
        give_more_t = pt_region[:, D:2 * D].rearrange("p (e c t) -> p e c t", e=2, c=2)
        ln_rows = glu_region[:, 0:2 * SEQ].rearrange("p (i t) -> p i t", i=2)
        ident = sb("ident", [P, P])
        ones = sb("ones", [P, P])
        mean_w = sb("mean_w", [P, P])
        before = sb("before", [P, P])
        number = sb("number", [P, P])
        eps_col = sb("eps_col", [P, 1])
        vec_rows = pt_region[0:V_ROWS, 1600:1600 + P]
        vec = sb("vec", [P, V_ROWS])
        cw_rows = pt_region[0:TAPS, 1088:1088 + CH]
        cw = sb("cw", [P, CT, TAPS])
        rel_sb = sb("rel_sb", [NB + 1, HEADS])
        bucket_sb = pt_region[0:NB + 1, 0:NTOE]
        toe_sb = pt_region[0:HEADS, 544:544 + NTOE]
        iw_t = pt_region[0:72, 1728:1728 + SEQ]
        iw = sb("iw", [P, QT, HEADS])
        stat = sb("stat", [P, 16])
        top8 = sb("top8", [P, QT, 8])
        smax = sb("smax", [P, QT, HEADS])
        sneg = sb("sneg", [P, QT, HEADS])
        ssum = sb("ssum", [P, QT, HEADS])
        srec = sb("srec", [P, QT, HEADS])
        wr_sb = sb("wr_sb", [P, KD, E])
        br_sb = sb("br_sb", [P, E])
        rank_rows = sb("rank_rows", [E, 2 * E + 2])
        fold = sb("fold", [P, E])
        rank = sb("rank", [E, 3 * E + 4])
        order_of = sb("order_of", [P, E * PASSES + 2], I32)
        rlog = sb("rlog", [P, QT, E])
        ridx = sb("ridx", [P, QT, 8], U32)
        ridxf = sb("ridxf", [P, QT, 8])
        rexp = sb("rexp", [P, QT, 4])
        hot = sb("hot", [P, QT, 4, E])
        chosen = sb("chosen", [P, QT, E])
        combine_w = sb("combine_w", [P, QT, E])
        place = sb("place", [P, QT, E * PASSES + 2])
        weight = sb("weight", [P, QT, E * PASSES + 2])
        counts = sb("counts", [P, 8])
        scrap = sb("scrap", [P, 1])
        two_blocks = sb("two_blocks", [1, E * PASSES])
        pair_kind = sb("pair_kind", [1, PAIRS * PASSES], I32)
        bodies = sb("bodies", [P, 1], I32)
        dram_toe = nc.dram_tensor("toeplitz_rows", (P, HEADS, NTOE), F32, kind="Internal").ap()

        ps = [ctx.enter_context(nc.psum_tensor(f"bank{i}", [P, 512], F32)) for i in range(8)]
        acc = ps[0:4]
        gate_ps, up_ps, t0_ps, t1_ps = ps[4:8]

        x_loaded = [sem(f"x{i}_loaded") for i in range(QT)]
        meta_loaded = sem("meta_loaded")
        vecs_loaded = sem("vecs_loaded")
        cw_loaded = sem("cw_loaded")
        rel_loaded = sem("rel_loaded")
        toe_stored = sem("toe_stored")
        toe_loaded = sem("toe_loaded")
        router_loaded = sem("router_loaded")
        ebias_loaded = sem("ebias_loaded")
        gfin_loaded = sem("gfin_loaded")
        slot_loaded = [sem(f"slot{i}_loaded") for i in range(RING)]
        unit_used = sem("unit_used")
        zeroed = sem("zeroed")
        pool_done = sem("pool_done")
        act_chain = sem("act_chain")
        dve_chain = sem("dve_chain")
        table_ready = sem("table_ready")
        ss_ready = sem("ss_ready")
        root_ready = sem("root_ready")
        scaled_ready = sem("scaled_ready")
        vec_ps_ready = sem("vec_ps_ready")
        vec_ready = sem("vec_ready")
        xt_ready = sem("xt_ready")
        hn_act = sem("hn_act")
        hn_dve = sem("hn_dve")
        toe_ps_ready = sem("toe_ps_ready")
        tile_ready = sem("tile_ready")
        tile_act = sem("tile_act")
        tile_dve = sem("tile_dve")
        iw_ps_ready = sem("iw_ps_ready")
        iw_ready = sem("iw_ready")
        idx_ready = sem("idx_ready")
        relu_ready = sem("relu_ready")
        relu_used = sem("relu_used")
        seen_ready = sem("seen_ready")
        bias_ready = sem("bias_ready")
        qk_ready = sem("qk_ready")
        logit_ready = sem("logit_ready")
        max_ready = sem("max_ready")
        exp_ready = sem("exp_ready")
        prob_ready = sem("prob_ready")
        attn_ps_ready = sem("attn_ps_ready")
        attn_copied = sem("attn_copied")
        meta_values = sem("meta_values")
        conv_ready = sem("conv_ready")
        mean_ready = sem("mean_ready")
        centred_ready = sem("centred_ready")
        squares_ready = sem("squares_ready")
        var_ready = sem("var_ready")
        ln_root = sem("ln_root")
        normed_ready = sem("normed_ready")
        swish_ready = sem("swish_ready")
        conv_out_ready = sem("conv_out_ready")
        merged_ready = sem("merged_ready")
        h2_ps_ready = sem("h2_ps_ready")
        h2_ready = sem("h2_ready")
        hs_ready = sem("hs_ready")
        hst_ready = sem("hst_ready")
        hf_dve = sem("hf_dve")
        rpart_ready = sem("rpart_ready")
        rpart_copied = sem("rpart_copied")
        rlog_ready = sem("rlog_ready")
        rank_ready = sem("rank_ready")
        order_ps_ready = sem("order_ps_ready")
        rmax_ready = sem("rmax_ready")
        rexp_ready = sem("rexp_ready")
        choice_ready = sem("choice_ready")
        weight_ready = sem("weight_ready")
        weight_ps_ready = sem("weight_ps_ready")
        give_zeroed = sem("give_zeroed")
        place_ps_ready = sem("place_ps_ready")
        ct_ready = sem("ct_ready")
        plan_ready = sem("plan_ready")
        pick_ready = sem("pick_ready")
        pick2_ready = sem("pick2_ready")
        give2_ready = sem("give2_ready")
        y_more_act = sem("y_more_act")
        y_more_dve = sem("y_more_dve")
        gather_ready = [sem("gather_ready"), sem("gather_ready_2")]
        picked_ready = [sem("picked_ready"), sem("picked_ready_2")]
        gate_read = [sem("gate_read"), sem("gate_read_2")]
        clipped = [sem("clipped"), sem("clipped_2")]
        sig_ready = [sem("sig_ready"), sem("sig_ready_2")]
        act_ready = [sem("act_ready"), sem("act_ready_2")]
        actt_ps_ready = [sem("actt_ps_ready"), sem("actt_ps_ready_2")]
        actt_ready = [sem("actt_ready"), sem("actt_ready_2")]
        givet_ps_ready = [sem("givet_ps_ready"), sem("givet_ps_ready_2")]
        givet_ready = [sem("givet_ready"), sem("givet_ready_2")]
        y_act = sem("y_act")
        y_dve = sem("y_dve")
        combined = sem("combined")
        fin_sum = sem("fin_sum")
        fold_ready = sem("fold_ready")
        fin_ss = sem("fin_ss")
        fin_root = sem("fin_root")
        fin_ready = sem("fin_ready")
        stored = sem("stored")

        tiles = []
        for i in range(2):
            tiles += [("g", 2 * i, 2 * i, 0), ("g", 2 * i + 1, 2 * i, P),
                      ("a", 2 * i, 2 * i + 1, 0), ("a", 2 * i + 1, 2 * i + 1, P)]
        tiles += [("iq", i, 4 + i // 2, P * (i % 2)) for i in range(4)]
        tiles += [("ik", 0, 6, 0)]
        tiles += [("q", i, 7 + i // 2, P * (i % 2)) for i in range(4)]
        tiles += [("k", i, 9 + i // 2, P * (i % 2)) for i in range(4)]
        tiles += [("v", i, 11, 0) for i in range(3)]
        tiles += [("gate", i, 13 + i // 2, P * (i % 2)) for i in range(16)]
        first = {}
        for n, (kind, *_) in enumerate(tiles):
            first.setdefault(kind, n)
        NT = len(tiles)
        U_CO, U_AO, U_WO = 21, 23, 25

        def read_by(n):
            if n >= NT:
                return tile_dve, 4 + n - NT + 1
            dve = sum(k == "a" for k, *_ in tiles[:n + 1])
            return (tile_dve, dve) if tiles[n][0] == "a" else (tile_act, n + 1 - dve)

        CONSTS = 13 + PASSES + 1

        block = ctx.enter_context(nc.Block())

        @block.sync
        def _(sp):
            for i in range(QT):
                sp.dma_start(x_nat[:, i, :], x[i * P:(i + 1) * P, :]).then_inc(x_loaded[i], 16)
            for r, n, v in ((V_MIX, 8, norm_mix), (V_FFN, 8, norm_ffn), (V_CB, 4, conv_b),
                            (V_LG, 4, ln_g), (V_LB, 4, ln_b), (V_BG, 16, b_gate)):
                sp.dma_start(vec_rows[r:r + n, :], v.rearrange("(k p) -> k p", p=P)).then_inc(vecs_loaded, 16)
            with nc.allow_non_contiguous_dma(reason="rows of the packed vectors and of the weights"):
                for u, (kind, c) in enumerate(FRONT):
                    if u >= RING:
                        sp.wait_ge(unit_used, u - RING + 1)
                    dst = ring[:, slot_of(u), :]
                    if kind == "in" or kind == "ik":
                        n = UNIT_COLS if kind == "in" else C_GLU - C_IK
                        dst = dst[:, 0:KD * n].rearrange("p (k n) -> p k n", k=KD)
                        src = w_in.rearrange("(k p) n -> p k n", p=P)[:, :, c:c + n]
                    else:
                        w = {"ao": w_attn_out, "co": w_conv_out, "wo": w_out}[kind]
                        dst = dst.rearrange("p (k n) -> p k n", k=2)
                        src = w.rearrange("(k p) n -> p k n", p=P)[:, c:c + 2, :]
                    sp.dma_start(dst, src).then_inc(slot_loaded[slot_of(u)], 16)

                def experts(first_body, i):
                    for j in range(BODY_UNITS):
                        pair, r = divmod(j, PAIR_UNITS)
                        u = NF + j
                        if r == 0:
                            if pair == 1:
                                sp.wait_ge(plan_ready, 1)
                            ids = [sp.value_load(order_of[0:1, bass.ds(4 * i + (2 * pair + e), 1)], min_val=0,
                                                 max_val=E - 1) for e in range(2)]
                        sp.wait_ge(unit_used, (first_body + i) * BODY_UNITS + (u - RING + 1))
                        dst = ring[:, slot_of(u), :]
                        if r < 2 * UP_UNITS:
                            e, k = divmod(r, UP_UNITS)
                            src = w_ug[bass.ds(ids[e], 1), k * P:(k + 1) * P, :].rearrange("e p n -> p (e n)")
                        else:
                            f, e = divmod(r - 2 * UP_UNITS, 2)
                            dst = dst.rearrange("p (f n) -> p f n", f=2)
                            src = w_down[bass.ds(ids[e], 1), 2 * f * P:(2 * f + 2) * P, :].rearrange(
                                "e (f p) n -> p (e f) n", p=P)
                        sp.dma_start(dst, src).then_inc(slot_loaded[slot_of(u)], 16)

                sp.wait_ge(pool_done, CONSTS)
                with sp.Fori(0, PAIRS // 2) as i:
                    experts(0, i)
                sp.wait_ge(plan_ready, 1)
                n_bodies = sp.value_load(bodies[0:1, 0:1], min_val=PAIRS // 2,
                                         max_val=PASSES * PAIRS // 2)
                with sp.If(n_bodies > PAIRS // 2):
                    with sp.Fori(PAIRS // 2, n_bodies, PAIRS // 2) as done:
                        with sp.Fori(0, PAIRS // 2) as i:
                            experts(done, i)
            for i in range(QT):
                sp.wait_ge(fin_ready, 2 * i + 2)
                sp.dma_start(out[i * P:(i + 1) * P, :], x_nat[:, i, :]).then_inc(stored, 16)
            sp.wait_ge(stored, 16 * QT)

        @block.gpsimd
        def _(pool):
            nc.gpsimd.memset(ident[:], 0.0).then_inc(zeroed, 1)
            nc.gpsimd.memset(ones[:], 1.0).then_inc(zeroed, 1)
            nc.gpsimd.memset(before[:], 1.0).then_inc(zeroed, 1)
            nc.gpsimd.memset(seen_bias[:], 0.0).then_inc(zeroed, 1)
            nc.gpsimd.memset(rel_sb[:], 1.0).then_inc(zeroed, 1)
            nc.gpsimd.memset(eps_col[:], EPS).then_inc(zeroed, 1)
            pool.wait_ge(zeroed, 6)
            nc.gpsimd.affine_select(out=ident[:], in_=ident[:], compare_op=ALU.not_equal, fill=1.0,
                                    base=0, pattern=[[-1, P]], channel_multiplier=1).then_inc(pool_done, 1)
            nc.gpsimd.affine_select(out=before[:], in_=before[:], compare_op=ALU.is_gt, fill=0.0,
                                    base=0, pattern=[[1, P]], channel_multiplier=-1).then_inc(pool_done, 1)
            for i in range(QT):
                nc.gpsimd.affine_select(out=seen_bias[:, i, :], in_=seen_bias[:, i, :],
                                        compare_op=ALU.is_ge, fill=FAR, base=META + i * P,
                                        pattern=[[-1, T]], channel_multiplier=1).then_inc(pool_done, 1)
            nc.gpsimd.memset(mean_w[:], 1.0 / CH).then_inc(pool_done, 1)
            nc.gpsimd.iota(number[:], pattern=[[1, P]], base=0, channel_multiplier=0,
                           allow_small_or_imprecise_dtypes=True).then_inc(pool_done, 1)
            nc.gpsimd.memset(glu[:, :, 0:TAPS - 1], 0.0).then_inc(pool_done, 1)
            pool.wait_ge(pool_done, 7)
            nc.gpsimd.memset(ik_half[64:128, 0, :], 0.0).then_inc(pool_done, 1)
            nc.gpsimd.memset(k_half[64:128, 0:HEADS:2, :], 0.0).then_inc(pool_done, 1)
            pool.wait_ge(pool_done, 9)
            nc.gpsimd.memset(ik_half[0:64, 1, :], 0.0).then_inc(pool_done, 1)
            nc.gpsimd.memset(k_half[0:64, 1:HEADS:2, :], 0.0).then_inc(pool_done, 1)
            nc.gpsimd.memset(place[:], -1.0).then_inc(pool_done, 1)
            nc.gpsimd.memset(weight[:], 0.0).then_inc(pool_done, 1)
            for q in range(PASSES + 1):
                nc.gpsimd.iota(order_of[:, q * E:q * E + 2], pattern=[[1, 2]], base=q * E,
                               channel_multiplier=0).then_inc(pool_done, 1)
            for i in range(QT):
                pool.wait_ge(toe_loaded, 32)
                pool.wait_ge(seen_ready, i + 1)
                w = SEEN[i]
                left_out = seen_bias[:, i, 0:w].unsqueeze(1).broadcast_to([P, HEADS, w])
                nc.gpsimd.tensor_tensor(probs[i], probs[i], left_out, ALU.add).then_inc(bias_ready, 1)

        @block.scalar
        def _(act):
            chain = [0]

            def link(ins):
                chain[0] += 1
                ins.then_inc(act_chain, 1)
                act.wait_ge(act_chain, chain[0])

            def load_root_table():
                nc.scalar.activation(scrap[:], eps_col[:], ACT.Sqrt).then_inc(table_ready, 1)

            with nc.allow_non_contiguous_dma(reason="small vectors"):
                act.dma_start(meta_nat[0:META, :], meta).then_inc(meta_loaded, 16)
                act.dma_start(cw_rows, conv_w).then_inc(cw_loaded, 16)
            act.wait_ge(zeroed, 6)
            load_root_table()

            for i in (2, 0, 1):
                act.wait_ge(x_loaded[i] if i < QT else meta_loaded, 16)
                rows = x_nat[:, i, :] if i < QT else meta_nat[0:META, :]
                n = P if i < QT else META
                nc.scalar.activation(x_scaled[0:n, i, :], rows, ACT.Square,
                                     accum_out=stat[0:n, i:i + 1]).then_inc(ss_ready, 1)
            act.wait_ge(ss_ready, 3)
            nc.scalar.activation(stat[:, 3:5], stat[:, 0:2], ACT.Sqrt, scale=1.0 / D,
                                 bias=eps_col[:]).then_inc(root_ready, 1)
            nc.scalar.activation(stat[0:META, 5:6], stat[0:META, 2:3], ACT.Sqrt, scale=1.0 / D,
                                 bias=eps_col[0:META]).then_inc(root_ready, 1)
            with nc.allow_non_contiguous_dma(reason="small tables"):
                act.dma_start(rel_sb[0:NB, :], rel_bias).then_inc(rel_loaded, 16)
                act.dma_start(bucket_sb, bucket_rows).then_inc(rel_loaded, 16)
                act.dma_start(wr_sb[:], w_router.rearrange("(k p) n -> p k n", p=P)).then_inc(router_loaded, 16)
                act.dma_start(br_sb[:], b_router.rearrange("(a n) -> a n", a=1).broadcast_to([P, E])).then_inc(router_loaded, 16)
                act.dma_start(rank_rows[:], order_rows).then_inc(router_loaded, 16)
            act.wait_ge(vec_ready, 2)
            for k in range(4):
                act.wait_ge(xt_ready, k + 1)
                nc.scalar.activation(hn[:, k, :], ps[k][:, 0:T], ACT.Copy,
                                     scale=vec[:, V_MIX + k:V_MIX + k + 1]).then_inc(hn_act, 1)

            def read_tile(n):
                kind, i, _, _ = tiles[n]
                bank = ps[n % 4]
                act.wait_ge(tile_ready, n + 1)
                if kind == "g":
                    if i >= 2:
                        act.wait_ge(tile_dve, i - 1)
                    ins = nc.scalar.activation(glu_sig[:, i % 2, :], bank[:, 0:T], ACT.Sigmoid)
                elif kind == "iq":
                    ins = nc.scalar.copy(iq[:, i, :], bank[:, 0:SEQ])
                elif kind == "ik":
                    act.wait_ge(pool_done, CONSTS)
                    for half in range(2):
                        nc.scalar.copy(ik_half[64 * half:64 * (half + 1), half, :], bank[0:64, 0:T]
                                       ).then_inc(idx_ready, 1)
                    ins = nc.scalar.copy(iw_t[64:72, :], bank[64:72, META:T])
                elif kind == "q":
                    ins = nc.scalar.copy(q_t[:, i, :], bank[:, 0:SEQ])
                elif kind == "k":
                    nc.scalar.copy(k_half[0:64, 2 * i, :], bank[0:64, 0:T]).then_inc(idx_ready, 1)
                    ins = nc.scalar.copy(k_half[64:128, 2 * i + 1, :], bank[64:128, 0:T])
                elif kind == "v" and i == 0:
                    for j in range(4):
                        ins = nc.scalar.copy(v_sb[0:META, 0, j * P:(j + 1) * P], bank[32 * j:32 * j + META, 0:P])
                        if j < 3:
                            ins.then_inc(meta_values, 1)
                elif kind == "v":
                    ins = nc.scalar.copy(v_sb[0:KEYN[i], i, :], bank[0:KEYN[i], :])
                else:
                    if i == 0:
                        act.wait_ge(hn_dve, 4)
                    ins = nc.scalar.activation(gates[:, i, :], bank[:, 0:SEQ], ACT.Sigmoid,
                                               bias=vec[:, V_BG + i:V_BG + i + 1])
                ins.then_inc(tile_act, 1)

            for n in range(first["ik"] + 1):
                if n == 4:
                    act.wait_ge(toe_ps_ready, 1)
                    link(nc.scalar.copy(toe_sb[:, 0:512], ps[4][0:HEADS, :]))
                    link(nc.scalar.copy(toe_sb[:, 512:NTOE], ps[5][0:HEADS, 0:NTOE - 512]))
                    with nc.allow_non_contiguous_dma(reason="Toeplitz rows"):
                        act.dma_start(dram_toe.rearrange("p h j -> h p j"),
                                      toe_sb.unsqueeze(1).broadcast_to([HEADS, P, NTOE])).then_inc(toe_stored, 16)
                if n == first["iq"]:
                    act.wait_ge(toe_stored, 16)
                    for i in range(QT):
                        w = SEEN[i]
                        rows = bass.AP(dram_toe.tensor, T - 1 - META - i * P,
                                       [[HEADS * NTOE - 1, P], [NTOE, HEADS], [1, w]])
                        act.dma_start(probs[i], rows).then_inc(toe_loaded, 16)
                if tiles[n][0] != "a":
                    read_tile(n)
            act.wait_ge(iw_ps_ready, 1)
            nc.scalar.mul(iw[:], ps[4][:, 0:QT * HEADS].rearrange("p (i h) -> p i h", i=QT),
                          IDX_SCALE).then_inc(iw_ready, 1)
            for m in range(QT * HEADS):
                w = SEEN[m // HEADS]
                act.wait_ge(qk_ready, m + 1)
                if m >= 2:
                    act.wait_ge(relu_used, m - 1)
                nc.scalar.activation(relu[:, m % 2, 0:w], ps[4 + m % 4][:, 0:w], ACT.Relu).then_inc(relu_ready, 1)
            for n in range(first["q"], first["gate"]):
                read_tile(n)

            def softmax_exp(i):
                act.wait_ge(max_ready, i + 1)
                for h in range(HEADS):
                    nc.scalar.activation(probs[i][:, h, :], probs[i][:, h, :], ACT.Exp,
                                         bias=sneg[:, i, h:h + 1],
                                         accum_out=ssum[:, i, h:h + 1]).then_inc(exp_ready, 1)

            def copy_probs(i):
                r0 = 0 if i == 0 else 5
                groups = [(s, g) for s in range(2 + i) for g in range(2)]
                if i == 0:
                    act.wait_ge(conv_out_ready, 1)
                for r, (s, g) in enumerate(groups):
                    act.wait_ge(attn_ps_ready, r0 + r + 1)
                    nc.scalar.copy(probs_t[0:KEYN[s], s, 4 * g:4 * g + 4, :],
                                   ps[4 + (r0 + r) % 4][0:KEYN[s], :].rearrange("p (h q) -> p h q", h=4)
                                   ).then_inc(attn_copied, 1)
                r = r0 + len(groups)
                act.wait_ge(attn_ps_ready, r + 1)
                nc.scalar.copy(attn[:, :, i * P:(i + 1) * P],
                               ps[4 + r % 4][:, :].rearrange("p (c q) -> p c q", c=HP)).then_inc(attn_copied, 1)

            def read_gates(i0, i1):
                for n in range(first["gate"] + i0, first["gate"] + i1):
                    read_tile(n)

            read_gates(0, 4)
            act.wait_ge(centred_ready, 1)
            nc.scalar.activation(squares, centred, ACT.Square).then_inc(squares_ready, 1)
            read_gates(4, 5)
            act.wait_ge(var_ready, 1)
            nc.scalar.activation(ln_rows[:, 0, :], ps[5][:, 0:SEQ], ACT.Sqrt,
                                 bias=eps_col[:]).then_inc(ln_root, 1)
            read_gates(5, 10)
            softmax_exp(0)
            act.wait_ge(normed_ready, 1)
            for c in range(CT):
                nc.scalar.activation(swish[:, c, :], centred[:, c, :], ACT.Sigmoid,
                                     scale=vec[:, V_LG + c:V_LG + c + 1],
                                     bias=vec[:, V_LB + c:V_LB + c + 1]).then_inc(swish_ready, 1)
            read_gates(10, 14)
            softmax_exp(1)
            read_gates(14, 16)
            copy_probs(0)
            copy_probs(1)

            act.wait_ge(logit_ready, QT * HEADS)
            act.dma_start(bu_sb, b_ug).then_inc(ebias_loaded, 16)
            act.wait_ge(give_zeroed, 1)
            act.dma_start(y_pair[0:E, :], b_down).then_inc(ebias_loaded, 16)

            load_root_table()
            for i in range(QT):
                act.wait_ge(h2_ready, 2 * i + 2)
                if i == 0:
                    act.wait_ge(merged_ready, 2 * KD)
                nc.scalar.activation(h_scaled[:, i, :], h2[:, i, :], ACT.Square,
                                     accum_out=stat[:, 6 + i:7 + i]).then_inc(ss_ready, 1)
                act.wait_ge(ss_ready, 4 + i)
                nc.scalar.activation(stat[:, 8 + i:9 + i], stat[:, 6 + i:7 + i], ACT.Sqrt, scale=1.0 / D,
                                     bias=eps_col[:]).then_inc(root_ready, 1)
            act.wait_ge(rmax_ready, 1)
            for i in range(QT):
                nc.scalar.activation(rexp[:, i, :], top8[:, i, 0:4], ACT.Exp, bias=stat[:, 10 + i:11 + i],
                                     accum_out=stat[:, 12 + i:13 + i]).then_inc(rexp_ready, 1)
            act.wait_ge(rlog_ready, 1)
            with nc.allow_non_contiguous_dma(reason="one row for every partition"):
                act.dma_start(gfin, norm_final.rearrange("(a n) -> a n", a=1).broadcast_to([P, D])
                              ).then_inc(gfin_loaded, 16)

            act.wait_ge(plan_ready, 1)
            n_bodies = act.value_load(bodies[0:1, 0:1], min_val=PAIRS // 2,
                                      max_val=PASSES * PAIRS // 2)
            for signal in (sig_ready[1], actt_ready[1], givet_ready[1], y_act, y_more_act):
                act.sem_inc(signal, 1)

            def expert(g, b, e, blocks):
                n = 4 * g + (2 * b + e)
                for q in range(blocks):
                    act.wait_ge(gate_read[q], n + (1 + q))
                    act.wait_ge(act_ready[0], n + (1 + q))
                    act.wait_ge(act_ready[1], n + 1)
                    nc.scalar.activation(glu_steps[:, 1, :], glu_steps[:, 0, :], ACT.Sigmoid,
                                         scale=1.702).then_inc(sig_ready[q], 1)
                    act.wait_ge(actt_ps_ready[q], n + (1 + q))
                    nc.scalar.copy(act_t[q][:, e].rearrange("p (h j) n -> p j h n", h=2),
                                   (gate_ps, t0_ps)[q][:, :].rearrange("p (j h n) -> p j h n", j=4, h=2)
                                   ).then_inc(actt_ready[q], 1)
                    if (q, e) == (0, 1):
                        act.wait_ge(givet_ps_ready[0], 2 * g + (b + 1))
                        nc.scalar.copy(give_t, up_ps[:, 0:SEQ]).then_inc(givet_ready[0], 1)
                if blocks == 2:
                    act.wait_ge(givet_ps_ready[1], n + 2)
                    nc.scalar.copy(give_more_t[:, e], t1_ps[:, :].rearrange("p (c t) -> p c t", c=2)
                                   ).then_inc(givet_ready[1], 1)
                else:
                    for signal in (sig_ready[1], actt_ready[1], givet_ready[1]):
                        act.wait_ge(signal, n + 1)
                        act.sem_inc(signal, 1)

            with act.Fori(0, n_bodies) as g:
                for b in range(2):
                    kind = act.value_load(pair_kind[0:1, bass.ds(2 * g + b, 1)], min_val=0, max_val=3)
                    two = [kind % 2 > 0, kind > 1]
                    for e in range(2):
                        with act.If(two[e]):
                            expert(g, b, e, 2)
                        with act.Else():
                            expert(g, b, e, 1)
                    act.wait_ge(unit_used, g * BODY_UNITS + (NF + (b + 1) * PAIR_UNITS))
                    nc.scalar.copy(y_pair[:, 0:512], t0_ps[:, :]).then_inc(y_act, 1)
                    with act.If(two[0]):
                        nc.scalar.copy(y_more[:, 0, :], gate_ps[:, :]).then_inc(y_more_act, 1)
                    with act.Else():
                        act.wait_ge(y_more_act, 2 * g + (b + 1))
                        act.sem_inc(y_more_act, 1)

            load_root_table()
            for i in range(QT):
                for c in range(2):
                    act.wait_ge(combined, 2 * i + c + 1)
                    nc.scalar.activation(h_scaled[:, i, c * 512:(c + 1) * 512], acc[2 * i + c][:, :], ACT.Square,
                                         accum_out=stat[:, 2 * i + c:2 * i + c + 1]).then_inc(fin_ss, 1)
                act.wait_ge(fin_sum, i + 1)
                nc.scalar.activation(stat[:, 8 + i:9 + i], stat[:, 6 + i:7 + i], ACT.Sqrt, scale=1.0 / D,
                                     bias=eps_col[:]).then_inc(fin_root, 1)

        @block.vector
        def _(dve):
            chain = [0]

            def link(ins, behind=0):
                chain[0] += 1
                ins.then_inc(dve_chain, 1)
                if chain[0] > behind:
                    dve.wait_ge(dve_chain, chain[0] - behind)

            dve.wait_ge(root_ready, 2)
            for signal in (meta_loaded, *x_loaded):
                dve.wait_ge(signal, 16)
            link(nc.vector.reciprocal(stat[:, 6:8], stat[:, 3:5]))
            link(nc.vector.reciprocal(stat[0:META, 8:9], stat[0:META, 5:6]))
            for i in range(3):
                n = P if i < QT else META
                rows = x_nat[:, i, :] if i < QT else meta_nat[0:META, :]
                nc.vector.tensor_scalar(x_scaled[0:n, i, :], rows, stat[0:n, 6 + i:7 + i], None,
                                        ALU.mult).then_inc(scaled_ready, 1)
            dve.wait_ge(vec_ps_ready, 1)
            nc.vector.tensor_copy(vec[:], ps[7][:, 0:V_ROWS]).then_inc(vec_ready, 1)
            nc.vector.tensor_copy(cw[:], ps[6][:, 0:CT * TAPS].rearrange("p (c j) -> p c j", c=CT)
                                  ).then_inc(vec_ready, 1)
            dve.wait_ge(vec_ready, 2)
            for k in range(4, KD):
                dve.wait_ge(xt_ready, k + 1)
                nc.vector.tensor_scalar(hn[:, k, :], ps[k][:, 0:T], vec[:, V_MIX + k:V_MIX + k + 1], None,
                                        ALU.mult).then_inc(hn_dve, 1)
            dve.wait_ge(pool_done, CONSTS)
            nc.vector.tensor_reduce(fold[:], ident[:].rearrange("p (g e) -> p e g", g=P // E), AX_X,
                                    ALU.add).then_inc(fold_ready, 1)
            for n, (kind, i, _, _) in enumerate(tiles):
                if kind == "a":
                    dve.wait_ge(tile_ready, n + 1)
                    dve.wait_ge(tile_act, i + 1)
                    nc.vector.tensor_tensor(glu[:, i, TAPS - 1:], ps[n % 4][:, 0:T], glu_sig[:, i % 2, :],
                                            ALU.mult).then_inc(tile_dve, 1)

            dve.wait_ge(iw_ready, 1)
            for m in range(QT * HEADS):
                i, h = divmod(m, HEADS)
                w = SEEN[i]
                dve.wait_ge(relu_ready, m + 1)
                if h:
                    dve.wait_ge(relu_used, m)
                nc.vector.scalar_tensor_tensor(
                    out=score[:, i, 0:w], in0=relu[:, m % 2, 0:w], scalar=iw[:, i, h:h + 1],
                    in1=(score if h else seen_bias)[:, i, 0:w], op0=ALU.mult,
                    op1=ALU.add).then_inc(relu_used, 1)
            dve.wait_ge(relu_used, QT * HEADS)
            for r in range(TOPK // 8):
                for i in range(QT):
                    link(nc.vector.max(top8[:, i, :], score[:, i, 0:SEEN[i]]), behind=1)
                for i in range(QT):
                    link(nc.vector.match_replace(score[:, i, 0:SEEN[i]], top8[:, i, :],
                                                 score[:, i, 0:SEEN[i]], TAKEN), behind=1)
            link(nc.vector.tensor_scalar(ssum[:, 0, :], iw[:, 0, :], 0.0, None, ALU.mult))
            for i in range(QT):
                nc.vector.tensor_scalar(seen_bias[:, i, 0:SEEN[i]], score[:, i, 0:SEEN[i]],
                                        0.5 * TAKEN, FAR, ALU.is_gt, ALU.mult).then_inc(seen_ready, 1)

            def convolve():
                for j in range(TAPS):
                    for c in range(CT):
                        src = glu[:, c, META + j:META + j + SEQ]
                        if j == 0:
                            ins = nc.vector.tensor_scalar(conv[:, c, :], src, cw[:, c, 0:1],
                                                          vec[:, V_CB + c:V_CB + c + 1], ALU.mult, ALU.add)
                        else:
                            ins = nc.vector.scalar_tensor_tensor(
                                out=conv[:, c, :], in0=src, scalar=cw[:, c, j:j + 1],
                                in1=conv[:, c, :], op0=ALU.mult, op1=ALU.add)
                        link(ins, behind=CT - 1)

            def softmax_logits(i):
                w = SEEN[i]
                dve.wait_ge(bias_ready, i + 1)
                for h in range(HEADS):
                    m = QT * HEADS + i * HEADS + h
                    dve.wait_ge(qk_ready, m + 1)
                    nc.vector.scalar_tensor_tensor(
                        out=probs[i][:, h, :], in0=ps[4 + m % 4][:, 0:w], scalar=DH ** -0.5,
                        in1=probs[i][:, h, :], op0=ALU.mult, op1=ALU.add).then_inc(logit_ready, 1)
                dve.wait_ge(logit_ready, HEADS * (i + 1))
                link(nc.vector.tensor_reduce(smax[:, i, :], probs[i], AX_X, ALU.max))
                nc.vector.tensor_scalar(sneg[:, i, :], smax[:, i, :], -1.0, None, ALU.mult).then_inc(max_ready, 1)

            def softmax_scale(i):
                dve.wait_ge(exp_ready, HEADS * (i + 1))
                link(nc.vector.reciprocal(srec[:, i, :], ssum[:, i, :]))
                nc.vector.tensor_tensor(probs[i], probs[i],
                                        srec[:, i, :].unsqueeze(2).broadcast_to([P, HEADS, SEEN[i]]),
                                        ALU.mult).then_inc(prob_ready, 1)

            convolve()
            nc.vector.memset(stat[:, 15:16], 0.0).then_inc(conv_ready, 1)
            dve.wait_ge(mean_ready, 1)
            dve.wait_ge(conv_ready, 1)
            dve.wait_ge(bias_ready, 1)
            nc.vector.tensor_tensor(centred, conv, ps[4][:, 0:SEQ].unsqueeze(1).broadcast_to([P, CT, SEQ]),
                                    ALU.subtract).then_inc(centred_ready, 1)
            softmax_logits(0)
            dve.wait_ge(ln_root, 1)
            link(nc.vector.reciprocal(ln_rows[:, 1, :], ln_rows[:, 0, :]))
            dve.wait_ge(squares_ready, 1)
            nc.vector.tensor_tensor(centred, centred, ln_rows[:, 1, :].unsqueeze(1).broadcast_to([P, CT, SEQ]),
                                    ALU.mult).then_inc(normed_ready, 1)
            softmax_logits(1)
            dve.wait_ge(normed_ready, 1)
            for c in range(CT):
                link(nc.vector.tensor_scalar(conv[:, c, :], centred[:, c, :], vec[:, V_LG + c:V_LG + c + 1],
                                             vec[:, V_LB + c:V_LB + c + 1], ALU.mult, ALU.add), behind=CT)
            softmax_scale(0)
            dve.wait_ge(swish_ready, CT)
            nc.vector.tensor_tensor(conv, conv, swish, ALU.mult).then_inc(conv_out_ready, 1)
            softmax_scale(1)

            for half in range(2):
                for k in range(KD):
                    n = NT + half * KD + k
                    dve.wait_ge(tile_ready, n + 1)
                    if half == 0:
                        dve.wait_ge(tile_act, NT - 4)
                        nc.vector.tensor_tensor(merged[:, k, :], ps[n % 4][:, 0:SEQ], gates[:, KD + k, :],
                                                ALU.mult).then_inc(tile_dve, 1)
                    else:
                        nc.vector.tensor_tensor(gates[:, k, :], ps[n % 4][:, 0:SEQ],
                                                gates[:, k, :], ALU.mult).then_inc(tile_dve, 1)
                        dve.wait_ge(tile_dve, 4 + KD + k + 1)
                        nc.vector.tensor_tensor(merged[:, k, :], merged[:, k, :], gates[:, k, :],
                                                ALU.add).then_inc(merged_ready, 2)
            dve.wait_ge(attn_copied, 12)
            nc.vector.memset(y_pair, 0.0).then_inc(give_zeroed, 1)
            nc.vector.memset(give_t, 0.0).then_inc(give_zeroed, 1)
            for e in range(2):
                nc.vector.memset(give_more[e], 0.0).then_inc(give_zeroed, 1)
            def copy_normed(i):
                dve.wait_ge(hst_ready, i + 1)
                for j in range(2):
                    g_ffn = vec[:, V_FFN + 4 * j:V_FFN + 4 * j + 4].unsqueeze(2).broadcast_to([P, 4, P])
                    nc.vector.tensor_tensor(hf[:, 4 * j:4 * j + 4, i * P:(i + 1) * P],
                                            ps[4 + 2 * i + j][:, :].rearrange("p (k n) -> p k n", k=4), g_ffn,
                                            ALU.mult).then_inc(hf_dve, 1)

            for i in range(QT):
                if i == 0:
                    dve.wait_ge(h2_ps_ready, 1)
                else:
                    dve.wait_ge(unit_used, NF)
                for c in range(2):
                    nc.vector.tensor_tensor(h2[:, i, c * 512:(c + 1) * 512], ps[4 + 2 * i + c][:, :],
                                            x_nat[:, i, c * 512:(c + 1) * 512], ALU.add).then_inc(h2_ready, 1)
                dve.wait_ge(root_ready, 3 + i)
                link(nc.vector.reciprocal(stat[:, 6 + i:7 + i], stat[:, 8 + i:9 + i]))
                dve.wait_ge(h2_ready, 2 * i + 2)
                nc.vector.tensor_scalar(h_scaled[:, i, :], h2[:, i, :], stat[:, 6 + i:7 + i], None,
                                        ALU.mult).then_inc(hs_ready, 1)
            copy_normed(0)
            copy_normed(1)

            dve.wait_ge(rpart_ready, 1)
            nc.vector.tensor_copy(rpart, ps[5][:, 0:SEQ]).then_inc(rpart_copied, 1)
            dve.wait_ge(rlog_ready, 1)
            link(nc.vector.tensor_tensor(rlog[:], ps[4][:, 0:QT * E].rearrange("p (i e) -> p i e", i=QT),
                                         br_sb[:].unsqueeze(1).broadcast_to([P, QT, E]), ALU.add))
            for i in range(QT):
                link(nc.vector.max(top8[:, i, :], rlog[:, i, :]), behind=1 - i)
            nc.vector.tensor_scalar(stat[:, 10:12], top8[:, :, 0], -1.0, None, ALU.mult).then_inc(rmax_ready, 1)
            for i in range(QT):
                link(nc.vector.max_index(ridx[:, i, :], top8[:, i, :], rlog[:, i, :]), behind=1 - i)
            link(nc.vector.memset(counts[:, 7:8], 0.0))
            link(nc.vector.tensor_copy(ridxf[:], ridx[:]))
            link(nc.vector.tensor_tensor(
                hot[:], number[:, 0:E].unsqueeze(1).unsqueeze(1).broadcast_to([P, QT, 4, E]),
                ridxf[:, :, 0:4].unsqueeze(3).broadcast_to([P, QT, 4, E]), ALU.is_equal))
            nc.vector.tensor_reduce(chosen[:], hot[:].rearrange("p i j e -> p i e j"), AX_X,
                                    ALU.add).then_inc(choice_ready, 1)
            dve.wait_ge(rexp_ready, QT)
            link(nc.vector.reciprocal(stat[:, 14:16], stat[:, 12:14]))
            link(nc.vector.tensor_tensor(rexp[:], rexp[:], stat[:, 14:16].unsqueeze(2).broadcast_to([P, QT, 4]),
                                         ALU.mult))
            dve.wait_ge(choice_ready, 1)
            link(nc.vector.tensor_tensor(hot[:], hot[:], rexp[:].unsqueeze(3).broadcast_to([P, QT, 4, E]),
                                         ALU.mult))
            nc.vector.tensor_reduce(combine_w[:], hot[:].rearrange("p i j e -> p i e j"), AX_X,
                                    ALU.add).then_inc(weight_ready, 1)

            dve.wait_ge(place_ps_ready, 1)
            where = ps[5][:, 0:QT * E].rearrange("p (i e) -> p i e", i=QT)
            link(nc.vector.scalar_tensor_tensor(out=place[:, :, 0:E], in0=where, scalar=1.0, in1=chosen[:],
                                                op0=ALU.add, op1=ALU.mult))
            link(nc.vector.tensor_scalar(place[:, :, 0:E], place[:, :, 0:E], -1.0, None, ALU.add))
            def experts_at(n):
                return [dve.value_load(order_of[0:1, bass.ds(n + e, 1)], min_val=0, max_val=E * PASSES + 1)
                        for e in range(2)]

            def one_hot(experts, q, dst, weighted, signal):
                for i in range(QT):
                    for e in range(2):
                        nc.vector.tensor_scalar(
                            dst[:, i, e * CAP:(e + 1) * CAP], number[:, q * CAP:(q + 1) * CAP],
                            place[:, i, bass.ds(experts[e], 1)],
                            weight[:, i, bass.ds(experts[e], 1)] if weighted else None,
                            ALU.is_equal, *([ALU.mult] if weighted else [])).then_inc(signal, 1)

            def plan_pick(experts, bank):
                one_hot(experts, 0, pick[0], False, pick_ready)
                for e in range(2):
                    nc.vector.tensor_copy(choose[0:E, bank, e * CAP:(e + 1) * CAP],
                                          ident[0:E, bass.ds(experts[e] % E, 1)].broadcast_to([E, CAP])
                                          ).then_inc(pick_ready, 1)

            def copy_picked(dst, q, value):
                dve.wait_ge(gather_ready[q], value)
                for j, src in enumerate((t0_ps, t1_ps)):
                    g_ffn = vec[:, V_FFN + 4 * j:V_FFN + 4 * j + 4].unsqueeze(2).broadcast_to([P, 4, P])
                    nc.vector.tensor_tensor(dst[:, 4 * j:4 * j + 4, :],
                                            src[:, :].rearrange("p (k n) -> p k n", k=4), g_ffn,
                                            ALU.mult).then_inc(picked_ready[q], 1)

            plan_pick([0, 1], 0)
            one_hot([0, 1], 1, pick[1], False, pick2_ready)
            dve.wait_ge(weight_ps_ready, 1)
            nc.vector.tensor_copy(give_t[0:E, :], ps[4][0:E, 0:SEQ]).then_inc(ct_ready, 1)
            link(nc.vector.tensor_copy(rank[:, 3 * E:3 * E + 1], ps[4][0:E, SEQ:SEQ + 1]))
            per_expert = ps[5][:, QT * E:(QT + 1) * E]
            dve.wait_ge(router_loaded, 48)
            link(nc.vector.scalar_tensor_tensor(out=rank[:, 0:E], in0=ps[5][0:E, QT * E:(QT + 1) * E],
                                                scalar=float(E), in1=rank_rows[:, 0:E],
                                                op0=ALU.mult, op1=ALU.add))
            link(nc.vector.scalar_tensor_tensor(out=rank[:, 3 * E + 1:3 * E + 2], in0=rank[:, 3 * E:3 * E + 1],
                                                scalar=float(E), in1=rank_rows[:, 2 * E + 1:2 * E + 2],
                                                op0=ALU.mult, op1=ALU.add))
            link(nc.vector.tensor_scalar(rank[:, E:2 * E], rank[:, 0:E], rank[:, 3 * E + 1:3 * E + 2], None,
                                         ALU.is_gt))
            link(nc.vector.tensor_reduce(rank[:, 3 * E + 2:3 * E + 3], rank[:, E:2 * E], AX_X, ALU.add))
            nc.vector.tensor_scalar(rank[:, 2 * E:3 * E], rank_rows[:, E:2 * E], rank[:, 3 * E + 2:3 * E + 3],
                                    None, ALU.is_equal).then_inc(rank_ready, 1)
            link(nc.vector.tensor_reduce(counts[:, 0:1], per_expert, AX_X, ALU.max))
            link(nc.vector.tensor_scalar(counts[:, 4:5], counts[:, 0:1], float(PASS_CAP),
                                         float(PAIRS // 2), ALU.is_gt, ALU.mult))
            link(nc.vector.tensor_scalar(bodies[:], counts[:, 4:5], float(PAIRS // 2), None, ALU.add))
            dve.wait_ge(order_ps_ready, 1)
            for q in range(PASSES):
                link(nc.vector.tensor_scalar(two_blocks[0:1, q * E:(q + 1) * E], ps[4][0:1, E:2 * E],
                                             float(q * PASS_CAP + CAP), None, ALU.is_gt), behind=1)
                link(nc.vector.tensor_scalar(order_of[0:1, q * E + 2:(q + 1) * E], ps[4][0:1, 2:E],
                                             float(q * E), None, ALU.add), behind=1)
            link(nc.vector.memset(counts[:, 7:8], 0.0))
            by_pair = two_blocks[:].rearrange("a (p e) -> a p e", e=2)
            nc.vector.scalar_tensor_tensor(out=pair_kind[:], in0=by_pair[:, :, 1], scalar=2.0,
                                           in1=by_pair[:, :, 0], op0=ALU.mult, op1=ALU.add
                                           ).then_inc(plan_ready, 1)
            copy_picked(picked[:, 0], 0, 1)
            for q in range(1, PASSES):
                link(nc.vector.tensor_scalar(place[:, :, q * E:(q + 1) * E], place[:, :, 0:E],
                                             -float(q * PASS_CAP), None, ALU.add), behind=1)
            for q in range(PASSES):
                link(nc.vector.tensor_copy(weight[:, :, q * E:(q + 1) * E], combine_w[:]), behind=1)
            link(nc.vector.memset(counts[:, 7:8], 0.0))
            dve.wait_ge(plan_ready, 1)
            for signal, n in ((give2_ready, 1), (picked_ready[1], 1), (gate_read[1], 1),
                              (clipped[0], 2), (clipped[1], 2), (act_ready[0], 1), (act_ready[1], 1),
                              (y_dve, 1), (y_more_dve, 1)):
                dve.sem_inc(signal, n)
            n_bodies = dve.value_load(bodies[0:1, 0:1], min_val=PAIRS // 2,
                                      max_val=PASSES * PAIRS // 2)

            dve.wait_ge(give_zeroed, 4)

            def count_on(signal, before, n):
                dve.wait_ge(signal, before)
                dve.sem_inc(signal, n)

            def expert(g, b, e, blocks, which):
                if blocks == 2:
                    for i in range(QT):
                        for c in range(2):
                            at = c * P + c * CAP
                            expert_at = bass.ds(which, 1)
                            nc.vector.tensor_scalar(
                                give_more[e][:, i, at:at + CAP], number[:, CAP:2 * CAP],
                                place[:, i, expert_at], weight[:, i, expert_at],
                                ALU.is_equal, ALU.mult).then_inc(give2_ready, 1)
                n = 4 * g + (2 * b + e)
                for q in range(blocks):
                    dve.wait_ge(unit_used, g * BODY_UNITS + (NF + b * PAIR_UNITS + (e + 1) * UP_UNITS))
                    gate, lin = ((gate_ps, up_ps), (t0_ps, t1_ps))[q]
                    nc.vector.tensor_scalar(glu_steps[:, 0, :], gate[:, :], 7.0, None,
                                            ALU.min).then_inc(gate_read[q], 1)
                    dve.wait_ge(act_ready[0], n + (1 + q))
                    dve.wait_ge(act_ready[1], n + 1)
                    nc.vector.tensor_scalar(glu_steps[:, 2, :], lin[:, :], 7.0, -7.0, ALU.min,
                                            ALU.max).then_inc(clipped[q], 1)
                    dve.wait_ge(clipped[q], 2 * n + 3)
                    nc.vector.scalar_tensor_tensor(
                        out=glu_steps[:, 2, :], in0=glu_steps[:, 2, :], scalar=1.0, in1=glu_steps[:, 0, :],
                        op0=ALU.add, op1=ALU.mult).then_inc(clipped[q], 1)
                    dve.wait_ge(clipped[q], 2 * n + 4)
                    dve.wait_ge(sig_ready[q], n + (1 + q))
                    nc.vector.tensor_tensor(glu_steps[:, 3, :], glu_steps[:, 2, :], glu_steps[:, 1, :],
                                            ALU.mult).then_inc(act_ready[q], 1)
                if blocks == 1:
                    count_on(give2_ready, 4 * n + 1, 4)
                    count_on(gate_read[1], n + 1, 1)
                    count_on(clipped[1], 2 * n + 2, 2)
                    count_on(act_ready[1], n + 1, 1)

            with dve.Fori(0, n_bodies) as g:
                for b in range(2):
                    kind = dve.value_load(pair_kind[0:1, bass.ds(2 * g + b, 1)], min_val=0, max_val=3)
                    two = [kind % 2 > 0, kind > 1]
                    with dve.If(kind > 0):
                        copy_picked(picked2, 1, 2 * g + (b + 2))
                    with dve.Else():
                        count_on(picked_ready[1], 4 * g + (2 * b + 1), 2)
                    now, then = experts_at(4 * g + 2 * b), experts_at(4 * g + (2 * b + 2))
                    one_hot(now, 0, give, True, pick_ready)
                    plan_pick(then, 1 - b)
                    one_hot(then, 1, pick[1], False, pick2_ready)
                    for e in range(2):
                        with dve.If(two[e]):
                            expert(g, b, e, 2, now[e])
                        with dve.Else():
                            expert(g, b, e, 1, now[e])
                        if e == 1:
                            copy_picked(picked[:, 1 - b], 0, 2 * g + (b + 2))
                    dve.wait_ge(unit_used, g * BODY_UNITS + (NF + (b + 1) * PAIR_UNITS))
                    nc.vector.tensor_copy(y_pair[:, 512:1024], t1_ps[:, :]).then_inc(y_dve, 1)
                    with dve.If(two[1]):
                        nc.vector.tensor_copy(y_more[:, 1, :], up_ps[:, :]).then_inc(y_more_dve, 1)
                    with dve.Else():
                        count_on(y_more_dve, 2 * g + (b + 1), 1)

            dve.wait_ge(gfin_loaded, 16)
            for i in range(QT):
                dve.wait_ge(fin_ss, 2 * i + 2)
                nc.vector.tensor_tensor(stat[:, 6 + i:7 + i], stat[:, 2 * i:2 * i + 1],
                                        stat[:, 2 * i + 1:2 * i + 2], ALU.add).then_inc(fin_sum, 1)
                dve.wait_ge(fin_root, i + 1)
                link(nc.vector.reciprocal(stat[:, 10 + i:11 + i], stat[:, 8 + i:9 + i]))
                for c in range(2):
                    nc.vector.scalar_tensor_tensor(
                        out=x_nat[:, i, c * 512:(c + 1) * 512], in0=acc[2 * i + c][:, :],
                        scalar=stat[:, 10 + i:11 + i], in1=gfin[:, c * 512:(c + 1) * 512],
                        op0=ALU.mult, op1=ALU.mult).then_inc(fin_ready, 1)

        @block.tensor
        def _(pe):
            mm = nc.tensor.matmul

            pe.wait_ge(pool_done, 1)
            pe.wait_ge(vecs_loaded, 96)
            pe.wait_ge(cw_loaded, 16)
            for c in range(CT):
                nc.tensor.transpose(ps[6][:, c * TAPS:(c + 1) * TAPS], cw_rows[:, c * P:(c + 1) * P],
                                    ident[0:TAPS, 0:TAPS])
            nc.tensor.transpose(ps[7][:, 0:V_ROWS], vec_rows, ident[0:V_ROWS, 0:V_ROWS]).then_inc(vec_ps_ready, 1)

            for k in range(KD):
                if k >= 6:
                    pe.wait_ge(vec_ready, 2)
                for i, (t0, n) in enumerate(((META, P), (META + P, P), (0, META))):
                    if k == 0:
                        pe.wait_ge(scaled_ready, i + 1)
                    ins = nc.tensor.transpose(ps[k][:, t0:t0 + n], x_scaled[0:n, i, k * P:(k + 1) * P],
                                              ident[0:n, 0:n])
                ins.then_inc(xt_ready, 1)
            pe.wait_ge(hn_act, 4)
            pe.wait_ge(hn_dve, 4)

            def front_unit(u, n, kk=KD):
                pe.wait_ge(slot_loaded[slot_of(u)], 16 * (loads_before(u) + 1))
                return ring[:, slot_of(u), 0:kk * n].rearrange("p (k n) -> p k n", k=kk)

            used = [0]

            def project(n):
                kind, i, u, c = tiles[n]
                if n >= 4:
                    pe.wait_ge(*read_by(n - 4))
                bank = ps[n % 4]
                if kind == "v":
                    ws = [front_unit(u + j, UNIT_COLS) for j in range(2)]
                    if i == 0:
                        for k in range(KD):
                            for j in range(4):
                                ins = mm(bank[32 * j:32 * j + META, 0:P], hn[:, k, 0:META],
                                         ws[j // 2][:, k, (j % 2) * P:(j % 2 + 1) * P],
                                         start=(k == 0), stop=(k == KD - 1))
                    for j, w in enumerate(ws if i else []):
                        for k in range(KD):
                            ins = mm(bank[0:KEYN[i], j * UNIT_COLS:(j + 1) * UNIT_COLS],
                                     hn[:, k, KEY0[i]:KEY0[i] + KEYN[i]], w[:, k, :],
                                     start=(k == 0), stop=(k == KD - 1))
                elif kind == "ik":
                    w = front_unit(u, C_GLU - C_IK)
                    rows = slice(0, C_GLU - C_IK)
                    for k in range(KD):
                        ins = mm(bank[rows, 0:T], w[:, k, :], hn[:, k, :], start=(k == 0), stop=(k == KD - 1))
                else:
                    w = front_unit(u, UNIT_COLS)
                    t0 = 0 if kind in ("g", "a", "k") else META
                    for k in range(KD):
                        ins = mm(bank[:, 0:T - t0], w[:, k, c:c + P], hn[:, k, t0:T],
                                 start=(k == 0), stop=(k == KD - 1))
                ins.then_inc(tile_ready, 1)
                nxt = tiles[n + 1][2] if n + 1 < NT else U_CO
                if nxt != u:
                    pe.wait_ge(tile_ready, n + 1)
                    pe.sem_inc(unit_used, nxt - u)

            for n in range(first["ik"] + 1):
                if n == 4:
                    pe.wait_ge(rel_loaded, 32)
                    mm(ps[4][0:HEADS, :], rel_sb[:], bucket_sb[:, 0:512], start=True, stop=True)
                    mm(ps[5][0:HEADS, 0:NTOE - 512], rel_sb[:], bucket_sb[:, 512:NTOE], start=True,
                       stop=True).then_inc(toe_ps_ready, 1)
                project(n)
            pe.wait_ge(tile_act, first["ik"] + 1 - 4)
            for i in range(QT):
                ins = nc.tensor.transpose(ps[4][:, i * HEADS:(i + 1) * HEADS], iw_t[64:72, i * P:(i + 1) * P],
                                          ident[64:72, 64:72])
            ins.then_inc(iw_ps_ready, 1)
            pe.wait_ge(iw_ready, 1)
            pe.wait_ge(idx_ready, 2)
            for m in range(QT * HEADS):
                i, h = divmod(m, HEADS)
                if m >= 4:
                    pe.wait_ge(relu_ready, m - 3)
                mm(ps[4 + m % 4][:, 0:SEEN[i]], iq[:, h // 2, i * P:(i + 1) * P], ik_half[:, h % 2, 0:SEEN[i]],
                   start=True, stop=True).then_inc(qk_ready, 1)
            for n in range(first["q"], first["gate"]):
                project(n)
            gate0 = first["gate"]
            for i in range(4):
                project(gate0 + i)
            pe.wait_ge(conv_ready, 1)
            pe.wait_ge(relu_ready, QT * HEADS)
            for c in range(CT):
                ins = mm(ps[4][:, 0:SEQ], mean_w[:], conv[:, c, :], start=(c == 0), stop=(c == CT - 1))
            ins.then_inc(mean_ready, 1)
            project(gate0 + 4)
            pe.wait_ge(squares_ready, 1)
            for c in range(CT):
                ins = mm(ps[5][:, 0:SEQ], mean_w[:], squares[:, c, :], start=(c == 0), stop=(c == CT - 1))
            ins.then_inc(var_ready, 1)
            project(gate0 + 5)
            pe.wait_ge(tile_act, first["k"] + 4 - 4)
            pe.wait_ge(idx_ready, 6)
            pe.wait_ge(centred_ready, 1)
            for j in range(QT * HEADS):
                m = QT * HEADS + j
                i, h = divmod(j, HEADS)
                if j == 1:
                    pe.wait_ge(ln_root, 1)
                if j >= 4:
                    pe.wait_ge(logit_ready, j - 3)
                mm(ps[4 + m % 4][:, 0:SEEN[i]], q_t[:, h // 2, i * P:(i + 1) * P], k_half[:, h, 0:SEEN[i]],
                   start=True, stop=True).then_inc(qk_ready, 1)
                if j % 2:
                    project(gate0 + 6 + j // 2)
            for i in range(14, 16):
                project(gate0 + i)

            def branch_tile(half, k):
                u, src = ((U_CO, conv), (U_AO, attn))[half]
                n = NT + half * KD + k
                pe.wait_ge(*read_by(n - 4))
                for q in range(4):
                    ins = mm(ps[n % 4][:, 0:SEQ], branch_w[half][q // 2][:, q % 2, k * P:(k + 1) * P],
                             src[:, q, :], start=(q == 0), stop=(q == 3))
                ins.then_inc(tile_ready, 1)

            def attend(i, meanwhile):
                r0 = 0 if i == 0 else 5
                pe.wait_ge(prob_ready, i + 1)
                pe.wait_ge(logit_ready, QT * HEADS)
                pe.wait_ge(meta_values, 3)
                r = r0
                for s in range(2 + i):
                    for half in range(2):
                        if r >= 4:
                            pe.wait_ge(attn_copied, r - 3)
                        for j in range(4):
                            ins = nc.tensor.transpose(
                                ps[4 + r % 4][0:KEYN[s], j * P:(j + 1) * P],
                                probs[i][:, 4 * half + j, KEY0[s]:KEY0[s] + KEYN[s]], ident[:])
                        ins.then_inc(attn_ps_ready, 1)
                        r += 1
                for k in meanwhile:
                    branch_tile(0, k)
                pe.wait_ge(attn_copied, r)
                bank = ps[4 + r % 4]
                for h in range(HEADS):
                    for s in range(2 + i):
                        ins = mm(bank[(h % 2) * DH:(h % 2 + 1) * DH, (h // 2) * P:(h // 2 + 1) * P],
                                 v_sb[0:KEYN[s], s, h * DH:(h + 1) * DH], probs_t[0:KEYN[s], s, h, :],
                                 start=(s == 0), stop=(s == 1 + i))
                ins.then_inc(attn_ps_ready, 1)

            pe.wait_ge(conv_out_ready, 1)
            branch_w = [[front_unit(U_CO + j, D, 2) for j in range(2)]]
            attend(0, [0, 1])
            attend(1, [2])
            for k in range(3, KD):
                branch_tile(0, k)
            pe.wait_ge(tile_ready, NT + KD)
            pe.sem_inc(unit_used, 2)
            branch_w.append([front_unit(U_AO + j, D, 2) for j in range(2)])
            pe.wait_ge(attn_copied, 12)
            for k in range(KD):
                branch_tile(1, k)
            pe.wait_ge(tile_ready, NT + 2 * KD)
            pe.sem_inc(unit_used, 2)
            pe.wait_ge(attn_copied, 12)
            ws = [front_unit(U_WO + j, D, 2) for j in range(KD // 2)]
            for i in range(QT):
                for k in range(KD):
                    if i == 0:
                        pe.wait_ge(merged_ready, 2 * (k + 1))
                    for c in range(2):
                        ins = mm(ps[4 + 2 * i + c][:, :], merged[:, k, i * P:(i + 1) * P],
                                 ws[k // 2][:, k % 2, c * 512:(c + 1) * 512], start=(k == 0), stop=(k == KD - 1))
                    if i == 1 and k % 2:
                        ins.then_inc(unit_used, 1)
                    elif k == KD - 1:
                        ins.then_inc(h2_ps_ready, 1)
            pe.wait_ge(tile_dve, 4 + 2 * KD)

            def begin_sum(i, c):
                mm(acc[2 * i + c][:, :], ident[:], h2[:, i, c * 512:(c + 1) * 512], start=True, stop=False,
                   skip_group_check=True)

            for i in range(QT):
                pe.wait_ge(hs_ready, i + 1)
                for k in range(KD):
                    ins = nc.tensor.transpose(ps[4 + 2 * i + k // 4][:, (k % 4) * P:(k % 4 + 1) * P],
                                              h_scaled[:, i, k * P:(k + 1) * P], ident[:])
                ins.then_inc(hst_ready, 1)
                begin_sum(0, i)
            pe.wait_ge(router_loaded, 48)
            pe.wait_ge(hf_dve, 4)
            for k in range(KD):
                ins = mm(ps[5][(k % 4) * E:(k % 4 + 1) * E, 0:SEQ], wr_sb[:, k, :], hf[:, k, :],
                         start=(k < 4), stop=(k >= 4))
            ins.then_inc(rpart_ready, 1)
            pe.wait_ge(rpart_copied, 1)
            pe.wait_ge(fold_ready, 1)
            for i in range(QT):
                ins = mm(ps[4][:, i * E:(i + 1) * E], rpart[:, i * P:(i + 1) * P], fold[:], start=True, stop=True)
            ins.then_inc(rlog_ready, 1)
            begin_sum(1, 0)
            begin_sum(1, 1)
            pe.wait_ge(choice_ready, 1)
            mm(ps[5][:, 0:E], before[:], chosen[:, 0, :], start=True, stop=True)
            mm(ps[5][:, E:2 * E], ones[:], chosen[:, 0, :], start=True, stop=False)
            mm(ps[5][:, E:2 * E], before[:], chosen[:, 1, :], start=False, stop=True)
            mm(ps[5][:, 2 * E:3 * E], ones[:], chosen[:, 0, :], start=True, stop=False)
            mm(ps[5][:, 2 * E:3 * E], ones[:], chosen[:, 1, :], start=False, stop=True).then_inc(place_ps_ready, 1)
            pe.wait_ge(weight_ready, 1)
            for i in range(QT):
                ins = nc.tensor.transpose(ps[4][0:E, i * P:(i + 1) * P], combine_w[:, i, :], ident[:])
            for i in range(QT):
                ins = mm(ps[4][0:E, SEQ:SEQ + 1], chosen[:, i, :], ones[:, 0:1], start=(i == 0), stop=(i == QT - 1))
            ins.then_inc(weight_ps_ready, 1)

            def gather(q):
                for k in range(KD):
                    for i in range(QT):
                        ins = mm((t0_ps, t1_ps)[k // 4][:, (k % 4) * P:(k % 4 + 1) * P],
                                 h_scaled[:, i, k * P:(k + 1) * P], pick[q][:, i, :],
                                 start=(i == 0), stop=(i == QT - 1))
                ins.then_inc(gather_ready[q], 1)

            pe.wait_ge(give_zeroed, 4)
            pe.wait_ge(pick_ready, 6)
            gather(0)
            pe.wait_ge(rank_ready, 1)
            mm(ps[4][0:1, 0:E], rank_rows[:, 2 * E:2 * E + 1], rank[:, 2 * E:3 * E], start=True, stop=True)
            mm(ps[4][0:1, E:2 * E], rank[:, 3 * E:3 * E + 1], rank[:, 2 * E:3 * E], start=True,
               stop=True).then_inc(order_ps_ready, 1)
            pe.wait_ge(ct_ready, 1)
            pe.wait_ge(ebias_loaded, 32)
            for signal in (gather_ready[1], actt_ps_ready[1], givet_ps_ready[1]):
                pe.sem_inc(signal, 1)
            pe.wait_ge(plan_ready, 1)
            n_bodies = pe.value_load(bodies[0:1, 0:1], min_val=PAIRS // 2,
                                     max_val=PASSES * PAIRS // 2)
            def unit(g, b, j):
                u = NF + b * PAIR_UNITS + j
                pe.wait_ge(slot_loaded[slot_of(u)], g * (16 * TURNS) + 16 * (loads_before(u) + 1))
                return ring[:, slot_of(u), :]

            def count_on(signal, before):
                pe.wait_ge(signal, before)
                pe.sem_inc(signal, 1)

            def add_outputs(n):
                for i, c in [(i, c) for i in range(QT) for c in range(2)][3 if n == 1 else 0:3 if n == 3 else 4]:
                    ins = mm(acc[2 * i + c][:, :], give_t[:, i * P:(i + 1) * P],
                             y_pair[:, c * 512:(c + 1) * 512], start=False, stop=False, skip_group_check=True)
                    if n == 4:
                        ins.then_inc(combined, 1)

            def expert(g, b, e, blocks):
                n = 4 * g + (2 * b + e)
                pe.wait_ge(clipped[0], 2 * n + 2)
                if e == 1 and blocks == 2:
                    pe.wait_ge(actt_ready[1], n + 1)
                    pe.wait_ge(givet_ready[1], n + 1)
                outs = [(q, c, ((gate_ps, up_ps), (t0_ps, t1_ps))[q][c // 2], c % 2)
                        for q in range(blocks) for c in range(4)]
                for q, c, bank, half in (outs if e == 0 else outs[::-1]):
                    if e == 1 and (q, c) == (0, 1):
                        pe.wait_ge(actt_ready[0], n)
                    if e == 0 and (q, c) == (1, 0):
                        pe.wait_ge(picked_ready[1], 4 * g + (2 * b + 3))
                    mm(bank[half * CAP:(half + 1) * CAP, :], choose[0:E, b, e * CAP:(e + 1) * CAP],
                       bu_sb[:, c * 512:(c + 1) * 512], start=True, stop=False)
                for k in range(UP_UNITS):
                    w = unit(g, b, e * UP_UNITS + k)
                    for q, c, bank, half in outs:
                        tokens = (picked[:, b], picked2)[q]
                        ins = mm(bank[half * CAP:(half + 1) * CAP, :], tokens[:, k, e * CAP:(e + 1) * CAP],
                                 w[:, c * 512:(c + 1) * 512], start=False, stop=(k == UP_UNITS - 1))
                    ins.then_inc(unit_used, 1)

                if e == 0:
                    if blocks == 1:
                        pe.wait_ge(picked_ready[1], 4 * g + (2 * b + 3))
                    add_outputs(3)

                def transpose_act(q):
                    pe.wait_ge(act_ready[q], n + 2)
                    for j in range(4):
                        ins = nc.tensor.transpose((gate_ps, t0_ps)[q][:, j * P:(j + 1) * P],
                                                  glu_steps[:, 3, j * P:(j + 1) * P], ident[:])
                    ins.then_inc(actt_ps_ready[q], 1)

                def transpose_give():
                    for i in range(QT):
                        ins = nc.tensor.transpose(up_ps[:, i * P:(i + 1) * P], give[:, i, :], ident[:])
                    ins.then_inc(givet_ps_ready[0], 1)

                if blocks == 2:
                    transpose_act(0)
                    if e == 0:
                        add_outputs(1)
                    else:
                        transpose_give()
                    pe.wait_ge(clipped[1], 2 * n + 4)
                if e == 1:
                    pe.wait_ge(actt_ready[1], n + 1)
                    pe.wait_ge(givet_ready[1], n + 1)
                    pe.wait_ge(pick_ready, 20 * g + (6 + 10 * (b + 1)))
                    gather(0)
                if blocks == 1:
                    transpose_act(0)
                    if e == 0:
                        add_outputs(1)
                    else:
                        transpose_give()
                    count_on(actt_ps_ready[1], n + 1)
                    count_on(givet_ps_ready[1], n + 1)
                else:
                    if e == 1:
                        pe.wait_ge(picked_ready[0], 4 * g + (2 * b + 4))
                    transpose_act(1)
                    pe.wait_ge(give2_ready, 4 * n + 5)
                    for c in range(2):
                        for i in range(QT):
                            ins = nc.tensor.transpose(t1_ps[:, c * SEQ + i * P:c * SEQ + (i + 1) * P],
                                                      give_more[e][:, i, c * P:(c + 1) * P], ident[:])
                    ins.then_inc(givet_ps_ready[1], 1)

            def down(g, b, more):
                if more:
                    pe.wait_ge(givet_ready[0], 2 * g + (b + 1))
                for f in range(DOWN_UNITS):
                    if f % 2 == 0:
                        both = [unit(g, b, 2 * UP_UNITS + f + e).rearrange("p (f n) -> p f n", f=2)
                                for e in range(2)]
                    for c, bank in enumerate((t0_ps, t1_ps)):
                        for e in range(2):
                            ins = mm(bank[e * CAP:(e + 1) * CAP, :], act_t[0][:, e, f, :],
                                     both[e][:, f % 2, c * 512:(c + 1) * 512],
                                     start=(f == 0), stop=(f == DOWN_UNITS - 1))
                    for e in more:
                        bank = (gate_ps, up_ps)[e]
                        for c in range(2):
                            ins = mm(bank[c * CAP:(c + 1) * CAP, :], act_t[1][:, e, f, :],
                                     both[e][:, f % 2, c * 512:(c + 1) * 512],
                                     start=(f == 0), stop=(f == DOWN_UNITS - 1))
                    if f % 2:
                        ins.then_inc(unit_used, 2)
                if not more:
                    pe.wait_ge(givet_ready[0], 2 * g + (b + 1))
                for e in more:
                    pe.wait_ge((y_more_act, y_more_dve)[e], 2 * g + (b + 2))
                    for i in range(QT):
                        for c in range(2):
                            ins = mm(acc[2 * i + c][:, :], give_more_t[:, e, c, i * P:(i + 1) * P],
                                     y_more[:, e, :], start=False, stop=False, skip_group_check=True)

            with pe.Fori(0, n_bodies) as g:
                for b in range(2):
                    kind = pe.value_load(pair_kind[0:1, bass.ds(2 * g + b, 1)], min_val=0, max_val=3)
                    two = [kind % 2 > 0, kind > 1]
                    for signal in (y_act, y_dve, y_more_act, y_more_dve):
                        pe.wait_ge(signal, 2 * g + (b + 1))
                    with pe.If(kind > 0):
                        pe.wait_ge(pick2_ready, 8 * g + (4 * b + 4))
                        gather(1)
                    with pe.Else():
                        count_on(gather_ready[1], 2 * g + (b + 1))
                    pe.wait_ge(picked_ready[0], 4 * g + (2 * b + 2))
                    for e in range(2):
                        with pe.If(two[e]):
                            expert(g, b, e, 2)
                        with pe.Else():
                            expert(g, b, e, 1)
                    pe.wait_ge(actt_ready[0], 4 * g + (2 * b + 2))
                    pe.wait_ge(actt_ready[1], 4 * g + (2 * b + 3))
                    pe.wait_ge(givet_ready[1], 4 * g + (2 * b + 3))
                    pe.wait_ge(picked_ready[0], 4 * g + (2 * b + 4))
                    with pe.If(kind < 2):
                        with pe.If(kind < 1):
                            down(g, b, [])
                        with pe.Else():
                            down(g, b, [0])
                        pe.nop()
                    with pe.Else():
                        with pe.If(kind < 3):
                            down(g, b, [1])
                        with pe.Else():
                            down(g, b, [0, 1])
                        pe.nop()
            pe.wait_ge(y_act, 2 * n_bodies + 1)
            pe.wait_ge(y_dve, 2 * n_bodies + 1)
            add_outputs(4)


def bucket_rows():
    j = np.arange(NTOE)
    dist = T - 1 - j
    n = np.maximum(dist, 0)
    exact = NB // 2
    large = exact + (np.log(np.maximum(n, 1) / exact) / np.log(128 / exact) * (NB - exact)).astype(np.int32)
    bucket = np.where(n < exact, n, np.minimum(large, NB - 1))
    rows = np.zeros((NB + 1, NTOE), np.float32)
    rows[bucket[dist >= 0], j[dist >= 0]] = 1.0
    rows[NB, dist < 0] = FAR
    return rows


def order_rows():
    key = -np.arange(E, dtype=np.float32)
    key[0:2] += (4 * E * SEQ, 2 * E * SEQ)
    pairs = PAIRS - 1
    slots = [*range(4, pairs + 1, 4), *range(2, pairs + 1, 4), *range(1, pairs + 1, 2)]
    rank_at = np.zeros(E, np.float32)
    rank_at[1] = 1
    for r, pair in enumerate(slots):
        rank_at[2 * pair] = 2 + r
        rank_at[2 * pair + 1] = 2 + pairs + r
    rows = np.zeros((E, 2 * E + 2), np.float32)
    rows[:, 0:E] = key
    rows[:, E:2 * E] = rank_at
    rows[:, 2 * E] = np.arange(E)
    rows[:, 2 * E + 1] = key
    return rows


def kernel(**inputs):
    import concourse.bacc as bacc
    from concourse.bass_utils import run_bass_kernel_spmd

    a = {k: np.ascontiguousarray(v) for k, v in inputs.items()}
    order = ["x", "meta_tokens", "rel_bias", "norm_mix", "w_in", "b_gate", "w_attn_out", "conv_w", "conv_b",
             "conv_ln_g", "conv_ln_b", "w_conv_out", "w_out", "norm_ffn", "w_router", "b_router",
             "w_up_gate", "b_up_gate", "w_down", "b_down", "norm_final"]
    whole = ("meta_tokens", "rel_bias", "norm_final")
    nc = bacc.Bacc("TRN2", target_bir_lowering=False, num_devices=1)
    arrays, args = {}, []
    for name in order:
        v = a[name] if name in whole else a[name][0]
        arrays["in_" + name] = v
        args.append(nc.dram_tensor("in_" + name, v.shape, F32, kind="ExternalInput").ap())
    arrays["in_bucket_rows"] = bucket_rows()
    args.append(nc.dram_tensor("in_bucket_rows", (NB + 1, NTOE), F32, kind="ExternalInput").ap())
    arrays["in_order_rows"] = order_rows()
    args.append(nc.dram_tensor("in_order_rows", (E, 2 * E + 2), F32, kind="ExternalInput").ap())
    args.append(nc.dram_tensor("out", (SEQ, D), F32, kind="ExternalOutput").ap())
    layer(nc, *args)
    r = run_bass_kernel_spmd(nc, [arrays], core_ids=[0])
    return r.results[0]["out"].reshape(1, SEQ, D)
```
